# Optimizing a Trainium2 kernel written in Bass

```python
import math
import jax, jax.numpy as jnp
from jax import lax
import numpy as np

D_MODEL = 1024
BATCH = 1
SEQ = 256
DEPTH = 2

CHUNK = 64
Q_BLOCK = 128
HEAD_DIM = 64
N_BRANCH = 4
D_BRANCH = D_MODEL // 4
D_CONV = D_BRANCH
CONV_WIDTH = 31
D_POOL = D_BRANCH
POOL_WINDOWS = (2, 4, 8, 16)
POOL_GROUP = D_POOL // len(POOL_WINDOWS)
SB_HEADS = D_BRANCH // HEAD_DIM
RET_HEADS = D_BRANCH // HEAD_DIM
XA_HEADS = 4
D_XA = XA_HEADS * HEAD_DIM
N_MEM = 256
D_FF = 2816
N_EXPERTS = 8
TOP_K = 2
ROPE_THETA = 10000.0
EPS = 1e-6
IN_SPLITS = (2 * D_CONV, 2 * D_CONV + D_POOL, 2 * D_CONV + D_POOL + 3 * D_BRANCH)
D_IN = 2 * D_CONV + D_POOL + 3 * D_BRANCH + 4 * D_BRANCH

kernel_name = 'hybrid_conv_pool_stickbreak_retention_moe_trunk'

def _rms_norm(x, g):
    xf = x.astype(jnp.float32)
    y = xf * lax.rsqrt(jnp.mean(xf * xf, axis=-1, keepdims=True) + EPS)
    return (y * g.astype(jnp.float32)).astype(x.dtype)

def _layer_norm(x, g, b):
    xf = x.astype(jnp.float32)
    xc = xf - jnp.mean(xf, axis=-1, keepdims=True)
    y = xc * lax.rsqrt(jnp.mean(xc * xc, axis=-1, keepdims=True) + EPS)
    return (y * g.astype(jnp.float32) + b.astype(jnp.float32)).astype(x.dtype)

def _head_norm(x):
    xc = x - jnp.mean(x, axis=-1, keepdims=True)
    return xc * lax.rsqrt(jnp.mean(xc * xc, axis=-1, keepdims=True) + EPS)

def _rotary(x, positions):
    half = x.shape[-1] // 2
    inv_freq = ROPE_THETA ** (-jnp.arange(half, dtype=jnp.float32) / half)
    ang = positions.astype(jnp.float32)[:, :, None, None] * inv_freq
    cos, sin = jnp.cos(ang), jnp.sin(ang)
    x1, x2 = x[..., :half], x[..., half:]
    return jnp.concatenate([x1 * cos - x2 * sin, x1 * sin + x2 * cos], axis=-1)

def _swiglu(h, w_gu, w_down):
    g, u = jnp.split(h @ w_gu, 2, axis=-1)
    return (jax.nn.silu(g) * u) @ w_down

def _conformer_conv(u, conv_w, conv_b, ln_g, ln_b):
    a, g = jnp.split(u, 2, axis=-1)
    v = a * jax.nn.sigmoid(g)
    v = lax.conv_general_dilated(
        v, conv_w.astype(v.dtype)[:, None, :], window_strides=(1,),
        padding=[(CONV_WIDTH - 1, 0)], dimension_numbers=('NWC', 'WIO', 'NWC'),
        feature_group_count=D_CONV) + conv_b
    return jax.nn.silu(_layer_norm(v, ln_g, ln_b))

def _multiscale_pool(u, pool_w, pool_scale):
    B, S, _ = u.shape
    uf = u.astype(jnp.float32)
    cs = jnp.pad(jnp.cumsum(uf, axis=1), ((0, 0), (1, 0), (0, 0)))
    t = jnp.arange(S, dtype=jnp.float32)[None, :, None]
    diffs = []
    for gi, w in enumerate(POOL_WINDOWS):
        sl = slice(gi * POOL_GROUP, (gi + 1) * POOL_GROUP)
        c = cs[:, :, sl]
        lower = jnp.pad(c, ((0, 0), (w - 1, 0), (0, 0)))[:, :S]
        mean = (c[:, 1:] - lower) / jnp.minimum(t + 1.0, float(w))
        diffs.append(mean - uf[:, :, sl])
    d = jnp.stack(diffs, axis=2).astype(u.dtype)
    y = jnp.einsum('bsgc,gcd->bsgd', d, pool_w).reshape(B, S, D_POOL)
    return y * pool_scale

def _stick_breaking(q, k, v):
    B, S, H, Dh = q.shape
    scale = Dh ** -0.5
    outs = []
    for qs in range(0, S, Q_BLOCK):
        qe = qs + Q_BLOCK
        z = jnp.einsum('bqhd,bkhd->bhqk', q[:, qs:qe], k[:, :qe]).astype(jnp.float32) * scale
        t_idx = qs + jnp.arange(Q_BLOCK)[:, None]
        s_idx = jnp.arange(qe)[None, :]
        mask = s_idx < t_idx
        log_1m = jnp.where(mask, jax.nn.log_sigmoid(-z), 0.0)
        tail = lax.cumsum(log_1m, axis=log_1m.ndim - 1, reverse=True) - log_1m
        a = jnp.where(mask, jnp.exp(jax.nn.log_sigmoid(z) + tail), 0.0)
        outs.append(jnp.einsum('bhqk,bkhd->bqhd', a.astype(v.dtype), v[:, :qe]))
    return jnp.concatenate(outs, axis=1)

def _retention(q, k, v, g, positions, gammas):
    B, S, _ = q.shape
    nc = S // CHUNK
    hs = (B, S, RET_HEADS, HEAD_DIM)
    cs = (B, nc, CHUNK, RET_HEADS, HEAD_DIM)
    q = _rotary(q.astype(jnp.float32).reshape(hs), positions).reshape(cs)
    k = (_rotary(k.astype(jnp.float32).reshape(hs), positions) * HEAD_DIM ** -0.5).reshape(cs)
    v = v.astype(jnp.float32).reshape(cs)
    log_g = jnp.log(gammas)
    idx = jnp.arange(CHUNK, dtype=jnp.float32)
    rel = idx[:, None] - idx[None, :]
    decay = jnp.where(rel >= 0, jnp.exp(jnp.maximum(rel, 0.0) * log_g[:, None, None]), 0.0)
    inner = jnp.einsum('bcnhd,bcmhd->bchnm', q, k) * decay
    inner = jnp.einsum('bchnm,bcmhd->bcnhd', inner, v)
    zeta = jnp.exp((CHUNK - 1 - idx)[:, None] * log_g)
    xi = jnp.exp((idx + 1.0)[:, None] * log_g)
    g_chunk = jnp.exp(CHUNK * log_g)
    kv = jnp.einsum('bcmhd,bcmhe->bchde', k * zeta[:, :, None], v)

    def step(state, inp):
        q_c, kv_c = inp
        cross = jnp.einsum('bnhd,bhde->bnhe', q_c, state)
        return state * g_chunk[:, None, None] + kv_c, cross

    state0 = jnp.zeros((B, RET_HEADS, HEAD_DIM, HEAD_DIM), jnp.float32)
    _, cross = lax.scan(step, state0, (jnp.moveaxis(q * xi[:, :, None], 1, 0), jnp.moveaxis(kv, 1, 0)))
    o = (inner + jnp.moveaxis(cross, 0, 1)).reshape(hs)
    o = _head_norm(o).reshape(B, S, D_BRANCH)
    return (jax.nn.silu(g.astype(jnp.float32)) * o).astype(g.dtype)

def _memory_cross_attention(h, m, wq, wkv, gq, gk, wo):
    B, S, _ = h.shape
    M = m.shape[1]
    q = _rms_norm((h @ wq).reshape(B, S, XA_HEADS, HEAD_DIM), gq)
    k, v = jnp.split(m @ wkv, 2, axis=-1)
    k = _rms_norm(k.reshape(B, M, XA_HEADS, HEAD_DIM), gk)
    v = v.reshape(B, M, XA_HEADS, HEAD_DIM)
    s = jnp.einsum('bshd,bmhd->bhsm', q, k).astype(jnp.float32) * HEAD_DIM ** -0.5
    p = jax.nn.softmax(s, axis=-1).astype(v.dtype)
    o = jnp.einsum('bhsm,bmhd->bshd', p, v).reshape(B, S, D_XA)
    return o @ wo

def _moe_swiglu(h, router, w_gu, w_down):
    B, S, D = h.shape
    t = h.reshape(B * S, D)
    logits = (t @ router).astype(jnp.float32)
    top_val, top_idx = lax.top_k(logits, TOP_K)
    w = jax.nn.softmax(top_val, axis=-1)
    combine = jnp.einsum('tk,tke->te', w, jax.nn.one_hot(top_idx, N_EXPERTS, dtype=jnp.float32)).astype(t.dtype)
    y = jnp.zeros_like(t)
    for e in range(N_EXPERTS):
        y = y + combine[:, e:e + 1] * _swiglu(t, w_gu[e], w_down[e])
    return y.reshape(B, S, D)

def setup_inputs(seed: int = 0) -> dict:
    key = jax.random.key(seed)
    ks = jax.random.split(key, 32)
    nd, nm = (DEPTH + 1) // 2, DEPTH // 2

    def nrm(k, shape, scale):
        return jax.random.normal(k, shape, jnp.float32) * scale

    def gain(k, shape):
        return 1.0 + 0.02 * jax.random.normal(k, shape, jnp.float32)

    x = nrm(ks[0], (BATCH, SEQ, D_MODEL), 1.0)
    mem = nrm(ks[1], (BATCH, N_MEM, D_MODEL), 1.0)
    offset = jax.random.randint(ks[2], (BATCH, 1), 0, 8192, dtype=jnp.int32)
    positions = (offset + jnp.arange(SEQ, dtype=jnp.int32)[None, :]).astype(jnp.int32)
    return {
        'x': x,
        'mem': mem,
        'positions': positions,
        'norm_mix_g': gain(ks[3], (DEPTH, D_MODEL)),
        'w_in': nrm(ks[4], (DEPTH, D_MODEL, D_IN), D_MODEL ** -0.5),
        'conv_w': nrm(ks[5], (DEPTH, CONV_WIDTH, D_CONV), CONV_WIDTH ** -0.5),
        'conv_b': nrm(ks[6], (DEPTH, D_CONV), 0.02),
        'conv_ln_g': gain(ks[7], (DEPTH, D_CONV)),
        'conv_ln_b': nrm(ks[8], (DEPTH, D_CONV), 0.02),
        'pool_w': nrm(ks[9], (DEPTH, len(POOL_WINDOWS), POOL_GROUP, POOL_GROUP), POOL_GROUP ** -0.5),
        'pool_scale': gain(ks[10], (DEPTH, D_POOL)),
        'w_gate': nrm(ks[11], (DEPTH, N_BRANCH, D_MODEL, D_MODEL), D_MODEL ** -0.5),
        'w_branch': nrm(ks[12], (DEPTH, N_BRANCH, D_BRANCH, D_MODEL), D_BRANCH ** -0.5),
        'w_out': nrm(ks[13], (DEPTH, D_MODEL, D_MODEL), D_MODEL ** -0.5),
        'norm_xa_g': gain(ks[14], (DEPTH, D_MODEL)),
        'norm_mem_g': gain(ks[15], (DEPTH, D_MODEL)),
        'xa_wq': nrm(ks[16], (DEPTH, D_MODEL, D_XA), D_MODEL ** -0.5),
        'xa_wkv': nrm(ks[17], (DEPTH, D_MODEL, 2 * D_XA), D_MODEL ** -0.5),
        'xa_q_norm_g': gain(ks[18], (DEPTH, HEAD_DIM)),
        'xa_k_norm_g': gain(ks[19], (DEPTH, HEAD_DIM)),
        'xa_wo': nrm(ks[20], (DEPTH, D_XA, D_MODEL), D_XA ** -0.5),
        'norm_ffn_g': gain(ks[21], (DEPTH, D_MODEL)),
        'ffn_w_gu': nrm(ks[22], (nd, D_MODEL, 2 * D_FF), D_MODEL ** -0.5),
        'ffn_w_down': nrm(ks[23], (nd, D_FF, D_MODEL), D_FF ** -0.5),
        'moe_router': nrm(ks[24], (nm, D_MODEL, N_EXPERTS), D_MODEL ** -0.5),
        'moe_w_gu': nrm(ks[25], (nm, N_EXPERTS, D_MODEL, 2 * D_FF), D_MODEL ** -0.5),
        'moe_w_down': nrm(ks[26], (nm, N_EXPERTS, D_FF, D_MODEL), D_FF ** -0.5),
    }

def reference(x, mem, positions, norm_mix_g, w_in, conv_w, conv_b, conv_ln_g, conv_ln_b,
              pool_w, pool_scale, w_gate, w_branch, w_out, norm_xa_g, norm_mem_g,
              xa_wq, xa_wkv, xa_q_norm_g, xa_k_norm_g, xa_wo, norm_ffn_g,
              ffn_w_gu, ffn_w_down, moe_router, moe_w_gu, moe_w_down):
    B, S, _ = x.shape
    gammas = 1.0 - jnp.exp2(-5.0 - jnp.arange(RET_HEADS, dtype=jnp.float32))
    for l in range(DEPTH):
        h = _rms_norm(x, norm_mix_g[l])
        u_conv, u_pool, u_sb, u_ret = jnp.split(h @ w_in[l], IN_SPLITS, axis=-1)
        y_conv = _conformer_conv(u_conv, conv_w[l], conv_b[l], conv_ln_g[l], conv_ln_b[l])
        y_pool = _multiscale_pool(u_pool, pool_w[l], pool_scale[l])
        q_sb, k_sb, v_sb = [t.reshape(B, S, SB_HEADS, HEAD_DIM) for t in jnp.split(u_sb, 3, axis=-1)]
        y_sb = _stick_breaking(q_sb, k_sb, v_sb).reshape(B, S, D_BRANCH)
        q_r, k_r, v_r, g_r = jnp.split(u_ret, 4, axis=-1)
        y_ret = _retention(q_r, k_r, v_r, g_r, positions, gammas)
        branches = (y_conv, y_pool, y_sb, y_ret)
        merged = jax.nn.sigmoid(h @ w_gate[l, 0]) * (branches[0].astype(x.dtype) @ w_branch[l, 0])
        for i in range(1, N_BRANCH):
            merged = merged + jax.nn.sigmoid(h @ w_gate[l, i]) * (branches[i].astype(x.dtype) @ w_branch[l, i])
        x = x + merged @ w_out[l]
        x = x + _memory_cross_attention(_rms_norm(x, norm_xa_g[l]), _rms_norm(mem, norm_mem_g[l]),
                                        xa_wq[l], xa_wkv[l], xa_q_norm_g[l], xa_k_norm_g[l], xa_wo[l])
        h = _rms_norm(x, norm_ffn_g[l])
        if l % 2 == 0:
            x = x + _swiglu(h, ffn_w_gu[l // 2], ffn_w_down[l // 2])
        else:
            x = x + _moe_swiglu(h, moe_router[l // 2], moe_w_gu[l // 2], moe_w_down[l // 2])
    return x


_drawn_inputs = setup_inputs


def setup_inputs(seed=0):
    import zlib

    import numpy as np

    out = dict(_drawn_inputs(seed))
    spreads = {}
    factors = {'conv_ln_b': 5.384,
     'norm_xa_g': 4.21,
     'norm_mem_g': 4.115,
     'xa_q_norm_g': 3.724,
     'xa_k_norm_g': 3.507,
     'norm_ffn_g': 4.094}
    for name, (base, spread) in spreads.items():
        noise = np.random.default_rng([zlib.crc32(name.encode()), seed]).standard_normal(out[name].shape)
        drawn = base * np.exp(spread * noise) if base else spread * noise
        out[name] = __import__('jax').numpy.asarray(drawn.astype(out[name].dtype))
    for name, factor in factors.items():
        out[name] = (out[name] * factor).astype(out[name].dtype)
    return out
```

```python
from contextlib import ExitStack

import numpy as np

import concourse.bass as bass
from concourse import mybir

F32 = mybir.dt.float32
F32R = mybir.dt.float32r
I32 = mybir.dt.int32
ALU = mybir.AluOpType
ACT = mybir.ActivationFunctionType
AX = mybir.AxisListType

P = 128
D = 1024
SEQ = 256
TT = SEQ // P
KT = D // P
DEPTH = 2
DB = D // 4
KB = DB // P
NH, HD = 4, 64
D_IN = 10 * DB
CONV_W = 31
WINDOWS = (2, 4, 8, 16)
D_FF = 2816
FB = 256
NF = D_FF // FB
NE = 8
EPS = 1e-6
CH = 2048
RING = 3
NEG = -3.0e38

CH_KV = 0
PER_LAYER = 36
IN0, GATE0, BR0, OUT0, XQ0, XO0 = 0, 10, 26, 30, 34, 35
LAYER0 = [4, 4 + PER_LAYER + 3 * NF]
FF0 = [LAYER0[0] + PER_LAYER, LAYER0[1] + PER_LAYER]
FF_LAP = [(f - 1) // RING for f in FF0]
assert all(f % RING == 1 for f in FF0)
IN_ORDER = (1, 2, 0, 3, 4)
BR_ORDER = (2, 1, 3, 0)

C_ID, C_TRIGE, C_TRILT, C_ONES, C_MASK = 0, 128, 256, 384, 512
C_DECAY = C_MASK + 256
C_BAND = C_DECAY + NH * 256
C_FREQ = C_BAND + 4 * 384
C_E8 = C_FREQ + 32
C_IOTA = C_E8 + 8
C_ALL = C_IOTA + 128


def shape_constants():
    c = np.zeros((P, C_ALL), np.float64)
    k, q = np.arange(P)[:, None], np.arange(P)[None, :]
    q2 = np.arange(SEQ)[None, :]
    c[:, C_ID:C_ID + P] = k == q
    c[:, C_TRIGE:C_TRIGE + P] = k >= q
    c[:, C_TRILT:C_TRILT + P] = k < q
    c[:, C_ONES:C_ONES + P] = 1
    c[:, C_MASK:C_MASK + SEQ] = k < q2
    for j, h in enumerate((0, 2, 1, 3)):
        gamma = np.float64(np.float32(1.0 - 2.0 ** (-5.0 - h)))
        c[:, C_DECAY + j * SEQ:C_DECAY + (j + 1) * SEQ] = np.where(
            q2 >= k, gamma ** np.maximum(q2 - k, 0), 0.0) * HD ** -0.5
    for g, w in enumerate(WINDOWS):
        band = np.where((q2 >= k) & (q2 - k < w), 1.0 / np.minimum(q2 + 1.0, w), 0.0) - (q2 == k)
        late = np.where((q >= k) & (q - k < w), 1.0 / w, 0.0) - (q == k)
        c[:, C_BAND + g * 384:C_BAND + g * 384 + 256] = band
        c[:, C_BAND + g * 384 + 256:C_BAND + (g + 1) * 384] = late
    c[:, C_FREQ:C_FREQ + 32] = 10000.0 ** (-np.arange(32) / 32)
    c[:, C_E8:C_E8 + 8] = 8 - np.arange(8)
    c[:, C_IOTA:C_IOTA + P] = q
    return c.astype(np.float32)


G_MIX, G_XA, G_FFN, G_MEM = 0, 8, 16, 24
G_CB, G_LG, G_LB, G_PS = 64, 68, 72, 76
G_QG, G_KG = 80, 82
G_ROWS = 84

TWO_PI_1 = 6.28125
TWO_PI_2 = float(np.float32(np.round((2 * np.pi - TWO_PI_1) * 2 ** 20) / 2 ** 20))
TWO_PI_3 = float(np.float32(2 * np.pi - TWO_PI_1 - TWO_PI_2))
ROUND = 12582912.0


def trunk(nc, consts, x, mem, positions, norm_mix_g, w_in, conv_w, conv_b, conv_ln_g, conv_ln_b, pool_w,
          pool_scale, w_gate, w_branch, w_out, norm_xa_g, norm_mem_g, xa_wq, xa_wkv, xa_q_norm_g,
          xa_k_norm_g, xa_wo, norm_ffn_g, ffn_w_gu, ffn_w_down, moe_router, moe_w_gu, moe_w_down, out):
    ctx = ExitStack()
    with ctx:
        def sb(name, shape, dt=F32, stack=ctx):
            return stack.enter_context(nc.sbuf_tensor(name, shape, dt))

        def sem(name):
            return ctx.enter_context(nc.semaphore(name))

        raw = [sb(f"raw{j}", [P, CH]) for j in range(RING)]
        w_hi = [sb(f"w_hi{j}", [P, CH], F32R) for j in range(RING)]
        w_lo = [sb(f"w_lo{j}", [P, CH], F32R) for j in range(RING)]
        cst = sb("cst", [P, C_ALL])
        xs = sb("xs", [P, TT, D])
        xn = sb("xn", [P, TT, D])
        merged = sb("merged", [P, TT, D])
        with ExitStack() as s:
            hT_f32 = sb("hT_f32", [P, KT, SEQ], F32, s)
        hT_hi = sb("hT_hi", [P, KT, SEQ], F32R)
        hT_lo = sb("hT_lo", [P, KT, SEQ], F32R)
        memk = sb("memk", [P, DEPTH, KB, SEQ])
        memv = sb("memv", [P, DEPTH, TT, DB])
        qT = sb("qT", [P, KB, SEQ])
        kT = sb("kT", [P, KB, SEQ])
        dT = sb("dT", [P, KB, SEQ])
        vT = sb("vT", [P, KB, CONV_W - 1 + SEQ])
        conv = sb("conv", [P, KB, SEQ])
        convn = sb("convn", [P, TT, DB])
        tmp = sb("tmp", [P, 2, TT, DB])
        gcol = sb("gcol", [P, G_ROWS])
        gqk = sb("gqk", [P, DEPTH])
        cwcol = sb("cwcol", [P, 2 * CONV_W * DEPTH])
        poolw = sb("poolw", [P, DEPTH, 2, 64])
        stat = sb("stat", [P, 8, 8])
        eps_col = sb("eps_col", [P, 1])
        half_pi = sb("half_pi", [P, 1])
        one_col = sb("one_col", [P, 1])
        root = sb("root", [P, 2, 8])
        ss = sb("ss", [P, 2, TT])
        posi = sb("posi", [P, TT], I32)
        trig = sb("trig", [P, 2, TT, 32])
        zm = xn[:].rearrange("p a b -> p (a b)")[:, 0:1536]
        zs = merged[:].rearrange("p a b -> p (a b)")[:, 0:1536]
        with ExitStack() as s:
            U = [sb(f"U{i}", [P, TT, 512], F32, s) for i in range(5)]
        with ExitStack() as s:
            yT = [[sb(f"yT{i}{part}", [P, KB, SEQ], F32R, s) for part in ("hi", "lo")] for i in range(4)]
        yT_extra = sb("u_hold", [P, 5 * 1024])
        with ExitStack() as s:
            gates = sb("gates", [P, 4, TT, D], F32, s)
        with ExitStack() as s:
            memn = sb("memn", [P, TT, D], F32, s)
            mT_hi = sb("mT_hi", [P, KT, SEQ], F32R, s)
            mT_lo = sb("mT_lo", [P, KT, SEQ], F32R, s)
        with ExitStack() as s:
            prob = sb("prob", [P, TT, NH, SEQ], F32, s)
            probT = sb("probT", [P, TT, NH, SEQ], F32, s)
            qn = sb("qn", [P, TT, DB], F32, s)
            on = sb("on", [P, TT, DB], F32, s)
            oT_hi = sb("oT_hi", [P, KB, SEQ], F32R, s)
            oT_lo = sb("oT_lo", [P, KB, SEQ], F32R, s)
        with ExitStack() as s:
            silu = sb("silu", [P, TT, FB], F32, s)
            act = sb("act", [P, TT, FB], F32, s)
            actT_hi = sb("actT_hi", [P, 2, SEQ], F32R, s)
            actT_lo = sb("actT_lo", [P, 2, SEQ], F32R, s)
            eT_hi = sb("eT_hi", [P, KT, P], F32R, s)
            eT_lo = sb("eT_lo", [P, KT, P], F32R, s)
            ye = sb("ye", [P, D], F32, s)
            sel = sb("sel", [P, TT, P], F32, s)
            selw = sb("selw", [P, TT, P], F32, s)
            selwT = sb("selwT", [P, SEQ], F32, s)
            rt = sb("rt", [P, KT, NE], F32, s)
            lg = sb("lg", [P, 12, TT, NE], F32, s)
            posm = sb("posm", [P, TT, 2 * NE], F32, s)
            comb = sb("comb", [P, TT, 2 * NE], F32, s)
            nit = sb("nit", [P, 2], I32, s)
            nitf = sb("nitf", [P, 2], F32, s)
        region_hold = sb("region_hold", [P, 4 * TT * D])
        rows_g, rows_c = tmp[:].rearrange("p a t c -> p (a t c)")[:, 0:128], \
            tmp[:].rearrange("p a t c -> p (a t c)")[:, 128:256]

        ident = cst[:, C_ID:C_ID + P]
        tri_ge = cst[:, C_TRIGE:C_TRIGE + P]
        tri_lt = cst[:, C_TRILT:C_TRILT + P]
        ones = cst[:, C_ONES:C_ONES + P]
        mask = cst[:, C_MASK:C_MASK + SEQ]
        decay = cst[:, C_DECAY:C_DECAY + NH * SEQ].rearrange("p (h q) -> p h q", h=NH)

        A = [ctx.enter_context(nc.psum_tensor(f"A{i}", [P, 512], F32)) for i in range(4)]
        G = [ctx.enter_context(nc.psum_tensor(f"G{i}", [P, 512], F32)) for i in range(2)]
        T = [ctx.enter_context(nc.psum_tensor(f"T{i}", [P, 512], F32)) for i in range(2)]

        landed = [sem(f"landed{j}") for j in range(RING)]
        hi_ready = sem("hi_ready")
        lo_ready = sem("lo_ready")
        used = sem("used")
        half = sem("half")
        act_step = sem("act_step")
        dve_step = sem("dve_step")
        names = {}

        def S(name):
            if name not in names:
                names[name] = sem(name)
            return names[name]

        def slot(k):
            return k % RING

        def number(lap0, k):
            return lap0 * RING + k

        UNIT_L = 14

        def unit_no(l, u):
            return DEPTH + UNIT_L * l + u

        def place(h):
            return (h % 2) * 2 + h // 2

        def half_no(l, j):
            return DEPTH + l * (16 + NF) + j

        block = ctx.enter_context(nc.Block())

        @block.sync
        def _(sp):
            sp.dma_start(memn[:], mem[0].rearrange("(t p) d -> p t d", p=P)).then_inc(S("mem_in"), 16)
            sp.dma_start(cst[:, 0:C_DECAY], consts[:, 0:C_DECAY]).then_inc(S("cst_in"), 16)

            def load(lap0, k, view, src):
                if not isinstance(lap0, int) or number(lap0, k) >= RING:
                    sp.wait_ge(lo_ready, number(lap0, k) - RING + 1)
                if not isinstance(lap0, int):
                    sp.sem_inc(S("asked"), 1)
                for dst, part in halves(view(raw[slot(k)][:]), src):
                    sp.dma_start(dst, part).then_inc(landed[slot(k)], 16)

            def halves(dst, src):
                if len(src.shape) == 4:
                    return [(dst[:, :, t, :], src[:, :, t, :]) for t in range(2)]
                k = src.shape[1] // 2
                return [(dst[:, 0:k], src[:, 0:k]), (dst[:, k:], src[:, k:])]

            def rows4(r):
                return r.rearrange("p (k n) -> p k n", k=4)

            def rows2(r):
                return r.rearrange("p (k n) -> p k n", k=2)

            def rows8(r):
                return r.rearrange("p (k n) -> p k n", k=8)

            def pairs(r):
                return r.rearrange("p (k t c) -> p k t c", k=4, t=2)

            n = 0
            for l in range(DEPTH):
                for c in range(2):
                    load(0, n, rows4, xa_wkv[l].rearrange("(k p) n -> p k n", p=P)[:, 4 * c:4 * c + 4, :])
                    n += 1
                if l == 0:
                    sp.dma_start(xs[:], x[0].rearrange("(t p) d -> p t d", p=P)).then_inc(S("x_in"), 16)
                    sp.dma_start(cst[:, C_DECAY:], consts[:, C_DECAY:]).then_inc(S("cst2_in"), 16)

            def stream_ff(gu, down, lap0, first, prev):
                for f in range(NF):
                    k = 3 * f
                    for c in range(2):
                        load(lap0, k + c + (first and f == 0), pairs, gu[:, 4 * c:4 * c + 4, :, f])
                    if f:
                        load(lap0, k + 2, rows2, down[:, 2 * f - 2:2 * f])
                    elif not first:
                        load(lap0, k + 2, rows2, prev[:, 2 * NF - 2:2 * NF])

            for l in range(DEPTH):
                base = LAYER0[l]
                wi = w_in[l].rearrange("(k p) n -> p k n", p=P)
                for i, b in enumerate(IN_ORDER):
                    for c in range(2):
                        load(0, base + IN0 + 2 * i + c, rows4, wi[:, 4 * c:4 * c + 4, b * 512:b * 512 + 512])
                for g in range(8):
                    wg = w_gate[l, g // 2].rearrange("(k p) n -> p k n", p=P)
                    for c in range(2):
                        load(0, base + GATE0 + 2 * g + c, rows4,
                             wg[:, 4 * c:4 * c + 4, (g % 2) * 512:(g % 2) * 512 + 512])
                for i, b in enumerate(BR_ORDER):
                    load(0, base + BR0 + i, rows2, w_branch[l, b].rearrange("(k p) n -> p k n", p=P))
                wo = w_out[l].rearrange("(k p) n -> p k n", p=P)
                for nb in range(2):
                    for c in range(2):
                        load(0, base + OUT0 + 2 * nb + c, rows4, wo[:, 4 * c:4 * c + 4, nb * 512:nb * 512 + 512])
                load(0, base + XQ0, rows8, xa_wq[l].rearrange("(k p) n -> p k n", p=P))
                load(0, base + XO0, rows2, xa_wo[l].rearrange("(k p) n -> p k n", p=P))
                if l == 0:
                    gu = ffn_w_gu[0].rearrange("(k p) (t f c) -> p k t f c", p=P, t=2, c=FB)
                    down = ffn_w_down[0].rearrange("(k p) n -> p k n", p=P)
                    stream_ff(gu, down, FF_LAP[0], True, None)
                    load(FF_LAP[0], 3 * NF, rows2, down[:, 2 * NF - 2:2 * NF])
            gu_e = moe_w_gu[0].rearrange("e (k p) (t f c) -> e p k t f c", p=P, t=2, c=FB)
            dn_e = moe_w_down[0].rearrange("e (k p) n -> e p k n", p=P)
            stream_ff(gu_e[0], dn_e[0], FF_LAP[1], True, None)
            sp.wait_ge(S("items"), 1)
            items = sp.snap(NE + sp.value_load(nit[0:1, 0:1], min_val=0, max_val=NE))
            with sp.Fori(1, items) as i:
                e = sp.snap(i & (NE - 1))
                p = sp.snap((i + (NE - 1)) & (NE - 1))
                stream_ff(gu_e[bass.ds(e, 1)].rearrange("a p k t f c -> (a p) k t f c"),
                          dn_e[bass.ds(e, 1)].rearrange("a p k n -> (a p) k n"),
                          FF_LAP[1] + NF * i, False,
                          dn_e[bass.ds(p, 1)].rearrange("a p k n -> (a p) k n"))
            load(FF_LAP[1] + NF * items, 0, rows2, dn_e[NE - 1, :, 2 * NF - 2:2 * NF])
            for tt in range(TT):
                sp.wait_ge(S("scattered"), 4 * items - 2 + 2 * tt)
                sp.dma_start(out[0].rearrange("(t p) d -> p t d", p=P)[:, tt], xs[:, tt]).then_inc(S("stored"), 16)
            sp.wait_ge(S("stored"), 16 * TT)

        @block.gpsimd
        def _(pool):
            for base, src in ((G_MIX, norm_mix_g), (G_XA, norm_xa_g), (G_FFN, norm_ffn_g), (G_MEM, norm_mem_g)):
                for l in range(DEPTH):
                    pool.dma_start(rows_g[base + 32 * l:base + 32 * l + KT, :],
                                   src[l].rearrange("(k p) -> k p", p=P)).then_inc(S("rows_in"), 16)
            for base, src in ((G_CB, conv_b), (G_LG, conv_ln_g), (G_LB, conv_ln_b), (G_PS, pool_scale)):
                pool.dma_start(rows_g[base:base + 2 * DEPTH, :],
                               src.rearrange("l (k p) -> (l k) p", p=P)).then_inc(S("rows_in"), 16)
            for base, src in ((G_QG, xa_q_norm_g), (G_KG, xa_k_norm_g)):
                for j in range(2):
                    pool.dma_start(rows_g[base:base + DEPTH, 64 * j:64 * j + 64], src).then_inc(S("rows_in"), 16)
            pool.dma_start(rows_c[0:2 * CONV_W * DEPTH, :],
                           conv_w.rearrange("l w (k p) -> (l w k) p", p=P)).then_inc(S("rows_in"), 16)
            for l in range(DEPTH):
                for j in range(2):
                    pool.dma_start(poolw[64 * j:64 * j + 64, l],
                                   pool_w[l].rearrange("(g j) c d -> j c g d", j=2)[j]).then_inc(S("poolw_in"), 16)
            pool.dma_start(posi[:], positions[0].rearrange("(t p) -> p t", p=P),
                           allow_slow_non_contiguous=True).then_inc(S("pos_in"), 16)
            for l in range(DEPTH):
                for i in range(1, 4):
                    for nb in range(2):
                        for tt in range(TT):
                            step = 16 * l + 4 * i + 2 * nb + tt
                            pool.wait_ge(S("prod"), step + 1)
                            if i > 1:
                                pool.wait_ge(S("summed"), 12 * l + 4 * (i - 1) + 2 * nb + tt - 3)
                            b = BR_ORDER[i]
                            sl = slice(nb * 512, nb * 512 + 512)
                            pool.tensor_tensor(merged[:, tt, sl], merged[:, tt, sl], gates[:, b, tt, sl],
                                               ALU.add).then_inc(S("summed"), 1)
            pool.wait_ge(S("xo_added"), 4 * DEPTH)
            pool.dma_start(rt[:], moe_router[0].rearrange("(k p) e -> p k e", p=P)).then_inc(S("rt_in"), 16)
            pool.dma_start(merged[:, 0, :], norm_ffn_g[DEPTH - 1:DEPTH, :].to_broadcast([P, D])).then_inc(S("rt_in"), 16)

        @block.tensor
        def _(pe):
            def product(dst, a_hi, a_lo, b_hi, b_lo, first, last):
                pe.matmul(dst, a_hi, b_hi, start=first, stop=False)
                pe.matmul(dst, a_lo, b_hi, start=False, stop=False)
                return pe.matmul(dst, a_hi, b_lo, start=False, stop=last)

            def have(lap0, k):
                pe.wait_ge(lo_ready, number(lap0, k) + 1)

            def streamed(n0, hi, lo, free, nchunks=2, kts=4, width=512):
                for c in range(nchunks):
                    n = n0 + c
                    have(0, n)
                    wh = w_hi[slot(n)][:].rearrange("p (k n) -> p k n", k=kts)
                    wl = w_lo[slot(n)][:].rearrange("p (k n) -> p k n", k=kts)
                    for tt in range(TT):
                        if c == 0 and free[tt]:
                            pe.wait_ge(*free[tt])
                        for k in range(kts):
                            kk = c * kts + k
                            mm = product(G[tt][:, 0:width], hi[:, kk, tt * P:tt * P + P], lo[:, kk, tt * P:tt * P + P],
                                         wh[:, k, :], wl[:, k, :], kk == 0, kk == nchunks * kts - 1)
                        if tt == 0 and c == nchunks - 1:
                            mm.then_inc(half, 1)
                    mm.then_inc(used, 1)

            def transpose_wide(src, done):
                for kt in range(KT):
                    for tt in range(TT):
                        mm = pe.transpose(A[kt // 2][:, (kt % 2) * 256 + tt * P:(kt % 2) * 256 + tt * P + P],
                                          src[:, tt, kt * P:kt * P + P], ident)
                    if kt % 2:
                        mm.then_inc(done, 1)

            def transpose_narrow(dst, src):
                for c in range(KB):
                    for tt in range(TT):
                        mm = pe.transpose(dst[:, c * SEQ + tt * P:c * SEQ + tt * P + P],
                                          src(tt, slice(c * P, c * P + P)), ident)
                return mm

            def scores(q, k, done):
                for h in range(NH):
                    r = slice((h % 2) * HD, (h % 2) * HD + HD)
                    pe.matmul(A[1 + h % 2][:, (h // 2) * SEQ:(h // 2) * SEQ + SEQ], k[r, h // 2, 0:P], q[r, h // 2, :],
                              start=True, stop=True)
                for h in (0, 2, 1, 3):
                    r = slice((h % 2) * HD, (h % 2) * HD + HD)
                    j = place(h)
                    mm = pe.matmul(A[3][:, j * P:j * P + P], k[r, h // 2, P:SEQ], q[r, h // 2, P:SEQ],
                                   start=True, stop=True)
                    if h == 2:
                        rows[0] += 1
                        mm.then_inc(S("even_heads"), 1)
                        pe.wait_ge(S("even_heads"), rows[0])
                mm.then_inc(done, 1)

            rows = [0]

            pe.wait_ge(S("cst_in"), 16)
            pe.wait_ge(S("rows_in"), 16 * 17)
            pe.transpose(T[0][:, 0:G_ROWS], rows_g[0:G_ROWS, :], ident[0:G_ROWS, 0:G_ROWS])
            pe.transpose(T[0][:, 128:128 + 2 * CONV_W * DEPTH], rows_c[0:2 * CONV_W * DEPTH, :],
                         ident[0:2 * CONV_W * DEPTH, 0:2 * CONV_W * DEPTH]).then_inc(S("cols"), 1)
            pe.wait_ge(S("mem_normed"), TT)
            transpose_wide(memn, S("memT"))
            for l in range(DEPTH):
                pe.wait_ge(S("mT_hi"), 4 * (l + 1))
                pe.wait_ge(S("mT_lo"), 4 * (l + 1))
                free = [None, None] if l == 0 else [(S("emptied"), 2 * l - 1), (S("emptied"), 2 * l)]
                streamed(CH_KV + 2 * l, mT_hi, mT_lo, free)
                pe.wait_ge(S("mk_normed"), l + 1)
                if l == 0:
                    pe.wait_ge(S("cols_out"), 1)
                transpose_narrow(T[l][:], lambda tt, c: tmp[:, 0, tt, c]).then_inc(S("memkT"), 1)

            def after_unit(l, u):
                n = unit_no(l, u)
                return [(S("emptied"), 2 * n - 1), (S("emptied"), 2 * n)]

            for l in range(DEPTH):
                base = LAYER0[l]
                pe.wait_ge(S("normed"), TT * (3 * l + 1))
                if l == 0:
                    pe.wait_ge(S("mT_lo"), 4 * DEPTH)
                    pe.wait_ge(S("mT_hi"), 4 * DEPTH)
                else:
                    pe.wait_ge(S("ffn_added"), 4)
                transpose_wide(xn, S("xnT"))
                pe.wait_ge(S("hT_hi"), 4 * (3 * l + 1))
                pe.wait_ge(S("hT_lo"), 4 * (3 * l + 1))
                if l == 0:
                    free0 = [(S("emptied"), 2 * DEPTH - 1), (S("emptied"), 2 * DEPTH)]
                else:
                    free0 = [(S("ff_act"), 2 * NF - 1), (S("ff_act"), 2 * NF)]
                streamed(base + IN0, hT_hi, hT_lo, free0)
                streamed(base + IN0 + 2, hT_hi, hT_lo, after_unit(l, 1))
                streamed(base + IN0 + 4, hT_hi, hT_lo, after_unit(l, 2))
                pe.wait_ge(S("emptied"), 2 * unit_no(l, 2))
                if l == 0:
                    pe.wait_ge(S("memk_out"), DEPTH)
                else:
                    pe.wait_ge(S("actT_hi"), NF)
                    pe.wait_ge(S("actT_lo"), NF)
                transpose_narrow(T[0][:], lambda tt, c: U[1][:, tt, 256 + c.start:256 + c.stop])
                transpose_narrow(T[1][:], lambda tt, c: U[2][:, tt, c]).then_inc(S("sb_qk"), 1)
                pe.wait_ge(S("cst2_in"), 16) if l == 0 else None
                for g in range(4):
                    o = A[0][(g % 2) * 64:(g % 2) * 64 + 64, (g // 2) * SEQ:(g // 2) * SEQ + SEQ]
                    c0 = C_BAND + g * 384
                    pe.matmul(o, U[1][:, 0, g * 64:g * 64 + 64], cst[:, c0:c0 + 256], start=True, stop=False)
                    mm = pe.matmul(A[0][(g % 2) * 64:(g % 2) * 64 + 64, (g // 2) * SEQ + P:(g // 2) * SEQ + SEQ],
                                   U[1][:, 1, g * 64:g * 64 + 64], cst[:, c0 + 256:c0 + 384], start=False, stop=True)
                mm.then_inc(S("pool_d"), 1)
                streamed(base + IN0 + 6, hT_hi, hT_lo, after_unit(l, 3))
                pe.wait_ge(S("sb_qk_out"), l + 1)
                scores(qT, kT, S("sb_z"))
                pe.wait_ge(S("dT_out"), l + 1)
                if l == 0:
                    pe.wait_ge(S("poolw_in"), 16 * 4)
                for g in range(4):
                    r = slice((g % 2) * 64, (g % 2) * 64 + 64)
                    mm = pe.matmul(T[0][r, (g // 2) * SEQ:(g // 2) * SEQ + SEQ], poolw[r, l, g // 2, :], dT[r, g // 2, :],
                                   start=True, stop=True)
                mm.then_inc(S("pool_y"), 1)
                streamed(base + IN0 + 8, hT_hi, hT_lo, after_unit(l, 4))
                pe.wait_ge(S("conv_v"), l + 1)
                transpose_narrow(T[1][:], lambda tt, c: convn[:, tt, c]).then_inc(S("conv_vT"), 1)

                def gate(g):
                    streamed(base + GATE0 + 2 * g, hT_hi, hT_lo, after_unit(l, 5 + g))

                gate(0)
                pe.wait_ge(S("sb_sp"), l + 1)
                for j in range(NH):
                    zk0 = zs[:, j * SEQ:j * SEQ + SEQ]
                    zk1 = zs[:, NH * SEQ + j * P:NH * SEQ + j * P + P]
                    o = A[1 + j // 2]
                    pe.matmul(o[:, (j % 2) * SEQ:(j % 2) * SEQ + SEQ], tri_ge, zk0, start=True, stop=False)
                    pe.matmul(o[:, (j % 2) * SEQ + P:(j % 2) * SEQ + SEQ], ones, zk1, start=False, stop=True)
                mm = pe.matmul(A[3][:], tri_ge, zs[:, NH * SEQ:NH * SEQ + NH * P], start=True, stop=True)
                mm.then_inc(S("sb_tail"), 1)
                gate(1)
                pe.wait_ge(S("rotated"), l + 1)
                pe.wait_ge(S("yT_lo1"), l + 1)
                pe.wait_ge(S("vT_out"), l + 1)
                transpose_narrow(T[0][:], lambda tt, c: U[3][:, tt, c])
                transpose_narrow(T[1][:], lambda tt, c: U[3][:, tt, 256 + c.start:256 + c.stop]).then_inc(S("ret_qk"), 1)
                gate(2)
                pe.wait_ge(S("sb_a"), l + 1)
                for h in (0, 2, 1, 3):
                    r = slice((h % 2) * HD, (h % 2) * HD + HD)
                    c0 = (h // 2) * SEQ
                    pe.matmul(A[0][r, c0:c0 + SEQ], U[2][:, 0, 256 + h * HD:256 + h * HD + HD],
                              zm[:, place(h) * SEQ:place(h) * SEQ + SEQ], start=True, stop=False)
                    mm = pe.matmul(A[0][r, c0 + P:c0 + SEQ], U[2][:, 1, 256 + h * HD:256 + h * HD + HD],
                                   zm[:, NH * SEQ + place(h) * P:NH * SEQ + place(h) * P + P], start=False, stop=True)
                mm.then_inc(S("sb_y"), 1)
                gate(3)
                pe.wait_ge(S("ret_qk_out"), l + 1)
                pe.wait_ge(S("sb_w"), l + 1)
                scores(qT, kT, S("ret_z"))
                gate(4)
                pe.wait_ge(S("ret_a"), l + 1)
                for tt in range(TT):
                    for h in range(NH):
                        o = T[1][:, tt * DB + h * HD:tt * DB + h * HD + HD]
                        mm = pe.matmul(o, zs[:, place(h) * SEQ + tt * P:place(h) * SEQ + tt * P + P], U[4][:, 0, h * HD:h * HD + HD],
                                       start=True, stop=(tt == 0))
                        if tt:
                            mm = pe.matmul(o, zs[:, NH * SEQ + place(h) * P:NH * SEQ + place(h) * P + P],
                                           U[4][:, 1, h * HD:h * HD + HD], start=False, stop=True)
                mm.then_inc(S("ret_o"), 1)
                gate(5)
                pe.wait_ge(S("tap"), KB * CONV_W * (l + 1))
                for c in range(KB):
                    for tt in range(TT):
                        mm = pe.transpose(T[0][:, tt * DB + c * P:tt * DB + c * P + P], conv[:, c, tt * P:tt * P + P],
                                          ident)
                mm.then_inc(S("conv_nat"), 1)
                gate(6)
                pe.wait_ge(S("ret_y"), l + 1)
                transpose_narrow(A[1][:], lambda tt, c: tmp[:, 0, tt, c]).then_inc(S("ret_yT"), 1)
                gate(7)
                pe.wait_ge(S("conv_ln"), l + 1)
                transpose_narrow(A[2][:], lambda tt, c: convn[:, tt, c]).then_inc(S("conv_lnT"), 1)
                for i, b in enumerate(BR_ORDER):
                    n = base + BR0 + i
                    pe.wait_ge(S(f"yT_lo{b}"), l + 1)
                    pe.wait_ge(S(f"yT_hi{b}"), l + 1)
                    have(0, n)
                    wh = w_hi[slot(n)][:].rearrange("p (k n) -> p k n", k=2)
                    wl = w_lo[slot(n)][:].rearrange("p (k n) -> p k n", k=2)
                    for nb in range(2):
                        for tt in range(TT):
                            if i:
                                pe.wait_ge(S("prod"), 16 * l + 4 * (i - 1) + 2 * nb + tt + 1)
                            elif nb == 0:
                                pe.wait_ge(S("emptied"), 2 * unit_no(l, 13))
                            for k in range(KB):
                                mm = product((G, T)[nb][tt][:], yT[b][0][:, k, tt * P:tt * P + P],
                                             yT[b][1][:, k, tt * P:tt * P + P], wh[:, k, nb * 512:nb * 512 + 512],
                                             wl[:, k, nb * 512:nb * 512 + 512], k == 0, k == KB - 1)
                            if nb == 0 or tt == 0:
                                mm.then_inc(S("branch"), 1)
                    mm.then_inc(used, 1)
                pe.wait_ge(S("summed"), 12 * (l + 1))
                pe.wait_ge(S("yT_lo0"), l + 1)
                transpose_wide(merged, S("mergedT"))
                pe.wait_ge(S("gT_hi"), 4 * (l + 1))
                pe.wait_ge(S("gT_lo"), 4 * (l + 1))
                done = 16 * (l + 1)
                streamed(base + OUT0, hT_hi, hT_lo, [(S("prod"), done), (S("prod"), done)])
                streamed(base + OUT0 + 2, hT_hi, hT_lo, [(S("out_added"), 4 * l + 1), (S("out_added"), 4 * l + 2)])
                pe.wait_ge(S("normed"), TT * (3 * l + 2))
                transpose_wide(xn, S("xnT"))
                pe.wait_ge(S("hT_hi"), 4 * (3 * l + 2))
                pe.wait_ge(S("hT_lo"), 4 * (3 * l + 2))
                streamed(base + XQ0, hT_hi, hT_lo, [(S("out_added"), 4 * l + 3), (S("out_added"), 4 * l + 4)],
                         nchunks=1, kts=8, width=256)
                pe.wait_ge(S("q_normed"), l + 1)
                transpose_narrow(T[0][:], lambda tt, c: qn[:, tt, c]).then_inc(S("xqT"), 1)
                pe.wait_ge(S("xqT_out"), l + 1)
                for tt in range(TT):
                    for h in range(NH):
                        r = slice((h % 2) * HD, (h % 2) * HD + HD)
                        mm = pe.matmul(A[2 * tt + h % 2][:, (h // 2) * SEQ:(h // 2) * SEQ + SEQ],
                                       qT[r, h // 2, tt * P:tt * P + P], memk[r, l, h // 2, :], start=True, stop=True)
                    mm.then_inc(S("x_scores"), 1)
                for tt in range(TT):
                    pe.wait_ge(S("xp"), 4 * TT * l + 4 * tt + 4)
                    for j in range(NH):
                        for mt in range(TT):
                            mm = pe.transpose(A[2 * tt + j // 2][:, (j % 2) * SEQ + mt * P:(j % 2) * SEQ + mt * P + P],
                                              prob[:, tt, j, mt * P:mt * P + P], ident)
                    mm.then_inc(S("xpT"), 1)
                pe.wait_ge(S("xpT_out"), 4 * (l + 1))
                for tt in range(TT):
                    for h in range(NH):
                        for mt in range(TT):
                            mm = pe.matmul(T[1][:, tt * DB + h * HD:tt * DB + h * HD + HD],
                                           probT[:, tt, place(h), mt * P:mt * P + P], memv[:, l, mt, h * HD:h * HD + HD],
                                           start=(mt == 0), stop=(mt == TT - 1))
                mm.then_inc(S("xo"), 1)
                pe.wait_ge(S("xo_normed"), l + 1)
                transpose_narrow(T[0][:], lambda tt, c: on[:, tt, c]).then_inc(S("xoT"), 1)
                pe.wait_ge(S("oT_hi"), l + 1)
                pe.wait_ge(S("oT_lo"), l + 1)
                n = base + XO0
                have(0, n)
                wh = w_hi[slot(n)][:].rearrange("p (k n) -> p k n", k=2)
                wl = w_lo[slot(n)][:].rearrange("p (k n) -> p k n", k=2)
                for nb in range(2):
                    for tt in range(TT):
                        if nb == 0:
                            pe.wait_ge(S("emptied"), 2 * unit_no(l, 13) + 1 + tt)
                        for k in range(KB):
                            mm = product((G, T)[nb][tt][:], oT_hi[:, k, tt * P:tt * P + P],
                                         oT_lo[:, k, tt * P:tt * P + P], wh[:, k, nb * 512:nb * 512 + 512],
                                         wl[:, k, nb * 512:nb * 512 + 512], k == 0, k == KB - 1)
                        if nb == 0 or tt == 0:
                            mm.then_inc(S("xproj"), 1)
                mm.then_inc(used, 1)
                pe.wait_ge(S("normed"), TT * (3 * l + 3))
                transpose_wide(xn, S("xnT"))
                if l:
                    break
                pe.wait_ge(S("hT_hi"), 4 * (3 * l + 3))
                pe.wait_ge(S("hT_lo"), 4 * (3 * l + 3))
                pe.wait_ge(S("xo_added"), 4 * (l + 1))

                def transposed_act(f):
                    pe.wait_ge(S("ff_act"), 2 * (f + 1))
                    if f:
                        pe.wait_ge(S("actT_hi"), f)
                        pe.wait_ge(S("actT_lo"), f)
                    transpose_narrow(T[0][:], lambda tt, c: act[:, tt, c]).then_inc(S("ff_actT"), 1)

                def down(f):
                    n = number(FF_LAP[0], 3 * f + 5 if f < NF - 1 else 3 * NF)
                    have(0, n)
                    pe.wait_ge(S("actT_hi"), f + 1)
                    pe.wait_ge(S("actT_lo"), f + 1)
                    wh = w_hi[slot(n)][:].rearrange("p (k n) -> p k n", k=2)
                    wl = w_lo[slot(n)][:].rearrange("p (k n) -> p k n", k=2)
                    for tt in range(TT):
                        for nb in range(2):
                            for k in range(2):
                                mm = product(A[2 * tt + nb][:], actT_hi[:, k, tt * P:tt * P + P],
                                             actT_lo[:, k, tt * P:tt * P + P], wh[:, k, nb * 512:nb * 512 + 512],
                                             wl[:, k, nb * 512:nb * 512 + 512], f == 0 and k == 0,
                                             f == NF - 1 and k == 1)
                    mm.then_inc(used, 1)

                for f in range(NF):
                    for c in range(2):
                        n = number(FF_LAP[0], 3 * f + c + (f == 0))
                        have(0, n)
                        wh = w_hi[slot(n)][:].rearrange("p (k n) -> p k n", k=4)
                        wl = w_lo[slot(n)][:].rearrange("p (k n) -> p k n", k=4)
                        for tt in range(TT):
                            if c == 0 and f:
                                pe.wait_ge(S("ff_act"), 2 * f - 1 + tt)
                            for k in range(4):
                                mm = product(G[tt][:], hT_hi[:, 4 * c + k, tt * P:tt * P + P],
                                             hT_lo[:, 4 * c + k, tt * P:tt * P + P], wh[:, k, :], wl[:, k, :],
                                             c + k == 0, c == 1 and k == 3)
                            if c == 1 and tt == 0:
                                mm.then_inc(half, 1)
                        mm.then_inc(used, 1)
                        if f and c == 0:
                            transposed_act(f - 1)
                    if f:
                        down(f - 1)
                transposed_act(NF - 1)
                down(NF - 1)

            pe.wait_ge(S("rhT"), 4)
            pe.wait_ge(S("rt_in"), 32)
            pe.wait_ge(S("xo_added"), 4 * DEPTH)
            for tt in range(TT):
                for k in range(KT):
                    mm = pe.matmul(T[0][:, tt * NE:tt * NE + NE], hT_f32[:, k, tt * P:tt * P + P], rt[:, k, :],
                                   start=(k == 0), stop=(k == KT - 1))
            mm.then_inc(S("logits"), 1)
            pe.wait_ge(S("picked"), 1)
            pe.matmul(T[1][:, 0:NE], tri_lt, lg[:, 6, 0, :], start=True, stop=True)
            pe.matmul(T[1][:, NE:2 * NE], ones, lg[:, 6, 0, :], start=True, stop=False)
            pe.matmul(T[1][:, NE:2 * NE], tri_lt, lg[:, 6, 1, :], start=False, stop=True)
            pe.matmul(T[1][:, 2 * NE:3 * NE], ones, lg[:, 6, 0, :], start=True, stop=False)
            pe.matmul(T[1][:, 2 * NE:3 * NE], ones, lg[:, 6, 1, :], start=False, stop=True).then_inc(S("counted"), 1)
            pe.wait_ge(S("items"), 1)
            items = pe.snap(NE + pe.value_load(nit[0:1, 0:1], min_val=0, max_val=NE))
            GB = [G[0], G[1], T[1]]

            def gather(i):
                pe.wait_ge(S("sel"), i + 1)
                for k in range(KT):
                    for tt in range(TT):
                        mm = pe.matmul(A[2 + k // 4][:, (k % 4) * P:(k % 4) * P + P], xn[:, tt, k * P:k * P + P],
                                       sel[:, tt, :], start=(tt == 0), stop=(tt == TT - 1))
                mm.then_inc(S("gathered"), 1)

            def turn_selection(i):
                for tt in range(TT):
                    mm = pe.transpose(T[0][:, 256 + tt * P:256 + tt * P + P], selw[:, tt, :], ident)
                mm.then_inc(S("selT"), 1)

            def e_transposed(step, turned=None):
                pe.wait_ge(S("e_act"), step + 1)
                if turned is not None:
                    pe.wait_ge(S("selT_out"), turned)
                for c in range(2):
                    mm = pe.transpose(T[0][:, c * P:c * P + P], act[:, 0, c * P:c * P + P], ident)
                mm.then_inc(S("e_actT"), 1)

            def e_down(lap0, k, step, f):
                have(lap0, k)
                pe.wait_ge(S("e_aT_hi"), step + 1)
                pe.wait_ge(S("e_aT_lo"), step + 1)
                wh = w_hi[slot(k)][:].rearrange("p (k n) -> p k n", k=2)
                wl = w_lo[slot(k)][:].rearrange("p (k n) -> p k n", k=2)
                for nb in range(2):
                    for kk in range(2):
                        mm = product(A[nb][:], actT_hi[:, kk, 0:P], actT_lo[:, kk, 0:P],
                                     wh[:, kk, nb * 512:nb * 512 + 512], wl[:, kk, nb * 512:nb * 512 + 512],
                                     f == 0 and kk == 0, f == NF - 1 and kk == 1)
                mm.then_inc(used, 1)

            def scatter(i, tt):
                pe.wait_ge(S("ye"), 2 * i + 2)
                pe.wait_ge(S("selT_out"), i + 1)
                if tt:
                    pe.wait_ge(S("scattered"), 4 * i + 2)
                for nb in range(2):
                    mm = pe.matmul(A[2 + nb][:], selwT[:, tt * P:tt * P + P], ye[:, nb * 512:nb * 512 + 512],
                                   start=True, stop=True)
                mm.then_inc(S("scat"), 1)

            def item(i, first=False, last=False):
                lap0 = FF_LAP[1] + NF * i
                pe.wait_ge(S("eT_lo"), 2 * i + 2)
                pe.wait_ge(S("eT_hi"), 2 * i + 2)
                for f in range(NF):
                    step = NF * i + f
                    for c in range(2):
                        k = 3 * f + c + (first and f == 0)
                        have(lap0, k)
                        if c == 0 and (f >= 3 or not first):
                            back = (2, 2, 5)[f] if f < 3 else 3
                            pe.wait_ge(S("e_act"), step - back + 1)
                        wh = w_hi[slot(k)][:].rearrange("p (k n) -> p k n", k=4)
                        wl = w_lo[slot(k)][:].rearrange("p (k n) -> p k n", k=4)
                        for kk in range(4):
                            mm = product(GB[f % 3][:], eT_hi[:, 4 * c + kk, :], eT_lo[:, 4 * c + kk, :],
                                         wh[:, kk, :], wl[:, kk, :], c + kk == 0, c == 1 and kk == 3)
                        mm.then_inc(used, 1)
                        if c == 0 and not (first and f == 0):
                            e_transposed(step - 1, i + 1 if f == 5 else None)
                    if f:
                        if f == 1 and not first:
                            pe.wait_ge(S("ye"), 2 * i)
                        e_down(lap0, 3 * f + 2, step - 1, f - 1)
                    elif not first:
                        e_down(lap0, 2, step - 1, NF - 1)
                    if f in (1, 2) and not first:
                        scatter(i - 1, f - 1)
                    if f == 4:
                        turn_selection(i)
                    if f == 8 and not last:
                        if not first:
                            pe.wait_ge(S("scattered"), 4 * i)
                        gather(i + 1)

            gather(0)
            item(0, first=True)
            with pe.Fori(1, items - 1) as i:
                item(i)
            last = pe.snap(items - 1)
            item(last, last=True)
            e_transposed(last * NF + NF - 1)
            e_down(FF_LAP[1] + NF * items, 0, last * NF + NF - 1, NF - 1)
            scatter(last, 0)
            scatter(last, 1)

        @block.scalar
        def _(act_e):
            steps = [0]

            def link(ins):
                steps[0] += 1
                ins.then_inc(act_step, 1)
                act_e.wait_ge(act_step, steps[0])

            nxt = [0]

            def split_to(k_end, lap0=0):
                while nxt[0] < k_end:
                    k = nxt[0]
                    act_e.wait_ge(landed[slot(k)], 32 * (lap0 + k // RING + 1))
                    if not isinstance(lap0, int) or number(lap0, k) >= RING:
                        act_e.wait_ge(used, number(lap0, k) - RING + 1)
                    nc.scalar.activation(w_hi[slot(k)][:], raw[slot(k)][:], ACT.Copy).then_inc(hi_ready, 1)
                    nxt[0] += 1

            def ahead(k, lap0=0):
                split_to(k + RING, lap0)

            def squares(src, junk):
                for tt in range(TT):
                    link(nc.scalar.activation(junk[:, tt, :], src[:, tt, :], ACT.Square, accum_out=ss[:, 0, tt:tt + 1]))
                for tt in range(TT):
                    nc.scalar.activation(ss[:, 1, tt:tt + 1], ss[:, 0, tt:tt + 1], ACT.Sqrt, scale=1.0 / D,
                                         bias=eps_col[:, 0:1]).then_inc(S("squared"), 1)

            roots = [0]

            def square_root():
                roots[0] += 1
                act_e.wait_ge(S("mean_square"), roots[0])
                nc.scalar.activation(root[:, 1, :], root[:, 0, :], ACT.Sqrt).then_inc(S("rooted"), 1)

            def round_wide(dst, gain, done, ready, count, count_done):
                for b in range(4):
                    act_e.wait_ge(ready, count + b + 1)
                    for kt in (2 * b, 2 * b + 1):
                        bank = A[b][:, (kt % 2) * SEQ:(kt % 2) * SEQ + SEQ]
                        ins = nc.scalar.activation(dst[:, kt, :], bank, ACT.Copy, scale=gcol[:, gain + kt:gain + kt + 1])
                    ins.then_inc(done, 1)

            act_e.wait_ge(S("mem_in"), 16)
            act_e.wait_ge(S("eps_set"), 3)
            squares(memn, merged)
            split_to(2)
            act_e.wait_ge(S("cols"), 1)
            nc.scalar.activation(gcol[:], T[0][:, 0:G_ROWS], ACT.Copy)
            nc.scalar.activation(cwcol[:], T[0][:, 128:128 + 2 * CONV_W * DEPTH], ACT.Copy).then_inc(S("cols_out"), 1)
            act_e.wait_ge(S("cols_out"), 1)
            round_wide(mT_hi, G_MEM, S("mT_hi"), S("memT"), 0, 0)
            for l in range(DEPTH):
                n = CH_KV + 2 * l + 1
                ahead(n - 1)
                for tt in range(TT):
                    if tt == 0:
                        act_e.wait_ge(half, l + 1)
                        if l:
                            act_e.wait_ge(S("mk_normed"), l)
                    else:
                        act_e.wait_ge(used, n + 1)
                    nc.scalar.activation(convn[:, tt, :], G[tt][:, 0:DB], ACT.Copy)
                    nc.scalar.activation(memv[:, l, tt, :], G[tt][:, DB:2 * DB], ACT.Copy).then_inc(S("emptied"), 1)
                square_root()
                if l + 1 < DEPTH:
                    round_wide(mT_hi, G_MEM + 32 * (l + 1), S("mT_hi"), S("memT"), 0, 0)
                ahead(n)
                act_e.wait_ge(S("memkT"), l + 1)
                nc.scalar.activation(memk[:, l].rearrange("p c t -> p (c t)"), T[l][:], ACT.Copy).then_inc(S("memk_out"), 1)

            for l in range(DEPTH):
                base = LAYER0[l]
                if l == 0:
                    act_e.wait_ge(S("x_in"), 16)
                else:
                    act_e.wait_ge(S("ffn_added"), 4)
                squares(xs, xn)
                round_wide(hT_hi, G_MIX + 32 * l, S("hT_hi"), S("xnT"), 12 * l, 0)

                def unit(u, n, evacuate):
                    ahead(n)
                    for tt in range(TT):
                        if tt == 0:
                            act_e.wait_ge(half, half_no(l, u if u < 13 else 15) + 1)
                        else:
                            act_e.wait_ge(used, n + 1)
                        evacuate(tt).then_inc(S("emptied"), 1)

                def whole(b):
                    return lambda tt: nc.scalar.activation(U[b][:, tt, :], G[tt][:], ACT.Copy)

                def two(b, func):
                    def evacuate(tt):
                        nc.scalar.activation(U[b][:, tt, 0:DB], G[tt][:, 0:DB], ACT.Copy)
                        return nc.scalar.activation(U[b][:, tt, DB:], G[tt][:, DB:], func)
                    return evacuate

                unit(0, base + 1, whole(1))
                unit(1, base + 3, whole(2))
                unit(2, base + 5, two(0, ACT.Sigmoid))
                act_e.wait_ge(S("sb_qk"), l + 1)
                nc.scalar.activation(qT[:].rearrange("p c t -> p (c t)"), T[0][:], ACT.Copy, scale=HD ** -0.5)
                nc.scalar.activation(kT[:].rearrange("p c t -> p (c t)"), T[1][:], ACT.Copy).then_inc(S("sb_qk_out"), 1)
                act_e.wait_ge(S("pool_d"), l + 1)
                nc.scalar.activation(dT[:].rearrange("p c t -> p (c t)"), A[0][:], ACT.Copy).then_inc(S("dT_out"), 1)
                if l == 0:
                    act_e.wait_ge(S("angles"), 1)
                    ang = tmp[:, 1].rearrange("p t c -> p (t c)")
                    link(nc.scalar.activation(ang[:, 64:128], ang[:, 0:64], ACT.Abs))
                    nc.scalar.activation(trig[:, 1].rearrange("p t c -> p (t c)"), ang[:, 0:64], ACT.Sin)
                    nc.scalar.activation(trig[:, 0].rearrange("p t c -> p (t c)"), ang[:, 64:128],
                                         ACT.Sin, scale=-1.0, bias=half_pi[:, 0:1]).then_inc(S("trig"), 1)
                unit(3, base + 7, whole(3))
                act_e.wait_ge(S("pool_y"), l + 1)
                for c in range(KB):
                    ins = nc.scalar.activation(yT[1][0][:, c, :], T[0][:, c * SEQ:c * SEQ + SEQ], ACT.Copy,
                                               scale=gcol[:, G_PS + 2 * l + c:G_PS + 2 * l + c + 1])
                ins.then_inc(S("yT_hi1"), 1)
                unit(4, base + 9, two(4, ACT.Silu))
                act_e.wait_ge(S("conv_vT"), l + 1)
                nc.scalar.activation(vT[:, :, CONV_W - 1:], T[1][:].rearrange("p (c t) -> p c t", c=KB),
                                     ACT.Copy).then_inc(S("vT_out"), 1)
                act_e.wait_ge(S("sb_zm"), l + 1)
                link(nc.scalar.activation(zs, zm, ACT.Abs))
                link(nc.scalar.activation(zs, zs, ACT.Exp, scale=-1.0))
                nc.scalar.activation(zs, zs, ACT.Ln, bias=one_col[:, 0:1]).then_inc(S("sb_l"), 1)

                def gate(g):
                    unit(5 + g, base + GATE0 + 2 * g + 1, lambda tt: nc.scalar.activation(
                        gates[:, g // 2, tt, (g % 2) * 512:(g % 2) * 512 + 512], G[tt][:], ACT.Sigmoid))

                gate(0)
                gate(1)
                act_e.wait_ge(S("sb_w"), l + 1)
                nc.scalar.activation(zm, zm, ACT.Exp).then_inc(S("sb_exp"), 1)
                act_e.wait_ge(S("ret_qk"), l + 1)
                nc.scalar.activation(qT[:].rearrange("p c t -> p (c t)"), T[0][:], ACT.Copy)
                nc.scalar.activation(kT[:].rearrange("p c t -> p (c t)"), T[1][:], ACT.Copy).then_inc(S("ret_qk_out"), 1)
                gate(2)
                gate(3)
                act_e.wait_ge(S("sb_y"), l + 1)
                nc.scalar.activation(yT[2][0][:].rearrange("p c t -> p (c t)"), A[0][:], ACT.Copy).then_inc(S("yT_hi2"), 1)
                gate(4)
                gate(5)
                square_root()
                gate(6)
                square_root()
                gate(7)
                act_e.wait_ge(S("ret_yT"), l + 1)
                nc.scalar.activation(yT[3][0][:].rearrange("p c t -> p (c t)"), A[1][:], ACT.Copy).then_inc(S("yT_hi3"), 1)
                act_e.wait_ge(S("conv_lnT"), l + 1)
                for c in range(KB):
                    g0, b0 = G_LG + 2 * l + c, G_LB + 2 * l + c
                    link(nc.scalar.activation(conv[:, c, :], A[2][:, c * SEQ:c * SEQ + SEQ], ACT.Silu,
                                              scale=gcol[:, g0:g0 + 1], bias=gcol[:, b0:b0 + 1]))
                nc.scalar.activation(yT[0][0][:], conv[:], ACT.Copy).then_inc(S("yT_hi0"), 1)
                ahead(base + BR0 + 3)
                for b in range(4):
                    act_e.wait_ge(S("mergedT"), 4 * l + b + 1)
                    nc.scalar.activation(hT_hi[:, 2 * b:2 * b + 2, :].rearrange("p c t -> p (c t)"), A[b][:],
                                         ACT.Copy).then_inc(S("gT_hi"), 1)
                ahead(base + OUT0 + 3)
                act_e.wait_ge(S("out_added"), 4 * (l + 1))
                squares(xs, xn)
                round_wide(hT_hi, G_XA + 32 * l, S("hT_hi"), S("xnT"), 12 * l + 4, 0)
                unit(13, base + XQ0, lambda tt: nc.scalar.activation(qn[:, tt, :], G[tt][:, 0:DB], ACT.Copy))
                square_root()
                act_e.wait_ge(S("xqT"), l + 1)
                nc.scalar.activation(qT[:].rearrange("p c t -> p (c t)"), T[0][:], ACT.Copy,
                                     scale=gqk[:, l:l + 1]).then_inc(S("xqT_out"), 1)
                for tt in range(TT):
                    act_e.wait_ge(S("xmax"), TT * l + tt + 1)
                    for i in range(NH):
                        j = tt * NH + i
                        nc.scalar.activation(prob[:, tt, i, :], A[2 * tt + i // 2][:, (i % 2) * SEQ:(i % 2) * SEQ + SEQ],
                                             ACT.Exp, bias=stat[:, 5, j:j + 1],
                                             accum_out=stat[:, 4, tt * NH + place(i):tt * NH + place(i) + 1]
                                             ).then_inc(S("xp"), 1)
                for tt in range(TT):
                    act_e.wait_ge(S("xpT"), TT * l + tt + 1)
                    for hp in range(2):
                        nc.scalar.activation(probT[:, tt, 2 * hp:2 * hp + 2, :].rearrange("p h m -> p (h m)"),
                                             A[2 * tt + hp][:], ACT.Copy).then_inc(S("xpT_out"), 1)
                act_e.wait_ge(S("xoT"), l + 1)
                nc.scalar.activation(oT_hi[:].rearrange("p c t -> p (c t)"), T[0][:], ACT.Copy).then_inc(S("oT_hi"), 1)
                ahead(base + XO0)
                act_e.wait_ge(S("xo_added"), 4 * (l + 1))
                squares(xs, xn)
                if l:
                    break
                round_wide(hT_hi, G_FFN + 32 * l, S("hT_hi"), S("xnT"), 12 * l + 8, 0)
                lap0 = FF_LAP[0]
                nxt[0] -= RING * lap0

                def ff_round(f):
                    act_e.wait_ge(S("ff_actT"), f + 1)
                    nc.scalar.activation(actT_hi[:].rearrange("p c t -> p (c t)"), T[0][:],
                                         ACT.Copy).then_inc(S("actT_hi"), 1)

                for f in range(NF):
                    if f:
                        ahead(3 * f, lap0)
                        ff_round(f - 1)
                    k = 3 * f + 1 + (f == 0)
                    ahead(k, lap0)
                    for tt in range(TT):
                        if tt == 0:
                            act_e.wait_ge(half, half_no(0, 16 + f) + 1)
                        else:
                            act_e.wait_ge(used, number(lap0, k) + 1)
                        if f:
                            act_e.wait_ge(S("ff_act"), 2 * f - 1 + tt)
                        nc.scalar.activation(silu[:, tt, :], G[tt][:, 0:FB], ACT.Silu).then_inc(S("ff_silu"), 1)
                ff_round(NF - 1)
                nxt[0] += RING * lap0

            for b in range(4):
                act_e.wait_ge(S("xnT"), 12 * (DEPTH - 1) + 8 + b + 1)
                nc.scalar.activation(hT_f32[:, 2 * b:2 * b + 2, :].rearrange("p c t -> p (c t)"), A[b][:],
                                     ACT.Copy).then_inc(S("rhT"), 1)
            act_e.wait_ge(S("gap"), 1)
            nc.scalar.activation(lg[:, 10, :, 0], lg[:, 10, :, 1], ACT.Exp).then_inc(S("gap_exp"), 1)
            lap0 = FF_LAP[1]
            nxt[0] -= RING * lap0
            split_to(1 + RING, lap0)
            act_e.wait_ge(S("items"), 1)
            items = act_e.snap(NE + act_e.value_load(nit[0:1, 0:1], min_val=0, max_val=NE))

            def round_gathered(i, after=None):
                act_e.wait_ge(S("gathered"), i + 1)
                for j in range(2):
                    nc.scalar.activation(eT_hi[:, 4 * j:4 * j + 4, :].rearrange("p k s -> p (k s)"), A[2 + j][:],
                                         ACT.Copy).then_inc(S("eT_hi"), 1)

            def e_round(step):
                act_e.wait_ge(S("e_actT"), step + 1)
                nc.scalar.activation(actT_hi[:, :, 0:P], T[0][:, 0:2 * P].rearrange("p (c t) -> p c t", c=2),
                                     ACT.Copy).then_inc(S("e_aT_hi"), 1)

            def item(i, first=False, last=False):
                lap0 = FF_LAP[1] + NF * i
                for f in range(NF):
                    step = NF * i + f
                    if not (first and f == 0):
                        ahead(3 * f, lap0)
                        e_round(step - 1)
                    k = 3 * f + 1 + (first and f == 0)
                    ahead(k, lap0)
                    act_e.wait_ge(used, number(lap0, k) + 1)
                    if not (first and f == 0):
                        act_e.wait_ge(S("e_act"), step)
                    nc.scalar.activation(silu[:, 0, :], (G[0], G[1], T[1])[f % 3][:, 0:FB],
                                         ACT.Silu).then_inc(S("e_silu"), 1)
                    if f == 0 and not first:
                        ahead(2, lap0)
                        act_e.wait_ge(used, number(lap0, 2) + 1)
                        for nb in range(2):
                            nc.scalar.activation(ye[:, nb * 512:nb * 512 + 512], A[nb][:], ACT.Copy).then_inc(S("ye"), 1)
                    if f == 4:
                        act_e.wait_ge(S("selT"), i + 1)
                        nc.scalar.activation(selwT[:], T[0][:, 2 * P:4 * P], ACT.Copy).then_inc(S("selT_out"), 1)
                if not last:
                    round_gathered(i + 1)

            round_gathered(0)
            item(0, first=True)
            nxt[0] = 1
            with act_e.Fori(1, items - 1) as i:
                item(i)
            assert nxt[0] == 1 + RING * NF
            nxt[0] = 1
            last = act_e.snap(items - 1)
            item(last, last=True)
            e_round(last * NF + NF - 1)
            act_e.wait_ge(used, RING * FF_LAP[1] + RING * NF * items + 1)
            for nb in range(2):
                nc.scalar.activation(ye[:, nb * 512:nb * 512 + 512], A[nb][:], ACT.Copy).then_inc(S("ye"), 1)

        @block.vector
        def _(dve):
            v = nc.vector
            steps = [0]

            def link(ins):
                steps[0] += 1
                ins.then_inc(dve_step, 1)
                dve.wait_ge(dve_step, steps[0])

            nxt = [0]

            def split_to(k_end, lap0=0):
                while nxt[0] < k_end:
                    k = nxt[0]
                    dve.wait_ge(hi_ready, number(lap0, k) + 1)
                    v.tensor_tensor(w_lo[slot(k)][:], raw[slot(k)][:], w_hi[slot(k)][:].bitcast(F32),
                                    ALU.subtract).then_inc(lo_ready, 1)
                    nxt[0] += 1

            def ahead(k, lap0=0):
                split_to(k + RING, lap0)

            def power(dst, src, scale, eps=EPS):
                w = dst.shape[1]
                v.tensor_scalar(root[:, 0, 0:w], src, scale, eps, ALU.mult, ALU.add).then_inc(S("mean_square"), 1)
                roots[0] += 1
                dve.wait_ge(S("rooted"), roots[0])
                link(v.reciprocal(dst, root[:, 1, 0:w]))

            norms = [0]
            roots = [0]
            v.memset(eps_col[:], EPS).then_inc(S("eps_set"), 1)
            v.memset(half_pi[:], float(np.float32(np.pi / 2))).then_inc(S("eps_set"), 1)
            v.memset(one_col[:], 1.0).then_inc(S("eps_set"), 1)
            link(v.memset(root[:], 1.0))

            def normalize(src, dst, done, gain_row=None):
                for tt in range(TT):
                    norms[0] += 1
                    dve.wait_ge(S("squared"), norms[0])
                    link(v.reciprocal(stat[:, 2, tt:tt + 1], ss[:, 1, tt:tt + 1]))
                    ins = v.tensor_scalar(dst[:, tt, :], src[:, tt, :], stat[:, 2, tt:tt + 1], None, ALU.mult)
                    if gain_row is not None:
                        link(ins)
                        ins = v.tensor_tensor(dst[:, tt, :], dst[:, tt, :], gain_row, ALU.mult)
                    ins.then_inc(done, 1)

            def rest_wide(dst, hi, gain, ready, count, done):
                for b in range(4):
                    dve.wait_ge(ready, count + b + 1)
                    for kt in (2 * b, 2 * b + 1):
                        bank = A[b][:, (kt % 2) * SEQ:(kt % 2) * SEQ + SEQ]
                        ins = v.scalar_tensor_tensor(out=dst[:, kt, :], in0=bank, scalar=gcol[:, gain + kt:gain + kt + 1],
                                                     in1=hi[:, kt, :].bitcast(F32), op0=ALU.mult, op1=ALU.subtract)
                    ins.then_inc(done, 1)

            def flat(t):
                return t.rearrange("p c t -> p (c t)")

            def head_scale(src, square, row):
                link(v.tensor_tensor(square, src, src, ALU.mult))
                link(v.tensor_reduce(stat[:, row, :], square.rearrange("p (g d) -> p g d", d=HD), AX.X, ALU.add))
                power(stat[:, row + 1, :], stat[:, row, :], 1.0 / HD)

            def per_head(t, row):
                return stat[:, row, :].unsqueeze(2).to_broadcast([P, TT * NH, HD])

            heads = "p (g d) -> p g d"
            v.memset(vT[:, :, 0:CONV_W - 1], 0.0)
            normalize(memn, memn, S("mem_normed"))
            dve.wait_ge(S("cols_out"), 1)
            for l in range(DEPTH):
                ins = v.scalar_tensor_tensor(out=gqk[:, l:l + 1], in0=gcol[:, G_QG + l:G_QG + l + 1], scalar=HD ** -0.5,
                                             in1=gcol[:, G_KG + l:G_KG + l + 1], op0=ALU.mult, op1=ALU.mult)
            ins.then_inc(S("gqk"), 1)
            rest_wide(mT_lo, mT_hi, G_MEM, S("mT_hi"), 0, S("mT_lo"))
            for l in range(DEPTH):
                n = CH_KV + 2 * l + 1
                ahead(n - 1)
                dve.wait_ge(S("emptied"), 2 * (l + 1))
                if l:
                    dve.wait_ge(S("memkT"), l)
                k_nat = convn[:].rearrange("p t c -> p (t c)")
                head_scale(k_nat, tmp[:, 1].rearrange("p t c -> p (t c)"), 0)
                v.tensor_tensor(tmp[:, 0].rearrange("p t (h d) -> p (t h) d", d=HD), k_nat.rearrange(heads, d=HD),
                                per_head(None, 1), ALU.mult).then_inc(S("mk_normed"), 1)
                if l + 1 < DEPTH:
                    rest_wide(mT_lo, mT_hi, G_MEM + 32 * (l + 1), S("mT_hi"), 4 * (l + 1), S("mT_lo"))
            dve.wait_ge(S("memkT"), DEPTH)
            dve.wait_ge(S("pos_in"), 16)
            dve.wait_ge(S("cst2_in"), 16)
            link(v.tensor_copy(stat[:, 6, 0:TT], posi[:]))
            ang = tmp[:, 1].rearrange("p t c -> p (t c)")
            r, n2, a0 = ang[:, 0:64], ang[:, 128:192], ang[:, 192:256]
            for tt in range(TT):
                link(v.tensor_scalar(a0[:, tt * 32:tt * 32 + 32], cst[:, C_FREQ:C_FREQ + 32], stat[:, 6, tt:tt + 1], None,
                                     ALU.mult))
            link(v.tensor_scalar(n2, a0, 1.0 / (2 * np.pi), ROUND, ALU.mult, ALU.add))
            link(v.tensor_scalar(n2, n2, -ROUND, None, ALU.add))
            link(v.scalar_tensor_tensor(out=r, in0=n2, scalar=-TWO_PI_1, in1=a0, op0=ALU.mult, op1=ALU.add))
            link(v.scalar_tensor_tensor(out=r, in0=n2, scalar=-TWO_PI_2, in1=r, op0=ALU.mult, op1=ALU.add))
            link(v.scalar_tensor_tensor(out=r, in0=n2, scalar=-TWO_PI_3, in1=r, op0=ALU.mult, op1=ALU.add))
            v.tensor_scalar(r, r, 3.1415925, -3.1415925, ALU.min, ALU.max).then_inc(S("angles"), 1)

            for l in range(DEPTH):
                base = LAYER0[l]
                normalize(xs, xn, S("normed"))
                rest_wide(hT_lo, hT_hi, G_MIX + 32 * l, S("hT_hi"), 12 * l, S("hT_lo"))
                ahead(base + 5)
                dve.wait_ge(S("emptied"), 2 * unit_no(l, 2) + 2)
                v.tensor_tensor(convn[:], U[0][:, :, 0:DB], U[0][:, :, DB:], ALU.mult).then_inc(S("conv_v"), 1)
                ahead(base + 7)
                dve.wait_ge(S("sb_z"), l + 1)
                m2 = mask.unsqueeze(1).to_broadcast([P, 2, SEQ])
                m4 = mask.unsqueeze(1).to_broadcast([P, NH, SEQ])
                m4s = mask[:, 0:P].unsqueeze(1).to_broadcast([P, NH, P])

                def near(t):
                    return t[:, 0:NH * SEQ].rearrange("p (h q) -> p h q", h=NH)

                def far(t):
                    return t[:, NH * SEQ:].rearrange("p (h q) -> p h q", h=NH)

                for j in range(2):
                    v.tensor_tensor(near(zm)[:, 2 * j:2 * j + 2], A[1 + j][:].rearrange("p (h q) -> p h q", h=2), m2, ALU.mult)
                v.tensor_tensor(far(zm), A[3][:].rearrange("p (h q) -> p h q", h=NH), m4s, ALU.mult).then_inc(S("sb_zm"), 1)
                dve.wait_ge(S("yT_hi1"), l + 1)
                for c in range(KB):
                    ins = v.scalar_tensor_tensor(out=yT[1][1][:, c, :], in0=T[0][:, c * SEQ:c * SEQ + SEQ],
                                                 scalar=gcol[:, G_PS + 2 * l + c:G_PS + 2 * l + c + 1],
                                                 in1=yT[1][0][:, c, :].bitcast(F32), op0=ALU.mult, op1=ALU.subtract)
                ins.then_inc(S("yT_lo1"), 1)
                dve.wait_ge(S("emptied"), 2 * unit_no(l, 3) + 2)
                if l == 0:
                    dve.wait_ge(S("trig"), 1)
                for tt in range(TT):
                    qk = U[3][:, tt, :].rearrange("p (h two d) -> p h two d", two=2, d=HD // 2)
                    x1, x2 = qk[:, :, 0, :], qk[:, :, 1, :]
                    cos = trig[:, 0, tt, :].unsqueeze(1).to_broadcast([P, 2 * NH, HD // 2])
                    sin = trig[:, 1, tt, :].unsqueeze(1).to_broadcast([P, 2 * NH, HD // 2])
                    t1 = tmp[:, 0, tt, :].rearrange("p (h d) -> p h d", d=HD // 2)
                    t2 = tmp[:, 1, tt, :].rearrange("p (h d) -> p h d", d=HD // 2)
                    v.tensor_tensor(t1, x1, sin, ALU.mult)
                    link(v.tensor_tensor(t2, x2, sin, ALU.mult))
                    v.tensor_tensor(x1, x1, cos, ALU.mult)
                    link(v.tensor_tensor(x2, x2, cos, ALU.mult))
                    v.tensor_tensor(x1, x1, t2, ALU.subtract)
                    ins = v.tensor_tensor(x2, x2, t1, ALU.add)
                ins.then_inc(S("rotated"), 1)
                ahead(base + 9)
                dve.wait_ge(S("sb_l"), l + 1)
                link(v.scalar_tensor_tensor(out=zs, in0=zm, scalar=0.0, in1=zs, op0=ALU.max, op1=ALU.add))
                v.tensor_tensor(near(zs), near(zs), m4, ALU.mult)
                v.tensor_tensor(far(zs), far(zs), m4s, ALU.mult).then_inc(S("sb_sp"), 1)

                dve.wait_ge(S("vT_out"), l + 1)
                taps = [0]

                def conv_taps(count):
                    for w in range(taps[0], min(taps[0] + count, CONV_W)):
                        for c in range(KB):
                            tap = cwcol[:, (l * CONV_W + w) * KB + c:(l * CONV_W + w) * KB + c + 1]
                            src = vT[:, c, w:w + SEQ]
                            if w == 0:
                                bias = gcol[:, G_CB + 2 * l + c:G_CB + 2 * l + c + 1]
                                ins = v.tensor_scalar(conv[:, c, :], src, tap, bias, ALU.mult, ALU.add)
                            else:
                                dve.wait_ge(S("tap"), KB * CONV_W * l + KB * (w - 1) + c + 1)
                                ins = v.scalar_tensor_tensor(out=conv[:, c, :], in0=src, scalar=tap, in1=conv[:, c, :],
                                                             op0=ALU.mult, op1=ALU.add)
                            ins.then_inc(S("tap"), 1)
                    taps[0] = min(taps[0] + count, CONV_W)

                ahead(base + GATE0 + 0)
                conv_taps(5)
                ahead(base + GATE0 + 1)
                dve.wait_ge(S("sb_tail"), l + 1)
                for j in range(3):
                    ins = v.tensor_tensor(zm[:, 512 * j:512 * j + 512], zm[:, 512 * j:512 * j + 512], A[1 + j][:], ALU.subtract)
                ins.then_inc(S("sb_w"), 1)
                conv_taps(3)
                ahead(base + GATE0 + 2)
                conv_taps(4)
                ahead(base + GATE0 + 3)
                dve.wait_ge(S("sb_exp"), l + 1)
                v.tensor_tensor(near(zm), near(zm), m4, ALU.mult)
                v.tensor_tensor(far(zm), far(zm), m4s, ALU.mult).then_inc(S("sb_a"), 1)
                for g in range(4, 7):
                    conv_taps(4)
                    ahead(base + GATE0 + g)
                ahead(base + GATE0 + 7)
                dve.wait_ge(S("ret_z"), l + 1)
                for j in range(2):
                    v.tensor_tensor(near(zs)[:, 2 * j:2 * j + 2], A[1 + j][:].rearrange("p (h q) -> p h q", h=2),
                                    decay[:, 2 * j:2 * j + 2, :], ALU.mult)
                v.tensor_tensor(far(zs), A[3][:].rearrange("p (h q) -> p h q", h=NH), decay[:, :, 0:P],
                                ALU.mult).then_inc(S("ret_a"), 1)
                dve.wait_ge(S("yT_hi2"), l + 1)
                v.tensor_tensor(flat(yT[2][1][:]), A[0][:], flat(yT[2][0][:]).bitcast(F32),
                                ALU.subtract).then_inc(S("yT_lo2"), 1)
                ahead(base + GATE0 + 8)
                conv_taps(4)
                ahead(base + GATE0 + 9)
                conv_taps(CONV_W)

                def centre(bank, groups, width, dst, square, row):
                    src = bank[:].rearrange("p (g d) -> p g d", d=width)
                    to = dst.rearrange("p (g d) -> p g d", d=width)
                    link(v.tensor_reduce(stat[:, row, 0:groups], src, AX.X, ALU.add))
                    link(v.tensor_scalar(stat[:, row, 0:groups], stat[:, row, 0:groups], 1.0 / width, None, ALU.mult))
                    mean = stat[:, row, 0:groups].unsqueeze(2).to_broadcast([P, groups, width])
                    link(v.tensor_tensor(to, src, mean, ALU.subtract))
                    link(v.tensor_tensor(square, dst, dst, ALU.mult))
                    link(v.tensor_reduce(stat[:, row, 0:groups], square.rearrange("p (g d) -> p g d", d=width), AX.X,
                                         ALU.add))
                    power(stat[:, row + 1, 0:groups], stat[:, row, 0:groups], 1.0 / width)
                    return stat[:, row + 1, 0:groups].unsqueeze(2).to_broadcast([P, groups, width])

                ahead(base + GATE0 + 11)
                dve.wait_ge(S("ret_o"), l + 1)
                y, sq = (tmp[:, j].rearrange("p t c -> p (t c)") for j in range(2))
                inv = centre(T[1], TT * NH, HD, y, sq, 0)
                link(v.tensor_tensor(y.rearrange(heads, d=HD), y.rearrange(heads, d=HD), inv, ALU.mult))
                v.tensor_tensor(tmp[:, 0], tmp[:, 0], U[4][:, :, DB:], ALU.mult).then_inc(S("ret_y"), 1)
                ahead(base + GATE0 + 13)
                dve.wait_ge(S("conv_nat"), l + 1)
                cn = convn[:].rearrange("p t c -> p (t c)")
                inv = centre(T[0], TT, DB, cn, flat(dT[:]), 0)
                v.tensor_tensor(cn.rearrange("p (g d) -> p g d", d=DB), cn.rearrange("p (g d) -> p g d", d=DB), inv,
                                ALU.mult).then_inc(S("conv_ln"), 1)
                ahead(base + GATE0 + 15)
                dve.wait_ge(S("yT_hi3"), l + 1)
                v.tensor_tensor(flat(yT[3][1][:]), A[1][:], flat(yT[3][0][:]).bitcast(F32),
                                ALU.subtract).then_inc(S("yT_lo3"), 1)
                for i, b in enumerate(BR_ORDER):
                    n = base + BR0 + i
                    if i == 1:
                        dve.wait_ge(S("yT_hi0"), l + 1)
                        v.tensor_tensor(flat(yT[0][1][:]), flat(conv[:]), flat(yT[0][0][:]).bitcast(F32),
                                        ALU.subtract).then_inc(S("yT_lo0"), 1)
                    ahead(n)
                    for nb in range(2):
                        for tt in range(TT):
                            j = 2 * nb + tt
                            if j < 3:
                                dve.wait_ge(S("branch"), 3 * (4 * l + i) + j + 1)
                            else:
                                dve.wait_ge(used, n + 1)
                            sl = slice(nb * 512, nb * 512 + 512)
                            dst = merged if i == 0 else gates[:, b]
                            v.tensor_tensor(dst[:, tt, sl], gates[:, b, tt, sl], (G, T)[nb][tt][:],
                                            ALU.mult).then_inc(S("prod"), 1)
                for b in range(4):
                    dve.wait_ge(S("gT_hi"), 4 * l + b + 1)
                    v.tensor_tensor(flat(hT_lo[:, 2 * b:2 * b + 2, :]), A[b][:],
                                    flat(hT_hi[:, 2 * b:2 * b + 2, :]).bitcast(F32), ALU.subtract).then_inc(S("gT_lo"), 1)
                for nb in range(2):
                    n = base + OUT0 + 2 * nb + 1
                    ahead(n)
                    for tt in range(TT):
                        if tt == 0:
                            dve.wait_ge(half, half_no(l, 13 + nb) + 1)
                        else:
                            dve.wait_ge(used, n + 1)
                        sl = slice(nb * 512, nb * 512 + 512)
                        v.tensor_tensor(xs[:, tt, sl], xs[:, tt, sl], G[tt][:], ALU.add).then_inc(S("out_added"), 1)
                dve.wait_ge(S("out_added"), 4 * (l + 1))
                normalize(xs, xn, S("normed"))
                rest_wide(hT_lo, hT_hi, G_XA + 32 * l, S("hT_hi"), 12 * l + 4, S("hT_lo"))
                ahead(base + XQ0)
                dve.wait_ge(S("emptied"), 2 * unit_no(l, 13) + 2)
                q_nat = qn[:].rearrange("p t c -> p (t c)")
                head_scale(q_nat, tmp[:, 0].rearrange("p t c -> p (t c)"), 0)
                v.tensor_tensor(q_nat.rearrange(heads, d=HD), q_nat.rearrange(heads, d=HD), per_head(None, 1),
                                ALU.mult).then_inc(S("q_normed"), 1)
                for tt in range(TT):
                    dve.wait_ge(S("x_scores"), TT * l + tt + 1)
                    for hp in range(2):
                        j = tt * NH + 2 * hp
                        link(v.tensor_reduce(stat[:, 3, j:j + 2], A[2 * tt + hp][:].rearrange("p (h m) -> p h m", h=2), AX.X,
                                             ALU.max))
                    v.tensor_scalar(stat[:, 5, tt * NH:tt * NH + NH], stat[:, 3, tt * NH:tt * NH + NH], -1.0, None,
                                    ALU.mult).then_inc(S("xmax"), 1)
                dve.wait_ge(S("xp"), 8 * (l + 1))
                link(v.reciprocal(stat[:, 6, :], stat[:, 4, :]))
                dve.wait_ge(S("xo"), l + 1)
                v.tensor_tensor(on[:].rearrange("p t (h d) -> p (t h) d", d=HD), T[1][:].rearrange(heads, d=HD),
                                per_head(None, 6), ALU.mult).then_inc(S("xo_normed"), 1)
                dve.wait_ge(S("oT_hi"), l + 1)
                v.tensor_tensor(flat(oT_lo[:]), T[0][:], flat(oT_hi[:]).bitcast(F32), ALU.subtract).then_inc(S("oT_lo"), 1)
                ahead(base + XO0)
                for nb in range(2):
                    for tt in range(TT):
                        j = 2 * nb + tt
                        if j < 3:
                            dve.wait_ge(S("xproj"), 3 * l + j + 1)
                        else:
                            dve.wait_ge(used, base + XO0 + 1)
                        sl = slice(nb * 512, nb * 512 + 512)
                        v.tensor_tensor(xs[:, tt, sl], xs[:, tt, sl], (G, T)[nb][tt][:], ALU.add).then_inc(S("xo_added"), 1)
                dve.wait_ge(S("xo_added"), 4 * (l + 1))
                if l:
                    dve.wait_ge(S("rt_in"), 32)
                    normalize(xs, xn, S("normed"), merged[:, 0, :])
                    break
                normalize(xs, xn, S("normed"))
                rest_wide(hT_lo, hT_hi, G_FFN + 32 * l, S("hT_hi"), 12 * l + 8, S("hT_lo"))
                lap0 = FF_LAP[0]
                nxt[0] -= RING * lap0

                def ff_rest(f):
                    dve.wait_ge(S("actT_hi"), f + 1)
                    v.tensor_tensor(flat(actT_lo[:]), T[0][:], flat(actT_hi[:]).bitcast(F32),
                                    ALU.subtract).then_inc(S("actT_lo"), 1)

                for f in range(NF):
                    if f:
                        ahead(3 * f, lap0)
                        ff_rest(f - 1)
                    ahead(3 * f + 1 + (f == 0), lap0)
                    for tt in range(TT):
                        dve.wait_ge(S("ff_silu"), 2 * f + tt + 1)
                        if f:
                            dve.wait_ge(S("ff_actT"), f)
                        v.tensor_tensor(act[:, tt, :], silu[:, tt, :], G[tt][:, FB:], ALU.mult).then_inc(S("ff_act"), 1)
                ff_rest(NF - 1)
                dve.wait_ge(used, number(lap0, 3 * NF) + 1)
                for nb in range(2):
                    for tt in range(TT):
                        sl = slice(nb * 512, nb * 512 + 512)
                        v.tensor_tensor(xs[:, tt, sl], xs[:, tt, sl], A[2 * tt + nb][:], ALU.add).then_inc(S("ffn_added"), 1)
                nxt[0] += RING * lap0

            dve.wait_ge(S("logits"), 1)
            link(v.tensor_copy(lg[:, 0].rearrange("p t e -> p (t e)"), T[0][:, 0:TT * NE]))
            e8 = cst[:, C_E8:C_E8 + NE].unsqueeze(1).to_broadcast([P, TT, NE])

            def wide(t):
                return t.unsqueeze(2).to_broadcast([P, TT, NE])

            def first_of_max(src, top, onehot, scratch):
                link(v.tensor_reduce(lg[:, top, :, 0], src, AX.X, ALU.max))
                link(v.tensor_tensor(lg[:, scratch], src, wide(lg[:, top, :, 0]), ALU.is_equal))
                link(v.tensor_tensor(lg[:, scratch], lg[:, scratch], e8, ALU.mult))
                link(v.tensor_reduce(lg[:, 11, :, 0], lg[:, scratch], AX.X, ALU.max))
                link(v.tensor_tensor(lg[:, onehot], lg[:, scratch], wide(lg[:, 11, :, 0]), ALU.is_equal))

            first_of_max(lg[:, 0], 1, 2, 3)
            link(v.scalar_tensor_tensor(out=lg[:, 4], in0=lg[:, 2], scalar=NEG, in1=lg[:, 0], op0=ALU.mult, op1=ALU.add))
            first_of_max(lg[:, 4], 5, 7, 3)
            v.tensor_tensor(lg[:, 10, :, 1], lg[:, 5, :, 0], lg[:, 1, :, 0], ALU.subtract).then_inc(S("gap"), 1)
            v.tensor_tensor(lg[:, 6], lg[:, 2], lg[:, 7], ALU.add).then_inc(S("picked"), 1)
            dve.wait_ge(S("gap_exp"), 1)
            link(v.tensor_scalar(lg[:, 8, :, 0], lg[:, 10, :, 0], 1.0, None, ALU.add))
            link(v.reciprocal(lg[:, 8, :, 1], lg[:, 8, :, 0]))
            link(v.tensor_tensor(lg[:, 8, :, 2], lg[:, 8, :, 1], lg[:, 10, :, 0], ALU.mult))
            link(v.tensor_tensor(lg[:, 2], lg[:, 2], wide(lg[:, 8, :, 1]), ALU.mult))
            link(v.tensor_tensor(lg[:, 7], lg[:, 7], wide(lg[:, 8, :, 2]), ALU.mult))
            for j in range(2):
                link(v.tensor_tensor(comb[:, :, j * NE:j * NE + NE], lg[:, 2], lg[:, 7], ALU.add))
            dve.wait_ge(S("counted"), 1)
            link(v.tensor_scalar(lg[:, 8].rearrange("p t e -> p (t e)"), T[1][:, 0:TT * NE], 1.0, None, ALU.add))
            link(v.tensor_tensor(lg[:, 8], lg[:, 8], lg[:, 6], ALU.mult))
            link(v.tensor_scalar(posm[:, :, 0:NE], lg[:, 8], -1.0, None, ALU.add))
            link(v.tensor_scalar(posm[:, :, NE:2 * NE], lg[:, 8], -1.0 - P, None, ALU.add))
            link(v.tensor_reduce(nitf[:, 0:1], T[1][:, 2 * NE:3 * NE], AX.X, ALU.max))
            link(v.tensor_scalar(nitf[:, 0:1], nitf[:, 0:1], float(P) + 0.5, float(NE), ALU.is_gt, ALU.mult))
            v.tensor_copy(nit[:, 0:1], nitf[:, 0:1]).then_inc(S("items"), 1)
            dve.wait_ge(S("items"), 1)
            items = dve.snap(NE + dve.value_load(nit[0:1, 0:1], min_val=0, max_val=NE))
            iota = cst[:, C_IOTA:C_IOTA + P]

            def select(i):
                one = bass.ds(i, 1)
                for tt in range(TT):
                    v.tensor_scalar(selw[:, tt, :], iota, posm[:, tt, one], comb[:, tt, one], ALU.is_equal, ALU.mult)
                for tt in range(TT):
                    ins = v.tensor_scalar(sel[:, tt, :], iota, posm[:, tt, one], None, ALU.is_equal)
                ins.then_inc(S("sel"), 1)

            def rest_gathered(i):
                for j in range(2):
                    dve.wait_ge(S("eT_hi"), 2 * i + j + 1)
                    part = slice(4 * j, 4 * j + 4)
                    v.tensor_tensor(eT_lo[:, part, :].rearrange("p k s -> p (k s)"), A[2 + j][:],
                                    eT_hi[:, part, :].rearrange("p k s -> p (k s)").bitcast(F32),
                                    ALU.subtract).then_inc(S("eT_lo"), 1)

            def e_rest(step):
                dve.wait_ge(S("e_aT_hi"), step + 1)
                v.tensor_tensor(actT_lo[:, :, 0:P], T[0][:, 0:2 * P].rearrange("p (c t) -> p c t", c=2),
                                actT_hi[:, :, 0:P].bitcast(F32), ALU.subtract).then_inc(S("e_aT_lo"), 1)

            def add_scattered(i, tt):
                dve.wait_ge(S("scat"), 2 * i + tt + 1)
                for nb in range(2):
                    sl = slice(nb * 512, nb * 512 + 512)
                    v.tensor_tensor(xs[:, tt, sl], xs[:, tt, sl], A[2 + nb][:], ALU.add).then_inc(S("scattered"), 1)

            def item(i, first=False, last=False):
                lap0 = FF_LAP[1] + NF * i
                for f in range(NF):
                    step = NF * i + f
                    if not (first and f == 0):
                        ahead(3 * f, lap0)
                        e_rest(step - 1)
                    ahead(3 * f + 1 + (first and f == 0), lap0)
                    dve.wait_ge(S("e_silu"), step + 1)
                    if not (first and f == 0):
                        dve.wait_ge(S("e_actT"), step)
                    v.tensor_tensor(act[:, 0, :], silu[:, 0, :], (G[0], G[1], T[1])[f % 3][:, FB:],
                                    ALU.mult).then_inc(S("e_act"), 1)
                    if f in (2, 3) and not first:
                        add_scattered(i - 1, f - 2)
                    if f == 5 and not last:
                        dve.wait_ge(S("gathered"), i + 1)
                        dve.wait_ge(S("selT"), i + 1)
                        select(i + 1)
                if not last:
                    rest_gathered(i + 1)

            select(0)
            nxt[0] -= RING * FF_LAP[1]
            rest_gathered(0)
            item(0, first=True)
            nxt[0] = 1
            with dve.Fori(1, items - 1) as i:
                item(i)
            assert nxt[0] == 1 + RING * NF
            nxt[0] = 1
            last = dve.snap(items - 1)
            item(last, last=True)
            e_rest(last * NF + NF - 1)
            for tt in range(TT):
                add_scattered(last, tt)


_INS = ["x", "mem", "positions", "norm_mix_g", "w_in", "conv_w", "conv_b", "conv_ln_g", "conv_ln_b", "pool_w",
        "pool_scale", "w_gate", "w_branch", "w_out", "norm_xa_g", "norm_mem_g", "xa_wq", "xa_wkv", "xa_q_norm_g",
        "xa_k_norm_g", "xa_wo", "norm_ffn_g", "ffn_w_gu", "ffn_w_down", "moe_router", "moe_w_gu", "moe_w_down"]


def kernel(**inputs):
    import concourse.bacc as bacc
    from concourse.bass_utils import run_bass_kernel_spmd

    nc = bacc.Bacc("TRN2", target_bir_lowering=False, num_devices=1)
    arrays = {"shape_constants": shape_constants()}
    arrays.update({name: np.ascontiguousarray(inputs[name]) for name in _INS})
    args = [nc.dram_tensor(f"in_{name}", a.shape, mybir.dt.from_np(a.dtype), kind="ExternalInput").ap()
            for name, a in arrays.items()]
    out = nc.dram_tensor("out_0", inputs["x"].shape, F32, kind="ExternalOutput").ap()
    trunk(nc, *args, out)
    r = run_bass_kernel_spmd(nc, [{f"in_{name}": a for name, a in arrays.items()}], core_ids=[0])
    return r.results[0]["out_0"]
```

```python
from contextlib import ExitStack

import numpy as np

import concourse.bass as bass
from concourse import mybir

F32 = mybir.dt.float32
F32R = mybir.dt.float32r
I32 = mybir.dt.int32
ALU = mybir.AluOpType
ACT = mybir.ActivationFunctionType
AX = mybir.AxisListType

P = 128
D = 1024
SEQ = 256
TT = SEQ // P
KT = D // P
DEPTH = 2
DB = D // 4
KB = DB // P
NH, HD = 4, 64
D_IN = 10 * DB
CONV_W = 31
WINDOWS = (2, 4, 8, 16)
D_FF = 2816
FB = 256
NF = D_FF // FB
NE = 8
EPS = 1e-6
CH = 1024
RING = 6
LEAD = 4
NEG = -3.0e38

IN0, GATE0, BR0, OUT0, XK0, XQ0, XV0, XO0, PER_LAYER = 0, 20, 52, 60, 68, 70, 72, 74, 76
FFS = 6
LAYER0 = [0, PER_LAYER + FFS * NF]
FF0 = [LAYER0[0] + PER_LAYER, LAYER0[1] + PER_LAYER]
FF_N0 = FF0[0] - 2
FF_LAP = FF0[1] // RING
assert RING == FFS and FF0[1] % RING == 2
IN_ORDER = (1, 2, 0, 3, 4)
BR_ORDER = (2, 1, 3, 0)

C_ID, C_TRIGE, C_TRILT, C_ONES, C_MASK = 0, 128, 256, 384, 512
C_DECAY = C_MASK + 256
C_BAND = C_DECAY + NH * 256
C_FREQ = C_BAND + 4 * 384
C_E8 = C_FREQ + 32
C_IOTA = C_E8 + 8
C_ALL = C_IOTA + 128


def shape_constants():
    c = np.zeros((P, C_ALL), np.float64)
    k, q = np.arange(P)[:, None], np.arange(P)[None, :]
    q2 = np.arange(SEQ)[None, :]
    c[:, C_ID:C_ID + P] = k == q
    c[:, C_TRIGE:C_TRIGE + P] = k >= q
    c[:, C_TRILT:C_TRILT + P] = k < q
    c[:, C_ONES:C_ONES + P] = 1
    c[:, C_MASK:C_MASK + SEQ] = k < q2
    for j, h in enumerate((0, 2, 1, 3)):
        gamma = np.float64(np.float32(1.0 - 2.0 ** (-5.0 - h)))
        c[:, C_DECAY + j * SEQ:C_DECAY + (j + 1) * SEQ] = np.where(
            q2 >= k, gamma ** np.maximum(q2 - k, 0), 0.0) * HD ** -0.5
    for g, w in enumerate(WINDOWS):
        band = np.where((q2 >= k) & (q2 - k < w), 1.0 / np.minimum(q2 + 1.0, w), 0.0) - (q2 == k)
        late = np.where((q >= k) & (q - k < w), 1.0 / w, 0.0) - (q == k)
        c[:, C_BAND + g * 384:C_BAND + g * 384 + 256] = band
        c[:, C_BAND + g * 384 + 256:C_BAND + (g + 1) * 384] = late
    c[:, C_FREQ:C_FREQ + 32] = 10000.0 ** (-np.arange(32) / 32)
    c[:, C_E8:C_E8 + 8] = 8 - np.arange(8)
    c[:, C_IOTA:C_IOTA + P] = q
    return c.astype(np.float32)


G_XA, G_FFN, G_MEM = 0, 16, 32
G_CB, G_LG, G_LB, G_PS = 48, 52, 56, 60
G_QG, G_KG = 64, 66
G_ROWS = 68

TWO_PI_1 = 6.28125
TWO_PI_2 = float(np.float32(np.round((2 * np.pi - TWO_PI_1) * 2 ** 20) / 2 ** 20))
TWO_PI_3 = float(np.float32(2 * np.pi - TWO_PI_1 - TWO_PI_2))
ROUND = 12582912.0


def trunk(nc, consts, x, mem, positions, norm_mix_g, w_in, conv_w, conv_b, conv_ln_g, conv_ln_b, pool_w,
          pool_scale, w_gate, w_branch, w_out, norm_xa_g, norm_mem_g, xa_wq, xa_wkv, xa_q_norm_g,
          xa_k_norm_g, xa_wo, norm_ffn_g, ffn_w_gu, ffn_w_down, moe_router, moe_w_gu, moe_w_down, out):
    ctx = ExitStack()
    with ctx:
        def sb(name, shape, dt=F32, stack=ctx):
            return stack.enter_context(nc.sbuf_tensor(name, shape, dt))

        def sem(name):
            return ctx.enter_context(nc.semaphore(name))

        raw = [sb(f"raw{j}", [P, CH]) for j in range(RING)]
        w_hi = [sb(f"w_hi{j}", [P, CH], F32R) for j in range(RING)]
        w_lo = [sb(f"w_lo{j}", [P, CH], F32R) for j in range(RING)]
        cst = sb("cst", [P, C_ALL])
        xs = sb("xs", [P, TT, D])
        xn = sb("xn", [P, TT, D])
        merged = sb("merged", [P, TT, D])
        with ExitStack() as s:
            hT_f32 = sb("hT_f32", [P, KT, SEQ], F32, s)
        hT_hi = sb("hT_hi", [P, KT, SEQ], F32R)
        hT_lo = sb("hT_lo", [P, KT, SEQ], F32R)
        memk = sb("memk", [P, KB, SEQ])
        memv = sb("memv", [P, TT, DB])
        qT = sb("qT", [P, KB, SEQ])
        kT = sb("kT", [P, KB, SEQ])
        dT = sb("dT", [P, KB, SEQ])
        vT = sb("vT", [P, KB, CONV_W - 1 + SEQ])
        conv = sb("conv", [P, KB, SEQ])
        convn = sb("convn", [P, TT, DB])
        tmp = sb("tmp", [P, 2, TT, DB])
        gmix = sb("gmix", [P, DEPTH * KT])
        gcol = sb("gcol", [P, G_ROWS])
        gqk = sb("gqk", [P, DEPTH])
        cwcol = sb("cwcol", [P, 2 * CONV_W * DEPTH])
        poolw = sb("poolw", [P, DEPTH, 2, 64])
        stat = sb("stat", [P, 8, 8])
        eps_col = sb("eps_col", [P, 1])
        half_pi = sb("half_pi", [P, 1])
        one_col = sb("one_col", [P, 1])
        root = sb("root", [P, 2, 8])
        ssq = sb("ssq", [P, 4 * DEPTH, TT])
        srt = sb("srt", [P, 4 * DEPTH, TT])
        rs = sb("rs", [P, 4 * DEPTH, TT])
        rt = sb("rt", [P, KT, NE])
        posi = sb("posi", [P, TT], I32)
        trig = sb("trig", [P, 2, TT, 32])
        zm = xn[:].rearrange("p a b -> p (a b)")[:, 0:1536]
        zs = merged[:].rearrange("p a b -> p (a b)")[:, 0:1536]
        with ExitStack() as s:
            U = [sb(f"U{i}", [P, TT, 512], F32, s) for i in range(5)]
        with ExitStack() as s:
            yT = [[sb(f"yT{i}{part}", [P, KB, SEQ], F32R, s) for part in ("hi", "lo")] for i in range(4)]
        with ExitStack() as s:
            xn_hi = sb("xn_hi", [P, TT, D], F32R, s)
            xn_lo = sb("xn_lo", [P, TT, D], F32R, s)
        yT_extra = sb("u_hold", [P, 5 * 1024])
        with ExitStack() as s:
            gates = sb("gates", [P, 4, TT, D], F32, s)
        with ExitStack() as s:
            qn = sb("qn", [P, TT, DB], F32, s)
            on = sb("on", [P, TT, DB], F32, s)
            oT_hi = sb("oT_hi", [P, KB, SEQ], F32R, s)
            oT_lo = sb("oT_lo", [P, KB, SEQ], F32R, s)
            mT_hi = sb("mT_hi", [P, KT, SEQ], F32R, s)
            memn = sb("memn", [P, TT, D], F32, s)
            mT_lo = sb("mT_lo", [P, KT, SEQ], F32R, s)
        with ExitStack() as s:
            sb("q_on_oT", [P, TT * D], F32, s)
            probT = sb("probT", [P, TT, NH, SEQ], F32, s)
            prob = sb("prob", [P, TT, NH, SEQ], F32, s)
        with ExitStack() as s:
            silu = sb("silu", [P, TT, FB], F32, s)
            act = sb("act", [P, TT, FB], F32, s)
            actT_hi = sb("actT_hi", [P, 2, SEQ], F32R, s)
            actT_lo = sb("actT_lo", [P, 2, SEQ], F32R, s)
            eT_hi = sb("eT_hi", [P, KT, P], F32R, s)
            eT_lo = sb("eT_lo", [P, KT, P], F32R, s)
            ye_hi = sb("ye_hi", [P, D], F32R, s)
            ye_lo = sb("ye_lo", [P, D], F32R, s)
            sel = sb("sel", [P, TT, P], F32R, s)
            selT = sb("selT", [P, SEQ], F32R, s)
            lg = sb("lg", [P, 12, TT, NE], F32, s)
            posm = sb("posm", [P, TT, 2 * NE], F32, s)
            comb = sb("comb", [P, TT, 2 * NE], F32, s)
            nit = sb("nit", [P, 2], I32, s)
            nitf = sb("nitf", [P, 2], F32, s)
        region_hold = sb("region_hold", [P, 4 * TT * D])
        rows_g, rows_c, rows_m = (tmp[:].rearrange("p a t c -> p (a t c)")[:, 128 * j:128 * j + 128] for j in range(3))

        ident = cst[:, C_ID:C_ID + P]
        tri_ge = cst[:, C_TRIGE:C_TRIGE + P]
        tri_lt = cst[:, C_TRILT:C_TRILT + P]
        ones = cst[:, C_ONES:C_ONES + P]
        mask = cst[:, C_MASK:C_MASK + SEQ]
        decay = cst[:, C_DECAY:C_DECAY + NH * SEQ].rearrange("p (h q) -> p h q", h=NH)

        A = [ctx.enter_context(nc.psum_tensor(f"A{i}", [P, 512], F32)) for i in range(4)]
        G = [ctx.enter_context(nc.psum_tensor(f"G{i}", [P, 512], F32)) for i in range(2)]
        T = [ctx.enter_context(nc.psum_tensor(f"T{i}", [P, 512], F32)) for i in range(2)]
        TB = [A[0], A[2], A[1], A[3]]

        landed = [sem(f"landed{j}") for j in range(RING)]
        hi_ready = sem("hi_ready")
        lo_ready = sem("lo_ready")
        used = sem("used")
        half = sem("half")
        act_step = sem("act_step")
        dve_step = sem("dve_step")
        names = {}

        def S(name):
            if name not in names:
                names[name] = sem(name)
            return names[name]

        def slot(k):
            return k % RING

        def number(lap0, k):
            return lap0 * RING + k

        MIX, MEM, XA, FFN = range(4)

        def unit_no(l, u):
            return 16 * l + u

        def place(h):
            return (h % 2) * 2 + h // 2

        def half_no(l, j):
            return l * (18 + NF) + j

        block = ctx.enter_context(nc.Block())

        @block.sync
        def _(sp):
            sp.dma_start(cst[:, 0:P], consts[:, 0:P]).then_inc(S("ident_in"), 16)
            sp.dma_start(rows_m[0:DEPTH * KT, :], norm_mix_g.rearrange("l (k p) -> (l k) p", p=P)).then_inc(S("mix_in"), 16)
            x_tiles = x[0].rearrange("(t p) d -> p t d", p=P)
            for nb in range(2):
                sp.dma_start(xs[:, :, nb * 512:nb * 512 + 512],
                             x_tiles[:, :, nb * 512:nb * 512 + 512]).then_inc(S(f"x_in{nb}"), 16)

            def load(lap0, k, view, src):
                if not isinstance(lap0, int) or number(lap0, k) >= RING:
                    sp.wait_ge(lo_ready, number(lap0, k) - RING + 1)
                if not isinstance(lap0, int):
                    sp.sem_inc(S("asked"), 1)
                for dst, part in halves(view(raw[slot(k)][:]), src):
                    sp.dma_start(dst, part).then_inc(landed[slot(k)], 16)

            def halves(dst, src):
                k = src.shape[1] // 2
                return [(dst[:, 0:k], src[:, 0:k]), (dst[:, k:], src[:, k:])]

            def rows2(r):
                return r.rearrange("p (k n) -> p k n", k=2)

            def rows4(r):
                return r.rearrange("p (k n) -> p k n", k=4)

            def pairs(r):
                return r.rearrange("p (k t c) -> p k t c", k=2, t=2)

            def block_of(n, w, col0):
                for c in range(w.shape[1] // 2):
                    load(0, n + c, rows2, w[:, 2 * c:2 * c + 2, col0:col0 + 512])

            def both_halves(lap0, k, w):
                for nb in range(2):
                    load(lap0, k + nb, rows2, w[:, :, nb * 512:nb * 512 + 512])

            def stream_ff(gu, down, lap0, first, prev, n0=0):
                for f in range(NF):
                    k = n0 + FFS * f
                    for c in range(4):
                        load(lap0, k + c + 2 * (first and f == 0), pairs, gu[:, 2 * c:2 * c + 2, :, f])
                    if f:
                        both_halves(lap0, k + 4, down[:, 2 * f - 2:2 * f])
                    elif not first:
                        both_halves(lap0, k + 4, prev[:, 2 * NF - 2:2 * NF])

            for l in range(DEPTH):
                base = LAYER0[l]
                wi = w_in[l].rearrange("(k p) n -> p k n", p=P)
                for i, b in enumerate(IN_ORDER):
                    block_of(base + IN0 + 4 * i, wi, b * 512)
                    if l + i == 0:
                        sp.dma_start(cst[:, P:], consts[:, P:]).then_inc(S("cst_in"), 16)
                for g in range(8):
                    wg = w_gate[l, g // 2].rearrange("(k p) n -> p k n", p=P)
                    block_of(base + GATE0 + 4 * g, wg, (g % 2) * 512)
                for i, b in enumerate(BR_ORDER):
                    both_halves(0, base + BR0 + 2 * i, w_branch[l, b].rearrange("(k p) n -> p k n", p=P))
                sp.wait_ge(S("prod"), 16 * l + 4)
                sp.dma_start(memn[:], mem[0].rearrange("(t p) d -> p t d", p=P)).then_inc(S("mem_in"), 16)
                wo = w_out[l].rearrange("(k p) n -> p k n", p=P)
                for nb in range(2):
                    block_of(base + OUT0 + 4 * nb, wo, nb * 512)
                wq = xa_wq[l].rearrange("(k p) n -> p k n", p=P)
                wkv = xa_wkv[l].rearrange("(k p) n -> p k n", p=P)
                for n, w in ((XK0, wkv[:, :, 0:DB]), (XQ0, wq), (XV0, wkv[:, :, DB:])):
                    for c in range(2):
                        load(0, base + n + c, rows4, w[:, 4 * c:4 * c + 4])
                both_halves(0, base + XO0, xa_wo[l].rearrange("(k p) n -> p k n", p=P))
                if l == 0:
                    gu = ffn_w_gu[0].rearrange("(k p) (t f c) -> p k t f c", p=P, t=2, c=FB)
                    down = ffn_w_down[0].rearrange("(k p) n -> p k n", p=P)
                    stream_ff(gu, down, 0, True, None, FF_N0)
                    both_halves(0, FF_N0 + FFS * NF, down[:, 2 * NF - 2:2 * NF])
            gu_e = moe_w_gu[0].rearrange("e (k p) (t f c) -> e p k t f c", p=P, t=2, c=FB)
            dn_e = moe_w_down[0].rearrange("e (k p) n -> e p k n", p=P)
            stream_ff(gu_e[0], dn_e[0], FF_LAP, True, None)
            sp.wait_ge(S("items"), 1)
            items = sp.snap(NE + sp.value_load(nit[0:1, 0:1], min_val=0, max_val=NE))
            with sp.Fori(1, items) as i:
                e = sp.snap(i & (NE - 1))
                p = sp.snap((i + (NE - 1)) & (NE - 1))
                stream_ff(gu_e[bass.ds(e, 1)].rearrange("a p k t f c -> (a p) k t f c"),
                          dn_e[bass.ds(e, 1)].rearrange("a p k n -> (a p) k n"),
                          FF_LAP + NF * i, False,
                          dn_e[bass.ds(p, 1)].rearrange("a p k n -> (a p) k n"))
            both_halves(FF_LAP + NF * items, 0, dn_e[NE - 1, :, 2 * NF - 2:2 * NF])
            for tt in range(TT):
                sp.wait_ge(S("scattered"), 4 * items - 2 + 2 * tt)
                sp.dma_start(out[0].rearrange("(t p) d -> p t d", p=P)[:, tt], xs[:, tt]).then_inc(S("stored"), 16)
            sp.wait_ge(S("stored"), 16 * TT)

        @block.gpsimd
        def _(pool):
            for base, src in ((G_XA, norm_xa_g), (G_FFN, norm_ffn_g), (G_MEM, norm_mem_g)):
                pool.dma_start(rows_g[base:base + DEPTH * KT, :],
                               src.rearrange("l (k p) -> (l k) p", p=P)).then_inc(S("rows_in"), 16)
            for base, src in ((G_CB, conv_b), (G_LG, conv_ln_g), (G_LB, conv_ln_b), (G_PS, pool_scale)):
                pool.dma_start(rows_g[base:base + 2 * DEPTH, :],
                               src.rearrange("l (k p) -> (l k) p", p=P)).then_inc(S("rows_in"), 16)
            for base, src in ((G_QG, xa_q_norm_g), (G_KG, xa_k_norm_g)):
                for j in range(2):
                    pool.dma_start(rows_g[base:base + DEPTH, 64 * j:64 * j + 64], src).then_inc(S("rows_in"), 16)
            pool.dma_start(rows_c[0:2 * CONV_W * DEPTH, :],
                           conv_w.rearrange("l w (k p) -> (l w k) p", p=P)).then_inc(S("rows_in"), 16)
            for l in range(DEPTH):
                for j in range(2):
                    pool.dma_start(poolw[64 * j:64 * j + 64, l],
                                   pool_w[l].rearrange("(g j) c d -> j c g d", j=2)[j]).then_inc(S("poolw_in"), 16)
            pool.dma_start(posi[:], positions[0].rearrange("(t p) -> p t", p=P),
                           allow_slow_non_contiguous=True).then_inc(S("pos_in"), 16)
            pool.dma_start(rt[:], moe_router[0].rearrange("(k p) e -> p k e", p=P)).then_inc(S("rt_in"), 16)
            for l in range(DEPTH):
                for i in range(1, 4):
                    for nb in range(2):
                        for tt in range(TT):
                            step = 16 * l + 4 * i + 2 * nb + tt
                            pool.wait_ge(S("prod"), step + 1)
                            if i > 1:
                                pool.wait_ge(S("summed"), 12 * l + 4 * (i - 1) + 2 * nb + tt - 3)
                            b = BR_ORDER[i]
                            sl = slice(nb * 512, nb * 512 + 512)
                            pool.tensor_tensor(merged[:, tt, sl], merged[:, tt, sl], gates[:, b, tt, sl],
                                               ALU.add).then_inc(S("summed"), 1)
            pool.wait_ge(S("mergedT"), 4 * DEPTH)
            pool.dma_start(merged[:, 0, :], norm_ffn_g[DEPTH - 1:DEPTH, :].to_broadcast([P, D])).then_inc(S("grow_in"), 16)

        @block.tensor
        def _(pe):
            def product(dst, a_hi, a_lo, b_hi, b_lo, first, last):
                pe.matmul(dst, a_hi, b_hi, start=first, stop=False)
                pe.matmul(dst, a_lo, b_hi, start=False, stop=False)
                return pe.matmul(dst, a_hi, b_lo, start=False, stop=last)

            def have(lap0, k):
                pe.wait_ge(lo_ready, number(lap0, k) + 1)

            def streamed(n0, hi, lo, free, before=None, banks=G, nchunks=4, kts=2, width=512):
                for c in range(nchunks):
                    n = n0 + c
                    if before:
                        before(c)
                    have(0, n)
                    wh = w_hi[slot(n)][:].rearrange("p (k n) -> p k n", k=kts)
                    wl = w_lo[slot(n)][:].rearrange("p (k n) -> p k n", k=kts)
                    for tt in range(TT):
                        if c == 0 and free[tt]:
                            pe.wait_ge(*free[tt])
                        for k in range(kts):
                            kk = c * kts + k
                            mm = product(banks[tt][:, 0:width], hi[:, kk, tt * P:tt * P + P],
                                         lo[:, kk, tt * P:tt * P + P], wh[:, k, :], wl[:, k, :],
                                         kk == 0, kk == nchunks * kts - 1)
                        if tt == 0 and c == nchunks - 1:
                            mm.then_inc(half, 1)
                    mm.then_inc(used, 1)

            def turn(src, banks, done):
                for b in banks:
                    for kt in (2 * b, 2 * b + 1):
                        for tt in range(TT):
                            mm = pe.transpose(TB[b][:, (kt % 2) * 256 + tt * P:(kt % 2) * 256 + tt * P + P],
                                              src[:, tt, kt * P:kt * P + P], ident)
                    mm.then_inc(done, 1)

            def parts(name, count):
                pe.wait_ge(S(name + "_hi"), count)
                pe.wait_ge(S(name + "_lo"), count)

            def transpose_narrow(dst, src):
                for c in range(KB):
                    for tt in range(TT):
                        mm = pe.transpose(dst[:, c * SEQ + tt * P:c * SEQ + tt * P + P],
                                          src(tt, slice(c * P, c * P + P)), ident)
                return mm

            def scores(q, k, done):
                for h in range(NH):
                    r = slice((h % 2) * HD, (h % 2) * HD + HD)
                    pe.matmul(A[1 + h % 2][:, (h // 2) * SEQ:(h // 2) * SEQ + SEQ], k[r, h // 2, 0:P], q[r, h // 2, :],
                              start=True, stop=True)
                for h in (0, 2, 1, 3):
                    r = slice((h % 2) * HD, (h % 2) * HD + HD)
                    j = place(h)
                    mm = pe.matmul(A[3][:, j * P:j * P + P], k[r, h // 2, P:SEQ], q[r, h // 2, P:SEQ],
                                   start=True, stop=True)
                    if h == 2:
                        rows[0] += 1
                        mm.then_inc(S("even_heads"), 1)
                        pe.wait_ge(S("even_heads"), rows[0])
                mm.then_inc(done, 1)

            rows = [0]

            pe.wait_ge(S("ident_in"), 16)
            pe.wait_ge(S("mix_in"), 16)
            pe.transpose(T[0][:, 0:DEPTH * KT], rows_m[0:DEPTH * KT, :],
                         ident[0:DEPTH * KT, 0:DEPTH * KT]).then_inc(S("mix_cols"), 1)

            def after_unit(l, u):
                n = unit_no(l, u)
                return [(S("emptied"), 2 * n - 1), (S("emptied"), 2 * n)]

            for l in range(DEPTH):
                base = LAYER0[l]
                def second_half(c):
                    if c == 1:
                        if l == 0:
                            pe.wait_ge(S("x_in1"), 16)
                        else:
                            pe.wait_ge(S("ffn_added"), 4)
                        turn(xs, (2, 3), S("xT"))
                    parts("hT", 12 * l + c + 1)

                if l == 0:
                    pe.wait_ge(S("x_in0"), 16)
                    free0 = [None, None]
                else:
                    pe.wait_ge(S("ffn_added"), 2)
                    free0 = [(S("ff_act"), 2 * NF - 1), (S("ff_act"), 2 * NF)]
                turn(xs, (0, 1), S("xT"))
                streamed(base + IN0, hT_hi, hT_lo, free0, second_half)
                if l == 0:
                    pe.wait_ge(S("rows_in"), 16 * 12)
                    pe.transpose(T[1][:, 0:G_ROWS], rows_g[0:G_ROWS, :], ident[0:G_ROWS, 0:G_ROWS])
                    pe.transpose(T[1][:, 128:128 + 2 * CONV_W * DEPTH], rows_c[0:2 * CONV_W * DEPTH, :],
                                 ident[0:2 * CONV_W * DEPTH, 0:2 * CONV_W * DEPTH]).then_inc(S("cols"), 1)
                streamed(base + IN0 + 4, hT_hi, hT_lo, after_unit(l, 1))
                streamed(base + IN0 + 8, hT_hi, hT_lo, after_unit(l, 2))
                pe.wait_ge(S("emptied"), 2 * unit_no(l, 2))
                if l == 0:
                    pe.wait_ge(S("cols_out"), 1)
                else:
                    pe.wait_ge(S("actT_hi"), NF)
                    pe.wait_ge(S("actT_lo"), NF)
                transpose_narrow(T[0][:], lambda tt, c: U[1][:, tt, 256 + c.start:256 + c.stop])
                transpose_narrow(T[1][:], lambda tt, c: U[2][:, tt, c]).then_inc(S("sb_qk"), 1)
                if l == 0:
                    pe.wait_ge(S("cst_in"), 16)
                for g in range(4):
                    o = A[0][(g % 2) * 64:(g % 2) * 64 + 64, (g // 2) * SEQ:(g // 2) * SEQ + SEQ]
                    c0 = C_BAND + g * 384
                    pe.matmul(o, U[1][:, 0, g * 64:g * 64 + 64], cst[:, c0:c0 + 256], start=True, stop=False)
                    mm = pe.matmul(A[0][(g % 2) * 64:(g % 2) * 64 + 64, (g // 2) * SEQ + P:(g // 2) * SEQ + SEQ],
                                   U[1][:, 1, g * 64:g * 64 + 64], cst[:, c0 + 256:c0 + 384], start=False, stop=True)
                mm.then_inc(S("pool_d"), 1)
                streamed(base + IN0 + 12, hT_hi, hT_lo, after_unit(l, 3))
                pe.wait_ge(S("sb_qk_out"), l + 1)
                scores(qT, kT, S("sb_z"))
                pe.wait_ge(S("dT_out"), l + 1)
                if l == 0:
                    pe.wait_ge(S("poolw_in"), 16 * 4)
                for g in range(4):
                    r = slice((g % 2) * 64, (g % 2) * 64 + 64)
                    mm = pe.matmul(T[0][r, (g // 2) * SEQ:(g // 2) * SEQ + SEQ], poolw[r, l, g // 2, :], dT[r, g // 2, :],
                                   start=True, stop=True)
                mm.then_inc(S("pool_y"), 1)
                streamed(base + IN0 + 16, hT_hi, hT_lo, after_unit(l, 4))
                pe.wait_ge(S("conv_v"), l + 1)
                transpose_narrow(T[1][:], lambda tt, c: convn[:, tt, c]).then_inc(S("conv_vT"), 1)

                def gate(g):
                    streamed(base + GATE0 + 4 * g, hT_hi, hT_lo, after_unit(l, 5 + g))

                gate(0)
                pe.wait_ge(S("sb_sp"), l + 1)
                for j in range(NH):
                    zk0 = zs[:, j * SEQ:j * SEQ + SEQ]
                    zk1 = zs[:, NH * SEQ + j * P:NH * SEQ + j * P + P]
                    o = A[1 + j // 2]
                    pe.matmul(o[:, (j % 2) * SEQ:(j % 2) * SEQ + SEQ], tri_ge, zk0, start=True, stop=False)
                    pe.matmul(o[:, (j % 2) * SEQ + P:(j % 2) * SEQ + SEQ], ones, zk1, start=False, stop=True)
                mm = pe.matmul(A[3][:], tri_ge, zs[:, NH * SEQ:NH * SEQ + NH * P], start=True, stop=True)
                mm.then_inc(S("sb_tail"), 1)
                gate(1)
                pe.wait_ge(S("rotated"), l + 1)
                pe.wait_ge(S("yT_lo1"), l + 1)
                pe.wait_ge(S("vT_out"), l + 1)
                transpose_narrow(T[0][:], lambda tt, c: U[3][:, tt, c])
                transpose_narrow(T[1][:], lambda tt, c: U[3][:, tt, 256 + c.start:256 + c.stop]).then_inc(S("ret_qk"), 1)
                gate(2)
                pe.wait_ge(S("sb_a"), l + 1)
                for h in (0, 2, 1, 3):
                    r = slice((h % 2) * HD, (h % 2) * HD + HD)
                    c0 = (h // 2) * SEQ
                    pe.matmul(A[0][r, c0:c0 + SEQ], U[2][:, 0, 256 + h * HD:256 + h * HD + HD],
                              zm[:, place(h) * SEQ:place(h) * SEQ + SEQ], start=True, stop=False)
                    mm = pe.matmul(A[0][r, c0 + P:c0 + SEQ], U[2][:, 1, 256 + h * HD:256 + h * HD + HD],
                                   zm[:, NH * SEQ + place(h) * P:NH * SEQ + place(h) * P + P], start=False, stop=True)
                mm.then_inc(S("sb_y"), 1)
                gate(3)
                pe.wait_ge(S("ret_qk_out"), l + 1)
                pe.wait_ge(S("sb_w"), l + 1)
                scores(qT, kT, S("ret_z"))
                gate(4)
                pe.wait_ge(S("ret_a"), l + 1)
                for tt in range(TT):
                    for h in range(NH):
                        o = T[1][:, tt * DB + h * HD:tt * DB + h * HD + HD]
                        mm = pe.matmul(o, zs[:, place(h) * SEQ + tt * P:place(h) * SEQ + tt * P + P], U[4][:, 0, h * HD:h * HD + HD],
                                       start=True, stop=(tt == 0))
                        if tt:
                            mm = pe.matmul(o, zs[:, NH * SEQ + place(h) * P:NH * SEQ + place(h) * P + P],
                                           U[4][:, 1, h * HD:h * HD + HD], start=False, stop=True)
                mm.then_inc(S("ret_o"), 1)
                gate(5)
                pe.wait_ge(S("tap"), KB * CONV_W * (l + 1))
                for c in range(KB):
                    for tt in range(TT):
                        mm = pe.transpose(T[0][:, tt * DB + c * P:tt * DB + c * P + P], conv[:, c, tt * P:tt * P + P],
                                          ident)
                mm.then_inc(S("conv_nat"), 1)
                gate(6)
                pe.wait_ge(S("ret_y"), l + 1)
                transpose_narrow(A[1][:], lambda tt, c: tmp[:, 0, tt, c]).then_inc(S("ret_yT"), 1)
                gate(7)
                pe.wait_ge(S("conv_ln"), l + 1)
                transpose_narrow(A[2][:], lambda tt, c: convn[:, tt, c]).then_inc(S("conv_lnT"), 1)
                for i, b in enumerate(BR_ORDER):
                    pe.wait_ge(S(f"yT_lo{b}"), l + 1)
                    pe.wait_ge(S(f"yT_hi{b}"), l + 1)
                    for nb in range(2):
                        n = base + BR0 + 2 * i + nb
                        have(0, n)
                        wh = w_hi[slot(n)][:].rearrange("p (k n) -> p k n", k=2)
                        wl = w_lo[slot(n)][:].rearrange("p (k n) -> p k n", k=2)
                        for tt in range(TT):
                            if i:
                                pe.wait_ge(S("prod"), 16 * l + 4 * (i - 1) + 2 * nb + tt + 1)
                            elif nb == 0:
                                pe.wait_ge(S("emptied"), 2 * unit_no(l, 13))
                            for k in range(KB):
                                mm = product((G, T)[nb][tt][:], yT[b][0][:, k, tt * P:tt * P + P],
                                             yT[b][1][:, k, tt * P:tt * P + P], wh[:, k, :], wl[:, k, :],
                                             k == 0, k == KB - 1)
                            mm.then_inc(S("branch") if tt == 0 else used, 1)
                def second_merged(c):
                    if c == 1:
                        pe.wait_ge(S("summed"), 12 * (l + 1))
                        turn(merged, (2, 3), S("mergedT"))
                    parts("gT", 4 * l + c + 1)

                pe.wait_ge(S("summed"), 12 * l + 10)
                turn(merged, (0, 1), S("mergedT"))
                done = 16 * (l + 1)
                streamed(base + OUT0, hT_hi, hT_lo, [(S("prod"), done), (S("prod"), done)], second_merged)
                pe.wait_ge(S("mem_in"), 16 * (l + 1))
                turn(memn, range(4), S("memT"))
                streamed(base + OUT0 + 4, hT_hi, hT_lo, [(S("out_added"), 4 * l + 1), (S("out_added"), 4 * l + 2)])

                def memory_parts(c):
                    if c == 1:
                        parts("mT", 4 * l + 4)
                        pe.wait_ge(S("out_added"), 4 * (l + 1))
                        turn(xs, range(4), S("xT"))
                    parts("mT", 4 * l + 2 * c + 2)

                streamed(base + XK0, mT_hi, mT_lo, [(S("out_added"), 4 * l + 3), (S("out_added"), 4 * l + 4)],
                         memory_parts, nchunks=2, kts=4, width=DB)
                streamed(base + XQ0, hT_hi, hT_lo, [None, None], lambda c: parts("hT", 12 * l + 4 + 2 * c + 2),
                         banks=T, nchunks=2, kts=4, width=DB)
                pe.wait_ge(S("mk_normed"), l + 1)
                transpose_narrow(A[0][:], lambda tt, c: tmp[:, 0, tt, c]).then_inc(S("memkT"), 1)

                def queries_between(c):
                    if c == 1:
                        pe.wait_ge(S("q_normed"), l + 1)
                        transpose_narrow(T[0][:], lambda tt, c: qn[:, tt, c]).then_inc(S("xqT"), 1)

                n = 2 * unit_no(l, 14)
                streamed(base + XV0, mT_hi, mT_lo, [(S("emptied"), n - 1), (S("emptied"), n)],
                         queries_between, nchunks=2, kts=4, width=DB)
                pe.wait_ge(S("memk_out"), l + 1)
                pe.wait_ge(S("xqT_out"), l + 1)
                for tt in range(TT):
                    for h in range(NH):
                        r = slice((h % 2) * HD, (h % 2) * HD + HD)
                        mm = pe.matmul(A[2 * tt + h % 2][:, (h // 2) * SEQ:(h // 2) * SEQ + SEQ],
                                       qT[r, h // 2, tt * P:tt * P + P], memk[r, h // 2, :], start=True, stop=True)
                    mm.then_inc(S("x_scores"), 1)
                for tt in range(TT):
                    pe.wait_ge(S("xp"), 4 * TT * l + 4 * tt + 4)
                    for j in range(NH):
                        for mt in range(TT):
                            mm = pe.transpose(A[2 * tt + j // 2][:, (j % 2) * SEQ + mt * P:(j % 2) * SEQ + mt * P + P],
                                              prob[:, tt, j, mt * P:mt * P + P], ident)
                    mm.then_inc(S("xpT"), 1)
                pe.wait_ge(S("xpT_out"), 4 * (l + 1))
                pe.wait_ge(S("emptied"), 2 * unit_no(l, 16))
                for tt in range(TT):
                    for h in range(NH):
                        for mt in range(TT):
                            mm = pe.matmul(T[1][:, tt * DB + h * HD:tt * DB + h * HD + HD],
                                           probT[:, tt, place(h), mt * P:mt * P + P], memv[:, mt, h * HD:h * HD + HD],
                                           start=(mt == 0), stop=(mt == TT - 1))
                mm.then_inc(S("xo"), 1)
                pe.wait_ge(S("xo_normed"), l + 1)
                transpose_narrow(T[0][:], lambda tt, c: on[:, tt, c]).then_inc(S("xoT"), 1)
                pe.wait_ge(S("oT_hi"), l + 1)
                pe.wait_ge(S("oT_lo"), l + 1)
                for nb in range(2):
                    n = base + XO0 + nb
                    have(0, n)
                    wh = w_hi[slot(n)][:].rearrange("p (k n) -> p k n", k=2)
                    wl = w_lo[slot(n)][:].rearrange("p (k n) -> p k n", k=2)
                    for tt in range(TT):
                        if nb and tt:
                            pe.wait_ge(S("xo_added"), 4 * l + 2)
                            turn(xs, (0, 1), S("xT"))
                        for k in range(KB):
                            mm = product((G, T)[nb][tt][:], oT_hi[:, k, tt * P:tt * P + P],
                                         oT_lo[:, k, tt * P:tt * P + P], wh[:, k, :], wl[:, k, :],
                                         k == 0, k == KB - 1)
                        mm.then_inc(S("xproj") if tt == 0 else used, 1)
                if l:
                    pe.wait_ge(S("xo_added"), 4 * (l + 1))
                    turn(xs, (2, 3), S("xT"))
                    break

                def transposed_act(f):
                    pe.wait_ge(S("ff_act"), 2 * (f + 1))
                    if f:
                        pe.wait_ge(S("actT_hi"), f)
                        pe.wait_ge(S("actT_lo"), f)
                    transpose_narrow(T[0][:], lambda tt, c: act[:, tt, c]).then_inc(S("ff_actT"), 1)

                def down(f):
                    pe.wait_ge(S("actT_hi"), f + 1)
                    pe.wait_ge(S("actT_lo"), f + 1)
                    for nb in range(2):
                        n = FF_N0 + FFS * (f + 1) + (4 if f < NF - 1 else 0) + nb
                        have(0, n)
                        wh = w_hi[slot(n)][:].rearrange("p (k n) -> p k n", k=2)
                        wl = w_lo[slot(n)][:].rearrange("p (k n) -> p k n", k=2)
                        for tt in range(TT):
                            for k in range(2):
                                mm = product(A[2 * tt + nb][:], actT_hi[:, k, tt * P:tt * P + P],
                                             actT_lo[:, k, tt * P:tt * P + P], wh[:, k, :], wl[:, k, :],
                                             f == 0 and k == 0, f == NF - 1 and k == 1)
                        mm.then_inc(used, 1)

                for f in range(NF):
                    for c in range(4):
                        n = FF_N0 + FFS * f + c + 2 * (f == 0)
                        if f == 0:
                            if c == 1:
                                pe.wait_ge(S("xo_added"), 4 * (l + 1))
                                turn(xs, (2, 3), S("xT"))
                            parts("hT", 12 * l + 8 + c + 1)
                        have(0, n)
                        wh = w_hi[slot(n)][:].rearrange("p (k n) -> p k n", k=2)
                        wl = w_lo[slot(n)][:].rearrange("p (k n) -> p k n", k=2)
                        for tt in range(TT):
                            if c == 0 and f:
                                pe.wait_ge(S("ff_act"), 2 * f - 1 + tt)
                            for k in range(2):
                                mm = product(G[tt][:], hT_hi[:, 2 * c + k, tt * P:tt * P + P],
                                             hT_lo[:, 2 * c + k, tt * P:tt * P + P], wh[:, k, :], wl[:, k, :],
                                             c + k == 0, c == 3 and k == 1)
                            if c == 3 and tt == 0:
                                mm.then_inc(half, 1)
                        mm.then_inc(used, 1)
                        if f and c == 1:
                            transposed_act(f - 1)
                    if f:
                        down(f - 1)
                transposed_act(NF - 1)
                down(NF - 1)

            pe.wait_ge(S("rhT"), 4)
            pe.wait_ge(S("rt_in"), 16)
            for tt in range(TT):
                for k in range(KT):
                    mm = pe.matmul(T[0][:, tt * NE:tt * NE + NE], hT_f32[:, k, tt * P:tt * P + P], rt[:, k, :],
                                   start=(k == 0), stop=(k == KT - 1))
            mm.then_inc(S("logits"), 1)
            pe.wait_ge(S("picked"), 1)
            pe.matmul(T[1][:, 0:NE], tri_lt, lg[:, 6, 0, :], start=True, stop=True)
            pe.matmul(T[1][:, NE:2 * NE], ones, lg[:, 6, 0, :], start=True, stop=False)
            pe.matmul(T[1][:, NE:2 * NE], tri_lt, lg[:, 6, 1, :], start=False, stop=True)
            pe.matmul(T[1][:, 2 * NE:3 * NE], ones, lg[:, 6, 0, :], start=True, stop=False)
            pe.matmul(T[1][:, 2 * NE:3 * NE], ones, lg[:, 6, 1, :], start=False, stop=True).then_inc(S("counted"), 1)
            pe.wait_ge(S("items"), 1)
            items = pe.snap(NE + pe.value_load(nit[0:1, 0:1], min_val=0, max_val=NE))
            GB = [G[0], G[1], T[1]]

            def gather(i):
                pe.wait_ge(S("sel"), i + 1)
                for k in range(KT):
                    for tt in range(TT):
                        for part in (xn_hi, xn_lo):
                            mm = pe.matmul(A[2 + k // 4][:, (k % 4) * P:(k % 4) * P + P], part[:, tt, k * P:k * P + P],
                                           sel[:, tt, :], start=(tt == 0 and part is xn_hi),
                                           stop=(tt == TT - 1 and part is xn_lo))
                mm.then_inc(S("gathered"), 1)

            def turn_selection(i):
                for tt in range(TT):
                    mm = pe.transpose(T[0][:, 256 + tt * P:256 + tt * P + P], sel[:, tt, :].bitcast(F32), ident)
                mm.then_inc(S("selT"), 1)

            def e_transposed(step, turned=None):
                pe.wait_ge(S("e_act"), step + 1)
                if turned is not None:
                    pe.wait_ge(S("selT_out"), turned)
                for c in range(2):
                    mm = pe.transpose(T[0][:, c * P:c * P + P], act[:, 0, c * P:c * P + P], ident)
                mm.then_inc(S("e_actT"), 1)

            def e_down(lap0, k, step, f):
                pe.wait_ge(S("e_aT_hi"), step + 1)
                pe.wait_ge(S("e_aT_lo"), step + 1)
                for nb in range(2):
                    have(lap0, k + nb)
                    wh = w_hi[slot(k + nb)][:].rearrange("p (k n) -> p k n", k=2)
                    wl = w_lo[slot(k + nb)][:].rearrange("p (k n) -> p k n", k=2)
                    for kk in range(2):
                        mm = product(A[nb][:], actT_hi[:, kk, 0:P], actT_lo[:, kk, 0:P], wh[:, kk, :], wl[:, kk, :],
                                     f == 0 and kk == 0, f == NF - 1 and kk == 1)
                    mm.then_inc(used, 1)

            def scatter(i, tt):
                pe.wait_ge(S("ye_hi"), 2 * i + 2)
                pe.wait_ge(S("ye_lo"), 2 * i + 2)
                pe.wait_ge(S("selT_out"), i + 1)
                if tt:
                    pe.wait_ge(S("scattered"), 4 * i + 2)
                for nb in range(2):
                    for part in (ye_hi, ye_lo):
                        mm = pe.matmul(A[2 + nb][:], selT[:, tt * P:tt * P + P], part[:, nb * 512:nb * 512 + 512],
                                       start=part is ye_hi, stop=part is ye_lo)
                mm.then_inc(S("scat"), 1)

            def item(i, first=False, last=False):
                lap0 = FF_LAP + NF * i
                pe.wait_ge(S("eT_lo"), 2 * i + 2)
                pe.wait_ge(S("eT_hi"), 2 * i + 2)
                for f in range(NF):
                    step = NF * i + f
                    for c in range(4):
                        k = FFS * f + c + 2 * (first and f == 0)
                        have(lap0, k)
                        if c == 0 and (f >= 3 or not first):
                            back = (2, 2, 5)[f] if f < 3 else 3
                            pe.wait_ge(S("e_act"), step - back + 1)
                        wh = w_hi[slot(k)][:].rearrange("p (k n) -> p k n", k=2)
                        wl = w_lo[slot(k)][:].rearrange("p (k n) -> p k n", k=2)
                        for kk in range(2):
                            mm = product(GB[f % 3][:], eT_hi[:, 2 * c + kk, :], eT_lo[:, 2 * c + kk, :],
                                         wh[:, kk, :], wl[:, kk, :], c + kk == 0, c == 3 and kk == 1)
                        mm.then_inc(used, 1)
                        if c == 1 and not (first and f == 0):
                            e_transposed(step - 1, i + 1 if f == 5 else None)
                    if f:
                        if f == 1 and not first:
                            pe.wait_ge(S("ye_hi"), 2 * i)
                            pe.wait_ge(S("ye_lo"), 2 * i)
                        e_down(lap0, FFS * f + 4, step - 1, f - 1)
                    elif not first:
                        e_down(lap0, 4, step - 1, NF - 1)
                    if f in (1, 2) and not first:
                        scatter(i - 1, f - 1)
                    if f == 4:
                        turn_selection(i)
                    if f == 8 and not last:
                        if not first:
                            pe.wait_ge(S("scattered"), 4 * i)
                        gather(i + 1)

            pe.wait_ge(S("xn_hi"), TT)
            pe.wait_ge(S("xn_lo"), TT)
            gather(0)
            item(0, first=True)
            with pe.Fori(1, items - 1) as i:
                item(i)
            last = pe.snap(items - 1)
            item(last, last=True)
            e_transposed(last * NF + NF - 1)
            e_down(FF_LAP + NF * items, 0, last * NF + NF - 1, NF - 1)
            scatter(last, 0)
            scatter(last, 1)

        @block.scalar
        def _(act_e):
            steps = [0]

            def link(ins):
                steps[0] += 1
                ins.then_inc(act_step, 1)
                act_e.wait_ge(act_step, steps[0])

            nxt = [0]

            def split_to(k_end, lap0=0):
                while nxt[0] < k_end:
                    k = nxt[0]
                    act_e.wait_ge(landed[slot(k)], 32 * (lap0 + k // RING + 1))
                    if not isinstance(lap0, int) or number(lap0, k) >= RING:
                        act_e.wait_ge(used, number(lap0, k) - RING + 1)
                    nc.scalar.activation(w_hi[slot(k)][:], raw[slot(k)][:], ACT.Copy).then_inc(hi_ready, 1)
                    nxt[0] += 1

            def ahead(k, lap0=0):
                split_to(k + RING, lap0)

            def token_roots(l, norm, src):
                j = 4 * l + norm
                for tt in range(TT):
                    ins = nc.scalar.activation(xn[:, tt, :], src[:, tt, :], ACT.Square, accum_out=ssq[:, j, tt:tt + 1])
                    link(ins)
                nc.scalar.activation(srt[:, j, :], ssq[:, j, :], ACT.Sqrt, scale=1.0 / D,
                                     bias=eps_col[:, 0:1]).then_inc(S("rooted_tokens"), 1)

            def scaled(dst, src, l, norm, tt, func=ACT.Copy):
                return nc.scalar.activation(dst, src, func, scale=rs[:, 4 * l + norm, tt:tt + 1])

            roots = [0]

            def square_root():
                roots[0] += 1
                act_e.wait_ge(S("mean_square"), roots[0])
                nc.scalar.activation(root[:, 1, :], root[:, 0, :], ACT.Sqrt).then_inc(S("rooted"), 1)

            def round_wide(dst, gain, done, ready, count, banks=range(4)):
                for b in banks:
                    act_e.wait_ge(ready, count + b + 1)
                    for kt in (2 * b, 2 * b + 1):
                        bank = TB[b][:, (kt % 2) * SEQ:(kt % 2) * SEQ + SEQ]
                        ins = nc.scalar.activation(dst[:, kt, :], bank, ACT.Copy, scale=gain[:, kt:kt + 1])
                    ins.then_inc(done, 1)

            def gains(l, first):
                return gcol[:, first + KT * l:first + KT * l + KT]

            act_e.wait_ge(S("mix_cols"), 1)
            nc.scalar.activation(gmix[:], T[0][:, 0:DEPTH * KT], ACT.Copy).then_inc(S("gmix_out"), 1)
            act_e.wait_ge(S("gmix_out"), 1)
            act_e.wait_ge(S("eps_set"), 3)

            for l in range(DEPTH):
                base = LAYER0[l]
                mix_gain = gmix[:, KT * l:KT * l + KT]
                round_wide(hT_hi, mix_gain, S("hT_hi"), S("xT"), 12 * l, (0, 1))
                if l == 0:
                    split_to(2)
                round_wide(hT_hi, mix_gain, S("hT_hi"), S("xT"), 12 * l, (2, 3))
                if l == 0:
                    split_to(3)
                token_roots(l, MIX, xs)

                def unit(u, n, evacuate):
                    ahead(n)
                    for tt in range(TT):
                        if tt == 0:
                            act_e.wait_ge(half, half_no(l, u if u < 13 else u + 2) + 1)
                        else:
                            act_e.wait_ge(used, n + 1)
                        if tt == 0 and u in (0, 13, 14):
                            act_e.wait_ge(S("token_scale"), 4 * l + {0: MIX, 13: MEM, 14: XA}[u] + 1)
                        evacuate(tt).then_inc(S("emptied"), 1)

                def whole(b):
                    return lambda tt: scaled(U[b][:, tt, :], G[tt][:], l, MIX, tt)

                def two(b, func):
                    def evacuate(tt):
                        scaled(U[b][:, tt, 0:DB], G[tt][:, 0:DB], l, MIX, tt)
                        return scaled(U[b][:, tt, DB:], G[tt][:, DB:], l, MIX, tt, func)
                    return evacuate

                unit(0, base + 3, whole(1))
                if l == 0:
                    act_e.wait_ge(S("cols"), 1)
                    nc.scalar.activation(gcol[:], T[1][:, 0:G_ROWS], ACT.Copy)
                    nc.scalar.activation(cwcol[:], T[1][:, 128:128 + 2 * CONV_W * DEPTH],
                                         ACT.Copy).then_inc(S("cols_out"), 1)
                    act_e.wait_ge(S("cols_out"), 1)
                unit(1, base + 7, whole(2))
                unit(2, base + 11, two(0, ACT.Sigmoid))
                act_e.wait_ge(S("sb_qk"), l + 1)
                nc.scalar.activation(qT[:].rearrange("p c t -> p (c t)"), T[0][:], ACT.Copy, scale=HD ** -0.5)
                nc.scalar.activation(kT[:].rearrange("p c t -> p (c t)"), T[1][:], ACT.Copy).then_inc(S("sb_qk_out"), 1)
                act_e.wait_ge(S("pool_d"), l + 1)
                nc.scalar.activation(dT[:].rearrange("p c t -> p (c t)"), A[0][:], ACT.Copy).then_inc(S("dT_out"), 1)
                if l == 0:
                    act_e.wait_ge(S("angles"), 1)
                    ang = tmp[:, 1].rearrange("p t c -> p (t c)")
                    link(nc.scalar.activation(ang[:, 64:128], ang[:, 0:64], ACT.Abs))
                    nc.scalar.activation(trig[:, 1].rearrange("p t c -> p (t c)"), ang[:, 0:64], ACT.Sin)
                    nc.scalar.activation(trig[:, 0].rearrange("p t c -> p (t c)"), ang[:, 64:128],
                                         ACT.Sin, scale=-1.0, bias=half_pi[:, 0:1]).then_inc(S("trig"), 1)
                unit(3, base + 15, whole(3))
                act_e.wait_ge(S("pool_y"), l + 1)
                for c in range(KB):
                    ins = nc.scalar.activation(yT[1][0][:, c, :], T[0][:, c * SEQ:c * SEQ + SEQ], ACT.Copy,
                                               scale=gcol[:, G_PS + 2 * l + c:G_PS + 2 * l + c + 1])
                ins.then_inc(S("yT_hi1"), 1)
                unit(4, base + 19, two(4, ACT.Silu))
                act_e.wait_ge(S("conv_vT"), l + 1)
                nc.scalar.activation(vT[:, :, CONV_W - 1:], T[1][:].rearrange("p (c t) -> p c t", c=KB),
                                     ACT.Copy).then_inc(S("vT_out"), 1)
                act_e.wait_ge(S("sb_zm"), l + 1)
                link(nc.scalar.activation(zs, zm, ACT.Abs))
                link(nc.scalar.activation(zs, zs, ACT.Exp, scale=-1.0))
                nc.scalar.activation(zs, zs, ACT.Ln, bias=one_col[:, 0:1]).then_inc(S("sb_l"), 1)

                def gate(g):
                    unit(5 + g, base + GATE0 + 4 * g + 3, lambda tt: scaled(
                        gates[:, g // 2, tt, (g % 2) * 512:(g % 2) * 512 + 512], G[tt][:], l, MIX, tt, ACT.Sigmoid))

                gate(0)
                gate(1)
                act_e.wait_ge(S("sb_w"), l + 1)
                nc.scalar.activation(zm, zm, ACT.Exp).then_inc(S("sb_exp"), 1)
                act_e.wait_ge(S("ret_qk"), l + 1)
                nc.scalar.activation(qT[:].rearrange("p c t -> p (c t)"), T[0][:], ACT.Copy)
                nc.scalar.activation(kT[:].rearrange("p c t -> p (c t)"), T[1][:], ACT.Copy).then_inc(S("ret_qk_out"), 1)
                gate(2)
                gate(3)
                act_e.wait_ge(S("sb_y"), l + 1)
                nc.scalar.activation(yT[2][0][:].rearrange("p c t -> p (c t)"), A[0][:], ACT.Copy).then_inc(S("yT_hi2"), 1)
                gate(4)
                gate(5)
                square_root()
                gate(6)
                square_root()
                gate(7)
                act_e.wait_ge(S("ret_yT"), l + 1)
                nc.scalar.activation(yT[3][0][:].rearrange("p c t -> p (c t)"), A[1][:], ACT.Copy).then_inc(S("yT_hi3"), 1)
                act_e.wait_ge(S("conv_lnT"), l + 1)
                for c in range(KB):
                    g0, b0 = G_LG + 2 * l + c, G_LB + 2 * l + c
                    link(nc.scalar.activation(conv[:, c, :], A[2][:, c * SEQ:c * SEQ + SEQ], ACT.Silu,
                                              scale=gcol[:, g0:g0 + 1], bias=gcol[:, b0:b0 + 1]))
                nc.scalar.activation(yT[0][0][:], conv[:], ACT.Copy).then_inc(S("yT_hi0"), 1)
                ahead(base + BR0 + 6)
                for b in range(4):
                    act_e.wait_ge(S("mergedT"), 4 * l + b + 1)
                    nc.scalar.activation(hT_hi[:, 2 * b:2 * b + 2, :].rearrange("p c t -> p (c t)"), TB[b][:],
                                         ACT.Copy).then_inc(S("gT_hi"), 1)
                act_e.wait_ge(S("mem_in"), 16 * (l + 1))
                token_roots(l, MEM, memn)
                ahead(base + OUT0 + 3)
                round_wide(mT_hi, gains(l, G_MEM), S("mT_hi"), S("memT"), 4 * l)
                ahead(base + OUT0 + 7)
                round_wide(hT_hi, gains(l, G_XA), S("hT_hi"), S("xT"), 12 * l + 4)
                token_roots(l, XA, xs)
                unit(13, base + XK0 + 1, lambda tt: scaled(convn[:, tt, :], G[tt][:, 0:DB], l, MEM, tt))
                square_root()
                unit(14, base + XQ0 + 1, lambda tt: scaled(qn[:, tt, :], T[tt][:, 0:DB], l, XA, tt))
                act_e.wait_ge(S("memkT"), l + 1)
                nc.scalar.activation(memk[:].rearrange("p c t -> p (c t)"), A[0][:], ACT.Copy).then_inc(S("memk_out"), 1)
                square_root()
                act_e.wait_ge(S("xqT"), l + 1)
                nc.scalar.activation(qT[:].rearrange("p c t -> p (c t)"), T[0][:], ACT.Copy,
                                     scale=gqk[:, l:l + 1]).then_inc(S("xqT_out"), 1)
                unit(15, base + XV0 + 1, lambda tt: scaled(memv[:, tt, :], G[tt][:, 0:DB], l, MEM, tt))
                for tt in range(TT):
                    act_e.wait_ge(S("xmax"), TT * l + tt + 1)
                    for i in range(NH):
                        j = tt * NH + i
                        nc.scalar.activation(prob[:, tt, i, :], A[2 * tt + i // 2][:, (i % 2) * SEQ:(i % 2) * SEQ + SEQ],
                                             ACT.Exp, bias=stat[:, 5, j:j + 1],
                                             accum_out=stat[:, 4, tt * NH + place(i):tt * NH + place(i) + 1]
                                             ).then_inc(S("xp"), 1)
                for tt in range(TT):
                    act_e.wait_ge(S("xpT"), TT * l + tt + 1)
                    for hp in range(2):
                        nc.scalar.activation(probT[:, tt, 2 * hp:2 * hp + 2, :].rearrange("p h m -> p (h m)"),
                                             A[2 * tt + hp][:], ACT.Copy).then_inc(S("xpT_out"), 1)
                act_e.wait_ge(S("xoT"), l + 1)
                nc.scalar.activation(oT_hi[:].rearrange("p c t -> p (c t)"), T[0][:], ACT.Copy).then_inc(S("oT_hi"), 1)
                ahead(base + XO0)
                if l:
                    break
                round_wide(hT_hi, gains(l, G_FFN), S("hT_hi"), S("xT"), 12 * l + 8)
                token_roots(l, FFN, xs)

                def ff_round(f):
                    act_e.wait_ge(S("ff_actT"), f + 1)
                    nc.scalar.activation(actT_hi[:].rearrange("p c t -> p (c t)"), T[0][:],
                                         ACT.Copy).then_inc(S("actT_hi"), 1)

                for f in range(NF):
                    if f:
                        ahead(FF_N0 + FFS * f + 1)
                        ff_round(f - 1)
                    else:
                        act_e.wait_ge(S("token_scale"), 4 * l + FFN + 1)
                    k = FF_N0 + FFS * f + 3 + 2 * (f == 0)
                    ahead(k)
                    for tt in range(TT):
                        if tt == 0:
                            act_e.wait_ge(half, half_no(0, 18 + f) + 1)
                        else:
                            act_e.wait_ge(used, k + 1)
                        if f:
                            act_e.wait_ge(S("ff_act"), 2 * f - 1 + tt)
                        scaled(silu[:, tt, :], G[tt][:, 0:FB], l, FFN, tt, ACT.Silu).then_inc(S("ff_silu"), 1)
                ff_round(NF - 1)

            for b in range(4):
                act_e.wait_ge(S("xT"), 12 * (DEPTH - 1) + 8 + b + 1)
                for kt in (2 * b, 2 * b + 1):
                    g = G_FFN + KT * (DEPTH - 1) + kt
                    ins = nc.scalar.activation(hT_f32[:, kt, :], TB[b][:, (kt % 2) * SEQ:(kt % 2) * SEQ + SEQ],
                                               ACT.Copy, scale=gcol[:, g:g + 1])
                ins.then_inc(S("rhT"), 1)
            token_roots(DEPTH - 1, FFN, xs)
            for tt in range(TT):
                act_e.wait_ge(S("xn"), tt + 1)
                nc.scalar.activation(xn_hi[:, tt, :], xn[:, tt, :], ACT.Copy).then_inc(S("xn_hi"), 1)
            act_e.wait_ge(S("gap"), 1)
            nc.scalar.activation(lg[:, 10, :, 0], lg[:, 10, :, 1], ACT.Exp).then_inc(S("gap_exp"), 1)
            lap0 = FF_LAP
            nxt[0] -= RING * lap0
            split_to(2 + LEAD, lap0)
            act_e.wait_ge(S("items"), 1)
            items = act_e.snap(NE + act_e.value_load(nit[0:1, 0:1], min_val=0, max_val=NE))

            def round_gathered(i, after=None):
                act_e.wait_ge(S("gathered"), i + 1)
                for j in range(2):
                    nc.scalar.activation(eT_hi[:, 4 * j:4 * j + 4, :].rearrange("p k s -> p (k s)"), A[2 + j][:],
                                         ACT.Copy).then_inc(S("eT_hi"), 1)

            def e_round(step):
                act_e.wait_ge(S("e_actT"), step + 1)
                nc.scalar.activation(actT_hi[:, :, 0:P], T[0][:, 0:2 * P].rearrange("p (c t) -> p c t", c=2),
                                     ACT.Copy).then_inc(S("e_aT_hi"), 1)

            def item(i, first=False, last=False):
                lap0 = FF_LAP + NF * i
                end = FFS * NF + (2 if last else LEAD)
                for f in range(NF):
                    step = NF * i + f
                    if not (first and f == 0):
                        split_to(FFS * f + 2 + LEAD, lap0)
                        e_round(step - 1)
                    k = FFS * f + 3 + 2 * (first and f == 0)
                    split_to(min(k + 1 + LEAD, end), lap0)
                    act_e.wait_ge(used, number(lap0, k) + 1)
                    if not (first and f == 0):
                        act_e.wait_ge(S("e_act"), step)
                    nc.scalar.activation(silu[:, 0, :], (G[0], G[1], T[1])[f % 3][:, 0:FB],
                                         ACT.Silu).then_inc(S("e_silu"), 1)
                    if f == 0 and not first:
                        for nb in range(2):
                            split_to(5 + nb + LEAD, lap0)
                            act_e.wait_ge(used, number(lap0, 4 + nb) + 1)
                            nc.scalar.activation(ye_hi[:, nb * 512:nb * 512 + 512], A[nb][:],
                                                 ACT.Copy).then_inc(S("ye_hi"), 1)
                    if f == 4:
                        act_e.wait_ge(S("selT"), i + 1)
                        nc.scalar.activation(selT[:], T[0][:, 2 * P:4 * P], ACT.Copy).then_inc(S("selT_out"), 1)
                if not last:
                    round_gathered(i + 1)

            round_gathered(0)
            item(0, first=True)
            nxt[0] = LEAD - 2
            with act_e.Fori(1, items - 1) as i:
                item(i)
            assert nxt[0] == LEAD - 2 + RING * NF
            nxt[0] = LEAD - 2
            last = act_e.snap(items - 1)
            item(last, last=True)
            e_round(last * NF + NF - 1)
            for nb in range(2):
                act_e.wait_ge(used, RING * FF_LAP + RING * NF * items + nb + 1)
                nc.scalar.activation(ye_hi[:, nb * 512:nb * 512 + 512], A[nb][:], ACT.Copy).then_inc(S("ye_hi"), 1)

        @block.vector
        def _(dve):
            v = nc.vector
            steps = [0]

            def link(ins):
                steps[0] += 1
                ins.then_inc(dve_step, 1)
                dve.wait_ge(dve_step, steps[0])

            nxt = [0]

            def split_to(k_end, lap0=0):
                while nxt[0] < k_end:
                    k = nxt[0]
                    dve.wait_ge(hi_ready, number(lap0, k) + 1)
                    v.tensor_tensor(w_lo[slot(k)][:], raw[slot(k)][:], w_hi[slot(k)][:].bitcast(F32),
                                    ALU.subtract).then_inc(lo_ready, 1)
                    nxt[0] += 1

            def ahead(k, lap0=0):
                split_to(k + RING, lap0)

            def power(dst, src, scale, eps=EPS):
                w = dst.shape[1]
                v.tensor_scalar(root[:, 0, 0:w], src, scale, eps, ALU.mult, ALU.add).then_inc(S("mean_square"), 1)
                roots[0] += 1
                dve.wait_ge(S("rooted"), roots[0])
                link(v.reciprocal(dst, root[:, 1, 0:w]))

            roots = [0]
            v.memset(eps_col[:], EPS).then_inc(S("eps_set"), 1)
            v.memset(half_pi[:], float(np.float32(np.pi / 2))).then_inc(S("eps_set"), 1)
            v.memset(one_col[:], 1.0).then_inc(S("eps_set"), 1)
            link(v.memset(root[:], 1.0))
            v.memset(vT[:, :, 0:CONV_W - 1], 0.0)

            def token_scale(l, norm):
                j = 4 * l + norm
                dve.wait_ge(S("rooted_tokens"), j + 1)
                v.reciprocal(rs[:, j, :], srt[:, j, :]).then_inc(S("token_scale"), 1)

            def rest_wide(dst, hi, gain, hi_done, count, done, banks=range(4)):
                for b in banks:
                    dve.wait_ge(hi_done, count + b + 1)
                    for kt in (2 * b, 2 * b + 1):
                        bank = TB[b][:, (kt % 2) * SEQ:(kt % 2) * SEQ + SEQ]
                        ins = v.scalar_tensor_tensor(out=dst[:, kt, :], in0=bank, scalar=gain[:, kt:kt + 1],
                                                     in1=hi[:, kt, :].bitcast(F32), op0=ALU.mult, op1=ALU.subtract)
                    ins.then_inc(done, 1)

            def gains(l, first):
                return gcol[:, first + KT * l:first + KT * l + KT]

            def flat(t):
                return t.rearrange("p c t -> p (c t)")

            def head_scale(src, square, row):
                link(v.tensor_tensor(square, src, src, ALU.mult))
                link(v.tensor_reduce(stat[:, row, :], square.rearrange("p (g d) -> p g d", d=HD), AX.X, ALU.add))
                power(stat[:, row + 1, :], stat[:, row, :], 1.0 / HD)

            def per_head(row):
                return stat[:, row, :].unsqueeze(2).to_broadcast([P, TT * NH, HD])

            heads = "p (g d) -> p g d"

            def turn_angles():
                dve.wait_ge(S("cols_out"), 1)
                for l in range(DEPTH):
                    v.scalar_tensor_tensor(out=gqk[:, l:l + 1], in0=gcol[:, G_QG + l:G_QG + l + 1], scalar=HD ** -0.5,
                                           in1=gcol[:, G_KG + l:G_KG + l + 1], op0=ALU.mult, op1=ALU.mult)
                dve.wait_ge(S("pos_in"), 16)
                dve.wait_ge(S("cst_in"), 16)
                link(v.tensor_copy(stat[:, 6, 0:TT], posi[:]))
                ang = tmp[:, 1].rearrange("p t c -> p (t c)")
                r, n2, a0 = ang[:, 0:64], ang[:, 128:192], ang[:, 192:256]
                for tt in range(TT):
                    link(v.tensor_scalar(a0[:, tt * 32:tt * 32 + 32], cst[:, C_FREQ:C_FREQ + 32], stat[:, 6, tt:tt + 1],
                                         None, ALU.mult))
                link(v.tensor_scalar(n2, a0, 1.0 / (2 * np.pi), ROUND, ALU.mult, ALU.add))
                link(v.tensor_scalar(n2, n2, -ROUND, None, ALU.add))
                link(v.scalar_tensor_tensor(out=r, in0=n2, scalar=-TWO_PI_1, in1=a0, op0=ALU.mult, op1=ALU.add))
                link(v.scalar_tensor_tensor(out=r, in0=n2, scalar=-TWO_PI_2, in1=r, op0=ALU.mult, op1=ALU.add))
                link(v.scalar_tensor_tensor(out=r, in0=n2, scalar=-TWO_PI_3, in1=r, op0=ALU.mult, op1=ALU.add))
                v.tensor_scalar(r, r, 3.1415925, -3.1415925, ALU.min, ALU.max).then_inc(S("angles"), 1)

            for l in range(DEPTH):
                base = LAYER0[l]
                if l == 0:
                    dve.wait_ge(S("gmix_out"), 1)
                mix_gain = gmix[:, KT * l:KT * l + KT]
                rest_wide(hT_lo, hT_hi, mix_gain, S("hT_hi"), 12 * l, S("hT_lo"), (0, 1))
                if l == 0:
                    split_to(2)
                rest_wide(hT_lo, hT_hi, mix_gain, S("hT_hi"), 12 * l, S("hT_lo"), (2, 3))
                if l == 0:
                    split_to(3)
                token_scale(l, MIX)
                if l == 0:
                    ahead(base + 5)
                    turn_angles()
                ahead(base + 11)
                dve.wait_ge(S("emptied"), 2 * unit_no(l, 2) + 2)
                v.tensor_tensor(convn[:], U[0][:, :, 0:DB], U[0][:, :, DB:], ALU.mult).then_inc(S("conv_v"), 1)
                ahead(base + 15)
                dve.wait_ge(S("sb_z"), l + 1)
                m2 = mask.unsqueeze(1).to_broadcast([P, 2, SEQ])
                m4 = mask.unsqueeze(1).to_broadcast([P, NH, SEQ])
                m4s = mask[:, 0:P].unsqueeze(1).to_broadcast([P, NH, P])

                def near(t):
                    return t[:, 0:NH * SEQ].rearrange("p (h q) -> p h q", h=NH)

                def far(t):
                    return t[:, NH * SEQ:].rearrange("p (h q) -> p h q", h=NH)

                for j in range(2):
                    v.tensor_tensor(near(zm)[:, 2 * j:2 * j + 2], A[1 + j][:].rearrange("p (h q) -> p h q", h=2), m2, ALU.mult)
                v.tensor_tensor(far(zm), A[3][:].rearrange("p (h q) -> p h q", h=NH), m4s, ALU.mult).then_inc(S("sb_zm"), 1)
                dve.wait_ge(S("yT_hi1"), l + 1)
                for c in range(KB):
                    ins = v.scalar_tensor_tensor(out=yT[1][1][:, c, :], in0=T[0][:, c * SEQ:c * SEQ + SEQ],
                                                 scalar=gcol[:, G_PS + 2 * l + c:G_PS + 2 * l + c + 1],
                                                 in1=yT[1][0][:, c, :].bitcast(F32), op0=ALU.mult, op1=ALU.subtract)
                ins.then_inc(S("yT_lo1"), 1)
                dve.wait_ge(S("emptied"), 2 * unit_no(l, 3) + 2)
                if l == 0:
                    dve.wait_ge(S("trig"), 1)
                for tt in range(TT):
                    qk = U[3][:, tt, :].rearrange("p (h two d) -> p h two d", two=2, d=HD // 2)
                    x1, x2 = qk[:, :, 0, :], qk[:, :, 1, :]
                    cos = trig[:, 0, tt, :].unsqueeze(1).to_broadcast([P, 2 * NH, HD // 2])
                    sin = trig[:, 1, tt, :].unsqueeze(1).to_broadcast([P, 2 * NH, HD // 2])
                    t1 = tmp[:, 0, tt, :].rearrange("p (h d) -> p h d", d=HD // 2)
                    t2 = tmp[:, 1, tt, :].rearrange("p (h d) -> p h d", d=HD // 2)
                    v.tensor_tensor(t1, x1, sin, ALU.mult)
                    link(v.tensor_tensor(t2, x2, sin, ALU.mult))
                    v.tensor_tensor(x1, x1, cos, ALU.mult)
                    link(v.tensor_tensor(x2, x2, cos, ALU.mult))
                    v.tensor_tensor(x1, x1, t2, ALU.subtract)
                    ins = v.tensor_tensor(x2, x2, t1, ALU.add)
                ins.then_inc(S("rotated"), 1)
                ahead(base + 19)
                dve.wait_ge(S("sb_l"), l + 1)
                link(v.scalar_tensor_tensor(out=zs, in0=zm, scalar=0.0, in1=zs, op0=ALU.max, op1=ALU.add))
                v.tensor_tensor(near(zs), near(zs), m4, ALU.mult)
                v.tensor_tensor(far(zs), far(zs), m4s, ALU.mult).then_inc(S("sb_sp"), 1)

                dve.wait_ge(S("vT_out"), l + 1)
                taps = [0]

                def conv_taps(count):
                    for w in range(taps[0], min(taps[0] + count, CONV_W)):
                        for c in range(KB):
                            tap = cwcol[:, (l * CONV_W + w) * KB + c:(l * CONV_W + w) * KB + c + 1]
                            src = vT[:, c, w:w + SEQ]
                            if w == 0:
                                bias = gcol[:, G_CB + 2 * l + c:G_CB + 2 * l + c + 1]
                                ins = v.tensor_scalar(conv[:, c, :], src, tap, bias, ALU.mult, ALU.add)
                            else:
                                dve.wait_ge(S("tap"), KB * CONV_W * l + KB * (w - 1) + c + 1)
                                ins = v.scalar_tensor_tensor(out=conv[:, c, :], in0=src, scalar=tap, in1=conv[:, c, :],
                                                             op0=ALU.mult, op1=ALU.add)
                            ins.then_inc(S("tap"), 1)
                    taps[0] = min(taps[0] + count, CONV_W)

                ahead(base + GATE0 + 1)
                conv_taps(5)
                ahead(base + GATE0 + 3)
                dve.wait_ge(S("sb_tail"), l + 1)
                for j in range(3):
                    ins = v.tensor_tensor(zm[:, 512 * j:512 * j + 512], zm[:, 512 * j:512 * j + 512], A[1 + j][:], ALU.subtract)
                ins.then_inc(S("sb_w"), 1)
                conv_taps(3)
                ahead(base + GATE0 + 5)
                conv_taps(4)
                ahead(base + GATE0 + 7)
                dve.wait_ge(S("sb_exp"), l + 1)
                v.tensor_tensor(near(zm), near(zm), m4, ALU.mult)
                v.tensor_tensor(far(zm), far(zm), m4s, ALU.mult).then_inc(S("sb_a"), 1)
                for g in range(4, 7):
                    conv_taps(4)
                    ahead(base + GATE0 + g)
                ahead(base + GATE0 + 15)
                dve.wait_ge(S("ret_z"), l + 1)
                for j in range(2):
                    v.tensor_tensor(near(zs)[:, 2 * j:2 * j + 2], A[1 + j][:].rearrange("p (h q) -> p h q", h=2),
                                    decay[:, 2 * j:2 * j + 2, :], ALU.mult)
                v.tensor_tensor(far(zs), A[3][:].rearrange("p (h q) -> p h q", h=NH), decay[:, :, 0:P],
                                ALU.mult).then_inc(S("ret_a"), 1)
                dve.wait_ge(S("yT_hi2"), l + 1)
                v.tensor_tensor(flat(yT[2][1][:]), A[0][:], flat(yT[2][0][:]).bitcast(F32),
                                ALU.subtract).then_inc(S("yT_lo2"), 1)
                ahead(base + GATE0 + 17)
                conv_taps(4)
                ahead(base + GATE0 + 19)
                conv_taps(CONV_W)

                def centre(bank, groups, width, dst, square, row):
                    src = bank[:].rearrange("p (g d) -> p g d", d=width)
                    to = dst.rearrange("p (g d) -> p g d", d=width)
                    link(v.tensor_reduce(stat[:, row, 0:groups], src, AX.X, ALU.add))
                    link(v.tensor_scalar(stat[:, row, 0:groups], stat[:, row, 0:groups], 1.0 / width, None, ALU.mult))
                    mean = stat[:, row, 0:groups].unsqueeze(2).to_broadcast([P, groups, width])
                    link(v.tensor_tensor(to, src, mean, ALU.subtract))
                    link(v.tensor_tensor(square, dst, dst, ALU.mult))
                    link(v.tensor_reduce(stat[:, row, 0:groups], square.rearrange("p (g d) -> p g d", d=width), AX.X,
                                         ALU.add))
                    power(stat[:, row + 1, 0:groups], stat[:, row, 0:groups], 1.0 / width)
                    return stat[:, row + 1, 0:groups].unsqueeze(2).to_broadcast([P, groups, width])

                ahead(base + GATE0 + 23)
                dve.wait_ge(S("ret_o"), l + 1)
                y, sq = (tmp[:, j].rearrange("p t c -> p (t c)") for j in range(2))
                inv = centre(T[1], TT * NH, HD, y, sq, 0)
                link(v.tensor_tensor(y.rearrange(heads, d=HD), y.rearrange(heads, d=HD), inv, ALU.mult))
                v.tensor_tensor(tmp[:, 0], tmp[:, 0], U[4][:, :, DB:], ALU.mult).then_inc(S("ret_y"), 1)
                ahead(base + GATE0 + 27)
                dve.wait_ge(S("conv_nat"), l + 1)
                cn = convn[:].rearrange("p t c -> p (t c)")
                inv = centre(T[0], TT, DB, cn, flat(dT[:]), 0)
                v.tensor_tensor(cn.rearrange("p (g d) -> p g d", d=DB), cn.rearrange("p (g d) -> p g d", d=DB), inv,
                                ALU.mult).then_inc(S("conv_ln"), 1)
                ahead(base + GATE0 + 31)
                dve.wait_ge(S("yT_hi3"), l + 1)
                v.tensor_tensor(flat(yT[3][1][:]), A[1][:], flat(yT[3][0][:]).bitcast(F32),
                                ALU.subtract).then_inc(S("yT_lo3"), 1)
                for i, b in enumerate(BR_ORDER):
                    if i == 1:
                        dve.wait_ge(S("yT_hi0"), l + 1)
                        v.tensor_tensor(flat(yT[0][1][:]), flat(conv[:]), flat(yT[0][0][:]).bitcast(F32),
                                        ALU.subtract).then_inc(S("yT_lo0"), 1)
                    for nb in range(2):
                        n = base + BR0 + 2 * i + nb
                        ahead(min(n, base + BR0 + 6))
                        for tt in range(TT):
                            if tt == 0:
                                dve.wait_ge(S("branch"), 2 * (4 * l + i) + nb + 1)
                            else:
                                dve.wait_ge(used, n + 1)
                            sl = slice(nb * 512, nb * 512 + 512)
                            dst = merged if i == 0 else gates[:, b]
                            v.tensor_tensor(dst[:, tt, sl], gates[:, b, tt, sl], (G, T)[nb][tt][:],
                                            ALU.mult).then_inc(S("prod"), 1)
                for b in range(4):
                    dve.wait_ge(S("gT_hi"), 4 * l + b + 1)
                    v.tensor_tensor(flat(hT_lo[:, 2 * b:2 * b + 2, :]), TB[b][:],
                                    flat(hT_hi[:, 2 * b:2 * b + 2, :]).bitcast(F32), ALU.subtract).then_inc(S("gT_lo"), 1)
                token_scale(l, MEM)
                for nb in range(2):
                    n = base + OUT0 + 4 * nb + 3
                    ahead(n)
                    for tt in range(TT):
                        if tt == 0:
                            dve.wait_ge(half, half_no(l, 13 + nb) + 1)
                        else:
                            dve.wait_ge(used, n + 1)
                        sl = slice(nb * 512, nb * 512 + 512)
                        v.tensor_tensor(xs[:, tt, sl], xs[:, tt, sl], G[tt][:], ALU.add).then_inc(S("out_added"), 1)
                    if nb == 0:
                        rest_wide(mT_lo, mT_hi, gains(l, G_MEM), S("mT_hi"), 4 * l, S("mT_lo"))
                rest_wide(hT_lo, hT_hi, gains(l, G_XA), S("hT_hi"), 12 * l + 4, S("hT_lo"))
                token_scale(l, XA)
                ahead(base + XK0 + 1)
                dve.wait_ge(S("emptied"), 2 * unit_no(l, 13) + 2)
                k_nat = convn[:].rearrange("p t c -> p (t c)")
                square = tmp[:, 1].rearrange("p t c -> p (t c)")
                head_scale(k_nat, square, 0)
                v.tensor_tensor(tmp[:, 0].rearrange("p t (h d) -> p (t h) d", d=HD), k_nat.rearrange(heads, d=HD),
                                per_head(1), ALU.mult).then_inc(S("mk_normed"), 1)
                ahead(base + XQ0 + 1)
                dve.wait_ge(S("emptied"), 2 * unit_no(l, 14) + 2)
                q_nat = qn[:].rearrange("p t c -> p (t c)")
                head_scale(q_nat, square, 0)
                v.tensor_tensor(q_nat.rearrange(heads, d=HD), q_nat.rearrange(heads, d=HD), per_head(1),
                                ALU.mult).then_inc(S("q_normed"), 1)
                ahead(base + XV0 + 1)
                for tt in range(TT):
                    dve.wait_ge(S("x_scores"), TT * l + tt + 1)
                    for hp in range(2):
                        j = tt * NH + 2 * hp
                        link(v.tensor_reduce(stat[:, 3, j:j + 2], A[2 * tt + hp][:].rearrange("p (h m) -> p h m", h=2), AX.X,
                                             ALU.max))
                    v.tensor_scalar(stat[:, 5, tt * NH:tt * NH + NH], stat[:, 3, tt * NH:tt * NH + NH], -1.0, None,
                                    ALU.mult).then_inc(S("xmax"), 1)
                dve.wait_ge(S("xp"), 8 * (l + 1))
                link(v.reciprocal(stat[:, 6, :], stat[:, 4, :]))
                dve.wait_ge(S("xo"), l + 1)
                v.tensor_tensor(on[:].rearrange("p t (h d) -> p (t h) d", d=HD), T[1][:].rearrange(heads, d=HD),
                                per_head(6), ALU.mult).then_inc(S("xo_normed"), 1)
                dve.wait_ge(S("oT_hi"), l + 1)
                v.tensor_tensor(flat(oT_lo[:]), T[0][:], flat(oT_hi[:]).bitcast(F32), ALU.subtract).then_inc(S("oT_lo"), 1)
                ahead(base + XO0)
                for nb in range(2):
                    for tt in range(TT):
                        if tt == 0:
                            dve.wait_ge(S("xproj"), 2 * l + nb + 1)
                        else:
                            dve.wait_ge(used, base + XO0 + nb + 1)
                        sl = slice(nb * 512, nb * 512 + 512)
                        v.tensor_tensor(xs[:, tt, sl], xs[:, tt, sl], (G, T)[nb][tt][:], ALU.add).then_inc(S("xo_added"), 1)
                if l:
                    token_scale(l, FFN)
                    dve.wait_ge(S("token_scale"), 4 * l + FFN + 1)
                    dve.wait_ge(S("grow_in"), 16)
                    for tt in range(TT):
                        v.scalar_tensor_tensor(out=xn[:, tt, :], in0=xs[:, tt, :], scalar=rs[:, 4 * l + FFN, tt:tt + 1],
                                               in1=merged[:, 0, :], op0=ALU.mult, op1=ALU.mult).then_inc(S("xn"), 1)
                    break
                rest_wide(hT_lo, hT_hi, gains(l, G_FFN), S("hT_hi"), 12 * l + 8, S("hT_lo"))
                token_scale(l, FFN)
                dve.wait_ge(S("token_scale"), 4 * l + FFN + 1)

                def ff_rest(f):
                    dve.wait_ge(S("actT_hi"), f + 1)
                    v.tensor_tensor(flat(actT_lo[:]), T[0][:], flat(actT_hi[:]).bitcast(F32),
                                    ALU.subtract).then_inc(S("actT_lo"), 1)

                for f in range(NF):
                    if f:
                        ahead(FF_N0 + FFS * f + 1)
                        ff_rest(f - 1)
                    ahead(FF_N0 + FFS * f + 3 + 2 * (f == 0))
                    for tt in range(TT):
                        dve.wait_ge(S("ff_silu"), 2 * f + tt + 1)
                        if f:
                            dve.wait_ge(S("ff_actT"), f)
                        v.scalar_tensor_tensor(out=act[:, tt, :], in0=G[tt][:, FB:], scalar=rs[:, 4 * l + FFN, tt:tt + 1],
                                               in1=silu[:, tt, :], op0=ALU.mult, op1=ALU.mult).then_inc(S("ff_act"), 1)
                ff_rest(NF - 1)
                for nb in range(2):
                    dve.wait_ge(used, FF_N0 + FFS * NF + nb + 1)
                    for tt in range(TT):
                        sl = slice(nb * 512, nb * 512 + 512)
                        v.tensor_tensor(xs[:, tt, sl], xs[:, tt, sl], A[2 * tt + nb][:], ALU.add).then_inc(S("ffn_added"), 1)

            dve.wait_ge(S("logits"), 1)
            for tt in range(TT):
                link(v.tensor_scalar(lg[:, 0, tt, :], T[0][:, tt * NE:tt * NE + NE], rs[:, 4 * (DEPTH - 1) + FFN, tt:tt + 1],
                                     None, ALU.mult))
            e8 = cst[:, C_E8:C_E8 + NE].unsqueeze(1).to_broadcast([P, TT, NE])

            def wide(t):
                return t.unsqueeze(2).to_broadcast([P, TT, NE])

            def first_of_max(src, top, onehot, scratch):
                link(v.tensor_reduce(lg[:, top, :, 0], src, AX.X, ALU.max))
                link(v.tensor_tensor(lg[:, scratch], src, wide(lg[:, top, :, 0]), ALU.is_equal))
                link(v.tensor_tensor(lg[:, scratch], lg[:, scratch], e8, ALU.mult))
                link(v.tensor_reduce(lg[:, 11, :, 0], lg[:, scratch], AX.X, ALU.max))
                link(v.tensor_tensor(lg[:, onehot], lg[:, scratch], wide(lg[:, 11, :, 0]), ALU.is_equal))

            first_of_max(lg[:, 0], 1, 2, 3)
            link(v.scalar_tensor_tensor(out=lg[:, 4], in0=lg[:, 2], scalar=NEG, in1=lg[:, 0], op0=ALU.mult, op1=ALU.add))
            first_of_max(lg[:, 4], 5, 7, 3)
            v.tensor_tensor(lg[:, 10, :, 1], lg[:, 5, :, 0], lg[:, 1, :, 0], ALU.subtract).then_inc(S("gap"), 1)
            v.tensor_tensor(lg[:, 6], lg[:, 2], lg[:, 7], ALU.add).then_inc(S("picked"), 1)
            for tt in range(TT):
                dve.wait_ge(S("xn_hi"), tt + 1)
                v.tensor_tensor(xn_lo[:, tt, :], xn[:, tt, :], xn_hi[:, tt, :].bitcast(F32),
                                ALU.subtract).then_inc(S("xn_lo"), 1)
            dve.wait_ge(S("gap_exp"), 1)
            link(v.tensor_scalar(lg[:, 8, :, 0], lg[:, 10, :, 0], 1.0, None, ALU.add))
            link(v.reciprocal(lg[:, 8, :, 1], lg[:, 8, :, 0]))
            link(v.tensor_tensor(lg[:, 8, :, 2], lg[:, 8, :, 1], lg[:, 10, :, 0], ALU.mult))
            link(v.tensor_tensor(lg[:, 2], lg[:, 2], wide(lg[:, 8, :, 1]), ALU.mult))
            link(v.tensor_tensor(lg[:, 7], lg[:, 7], wide(lg[:, 8, :, 2]), ALU.mult))
            for j in range(2):
                link(v.tensor_tensor(comb[:, :, j * NE:j * NE + NE], lg[:, 2], lg[:, 7], ALU.add))
            dve.wait_ge(S("counted"), 1)
            link(v.tensor_scalar(lg[:, 8].rearrange("p t e -> p (t e)"), T[1][:, 0:TT * NE], 1.0, None, ALU.add))
            link(v.tensor_tensor(lg[:, 8], lg[:, 8], lg[:, 6], ALU.mult))
            link(v.tensor_scalar(posm[:, :, 0:NE], lg[:, 8], -1.0, None, ALU.add))
            link(v.tensor_scalar(posm[:, :, NE:2 * NE], lg[:, 8], -1.0 - P, None, ALU.add))
            link(v.tensor_reduce(nitf[:, 0:1], T[1][:, 2 * NE:3 * NE], AX.X, ALU.max))
            link(v.tensor_scalar(nitf[:, 0:1], nitf[:, 0:1], float(P) + 0.5, float(NE), ALU.is_gt, ALU.mult))
            v.tensor_copy(nit[:, 0:1], nitf[:, 0:1]).then_inc(S("items"), 1)
            dve.wait_ge(S("items"), 1)
            items = dve.snap(NE + dve.value_load(nit[0:1, 0:1], min_val=0, max_val=NE))
            iota = cst[:, C_IOTA:C_IOTA + P]

            def select(i):
                for tt in range(TT):
                    ins = v.tensor_scalar(sel[:, tt, :], iota, posm[:, tt, bass.ds(i, 1)], None, ALU.is_equal)
                ins.then_inc(S("sel"), 1)

            def rest_gathered(i):
                for j in range(2):
                    dve.wait_ge(S("eT_hi"), 2 * i + j + 1)
                    part = slice(4 * j, 4 * j + 4)
                    v.tensor_tensor(eT_lo[:, part, :].rearrange("p k s -> p (k s)"), A[2 + j][:],
                                    eT_hi[:, part, :].rearrange("p k s -> p (k s)").bitcast(F32),
                                    ALU.subtract).then_inc(S("eT_lo"), 1)

            def e_rest(step):
                dve.wait_ge(S("e_aT_hi"), step + 1)
                v.tensor_tensor(actT_lo[:, :, 0:P], T[0][:, 0:2 * P].rearrange("p (c t) -> p c t", c=2),
                                actT_hi[:, :, 0:P].bitcast(F32), ALU.subtract).then_inc(S("e_aT_lo"), 1)

            def add_scattered(i, tt):
                dve.wait_ge(S("scat"), 2 * i + tt + 1)
                for nb in range(2):
                    sl = slice(nb * 512, nb * 512 + 512)
                    v.scalar_tensor_tensor(out=xs[:, tt, sl], in0=A[2 + nb][:], scalar=comb[:, tt, bass.ds(i, 1)],
                                           in1=xs[:, tt, sl], op0=ALU.mult, op1=ALU.add).then_inc(S("scattered"), 1)

            def rest_outputs(i, nb):
                dve.wait_ge(S("ye_hi"), 2 * i + nb + 1)
                sl = slice(nb * 512, nb * 512 + 512)
                v.tensor_tensor(ye_lo[:, sl], A[nb][:], ye_hi[:, sl].bitcast(F32), ALU.subtract).then_inc(S("ye_lo"), 1)

            def item(i, first=False, last=False):
                lap0 = FF_LAP + NF * i
                end = FFS * NF + (2 if last else LEAD)
                for f in range(NF):
                    step = NF * i + f
                    if not (first and f == 0):
                        split_to(FFS * f + 2 + LEAD, lap0)
                        e_rest(step - 1)
                    split_to(min(FFS * f + 4 + 2 * (first and f == 0) + LEAD, end), lap0)
                    dve.wait_ge(S("e_silu"), step + 1)
                    if not (first and f == 0):
                        dve.wait_ge(S("e_actT"), step)
                    v.tensor_tensor(act[:, 0, :], silu[:, 0, :], (G[0], G[1], T[1])[f % 3][:, FB:],
                                    ALU.mult).then_inc(S("e_act"), 1)
                    if f == 0 and not first:
                        for nb in range(2):
                            split_to(5 + nb + LEAD, lap0)
                            rest_outputs(i - 1, nb)
                    if f in (2, 3) and not first:
                        add_scattered(i - 1, f - 2)
                    if f == 5 and not last:
                        dve.wait_ge(S("gathered"), i + 1)
                        dve.wait_ge(S("selT"), i + 1)
                        select(i + 1)
                if not last:
                    rest_gathered(i + 1)

            select(0)
            nxt[0] -= RING * FF_LAP
            rest_gathered(0)
            item(0, first=True)
            nxt[0] = LEAD - 2
            with dve.Fori(1, items - 1) as i:
                item(i)
            assert nxt[0] == LEAD - 2 + RING * NF
            nxt[0] = LEAD - 2
            last = dve.snap(items - 1)
            item(last, last=True)
            e_rest(last * NF + NF - 1)
            for nb in range(2):
                rest_outputs(last, nb)
            for tt in range(TT):
                add_scattered(last, tt)


_INS = ["x", "mem", "positions", "norm_mix_g", "w_in", "conv_w", "conv_b", "conv_ln_g", "conv_ln_b", "pool_w",
        "pool_scale", "w_gate", "w_branch", "w_out", "norm_xa_g", "norm_mem_g", "xa_wq", "xa_wkv", "xa_q_norm_g",
        "xa_k_norm_g", "xa_wo", "norm_ffn_g", "ffn_w_gu", "ffn_w_down", "moe_router", "moe_w_gu", "moe_w_down"]


def kernel(**inputs):
    import concourse.bacc as bacc
    from concourse.bass_utils import run_bass_kernel_spmd

    nc = bacc.Bacc("TRN2", target_bir_lowering=False, num_devices=1)
    arrays = {"shape_constants": shape_constants()}
    arrays.update({name: np.ascontiguousarray(inputs[name]) for name in _INS})
    args = [nc.dram_tensor(f"in_{name}", a.shape, mybir.dt.from_np(a.dtype), kind="ExternalInput").ap()
            for name, a in arrays.items()]
    out = nc.dram_tensor("out_0", inputs["x"].shape, F32, kind="ExternalOutput").ap()
    trunk(nc, *args, out)
    r = run_bass_kernel_spmd(nc, [{f"in_{name}": a for name, a in arrays.items()}], core_ids=[0])
    return r.results[0]["out_0"]
```

```python
from contextlib import ExitStack

import numpy as np

import concourse.bass as bass
from concourse import mybir

F32 = mybir.dt.float32
F32R = mybir.dt.float32r
I32 = mybir.dt.int32
ALU = mybir.AluOpType
ACT = mybir.ActivationFunctionType
AX = mybir.AxisListType

P = 128
D = 1024
SEQ = 256
TT = SEQ // P
KT = D // P
DEPTH = 2
DB = D // 4
KB = DB // P
NH, HD = 4, 64
CONV_W = 31
WINDOWS = (2, 4, 8, 16)
D_FF = 2816
FB = 256
NF = D_FF // FB
NE = 8
EPS = 1e-6
CH = 1024
RING = 6
LEAD = 4
E_RING = 11
NEG = -3.0e38

IN0, GATE0, BR0, OUT0, XK0, XQ0, XV0, XO0, PER_LAYER = 0, 20, 52, 60, 68, 70, 72, 74, 76
FFS = 6
LAYER0 = [0, PER_LAYER + FFS * NF]
FF0 = [LAYER0[0] + PER_LAYER, LAYER0[1] + PER_LAYER]
FF_N0 = FF0[0] - 2
FF_LAP = FF0[1] // RING
assert RING == FFS and FF0[1] % RING == 2
E_LAPS = FFS * NF // E_RING
assert E_LAPS * E_RING == FFS * NF
IN_ORDER = (1, 2, 0, 3, 4)
BR_ORDER = (2, 1, 3, 0)

C_ID, C_TRIGE, C_TRILT, C_ONES, C_MASK = 0, 128, 256, 384, 512
C_DECAY = C_MASK + 256
C_BAND = C_DECAY + NH * 256
C_FREQ = C_BAND + 4 * 384
C_E8 = C_FREQ + 32
C_IOTA = C_E8 + 8
C_ALL = C_IOTA + 128


def shape_constants():
    c = np.zeros((P, C_ALL), np.float64)
    k, q = np.arange(P)[:, None], np.arange(P)[None, :]
    q2 = np.arange(SEQ)[None, :]
    c[:, C_ID:C_ID + P] = k == q
    c[:, C_TRIGE:C_TRIGE + P] = k >= q
    c[:, C_TRILT:C_TRILT + P] = k < q
    c[:, C_ONES:C_ONES + P] = 1
    c[:, C_MASK:C_MASK + SEQ] = k < q2
    for j, h in enumerate((0, 2, 1, 3)):
        gamma = np.float64(np.float32(1.0 - 2.0 ** (-5.0 - h)))
        c[:, C_DECAY + j * SEQ:C_DECAY + (j + 1) * SEQ] = np.where(
            q2 >= k, gamma ** np.maximum(q2 - k, 0), 0.0) * HD ** -0.5
    for g, w in enumerate(WINDOWS):
        band = np.where((q2 >= k) & (q2 - k < w), 1.0 / np.minimum(q2 + 1.0, w), 0.0) - (q2 == k)
        late = np.where((q >= k) & (q - k < w), 1.0 / w, 0.0) - (q == k)
        c[:, C_BAND + g * 384:C_BAND + g * 384 + 256] = band
        c[:, C_BAND + g * 384 + 256:C_BAND + (g + 1) * 384] = late
    c[:, C_FREQ:C_FREQ + 32] = 10000.0 ** (-np.arange(32) / 32)
    c[:, C_E8:C_E8 + 8] = 8 - np.arange(8)
    c[:, C_IOTA:C_IOTA + P] = q
    return c.astype(np.float32)


G_XA, G_FFN, G_MEM = 0, 16, 32
G_CB, G_LG, G_LB, G_PS = 48, 52, 56, 60
G_QG, G_KG = 64, 66
G_ROWS = 68

TWO_PI_1 = 6.28125
TWO_PI_2 = float(np.float32(np.round((2 * np.pi - TWO_PI_1) * 2 ** 20) / 2 ** 20))
TWO_PI_3 = float(np.float32(2 * np.pi - TWO_PI_1 - TWO_PI_2))
ROUND = 12582912.0


def trunk(nc, consts, x, mem, positions, norm_mix_g, w_in, conv_w, conv_b, conv_ln_g, conv_ln_b, pool_w,
          pool_scale, w_gate, w_branch, w_out, norm_xa_g, norm_mem_g, xa_wq, xa_wkv, xa_q_norm_g,
          xa_k_norm_g, xa_wo, norm_ffn_g, ffn_w_gu, ffn_w_down, moe_router, moe_w_gu, moe_w_down, out):
    ctx = ExitStack()
    with ctx:
        def sb(name, shape, dt=F32, stack=ctx):
            return stack.enter_context(nc.sbuf_tensor(name, shape, dt))

        def sem(name):
            return ctx.enter_context(nc.semaphore(name))

        raw = [sb(f"raw{j}", [P, CH]) for j in range(RING)]
        w_hi = [sb(f"w_hi{j}", [P, CH], F32R) for j in range(RING)]
        w_lo = [sb(f"w_lo{j}", [P, CH], F32R) for j in range(RING)]
        cst = sb("cst", [P, C_ALL])
        xs = sb("xs", [P, TT, D])
        xn = sb("xn", [P, TT, D])
        with ExitStack() as s:
            sb("merged_first", [P, D], F32, s)
            spare = [sb("spare0", [P, CH], F32, s)]
        merged = sb("merged", [P, TT, D])
        with ExitStack() as s:
            hT_f32 = sb("hT_f32", [P, KT, SEQ], F32, s)
        hT_hi = sb("hT_hi", [P, KT, SEQ], F32R)
        with ExitStack() as s:
            spare += [sb(f"spare{j}", [P, CH], F32, s) for j in (1, 2)]
        hT_lo = sb("hT_lo", [P, KT, SEQ], F32R)
        memk = sb("memk", [P, KB, SEQ])
        memv = sb("memv", [P, TT, DB])
        qT = sb("qT", [P, KB, SEQ])
        kT = sb("kT", [P, KB, SEQ])
        dT = sb("dT", [P, KB, SEQ])
        vT = sb("vT", [P, KB, CONV_W - 1 + SEQ])
        conv = sb("conv", [P, KB, SEQ])
        convn = sb("convn", [P, TT, DB])
        with ExitStack() as s:
            spare += [sb("spare3", [P, CH], F32, s)]
        tmp = sb("tmp", [P, 2, TT, DB])
        gmix = sb("gmix", [P, DEPTH * KT])
        gcol = sb("gcol", [P, G_ROWS])
        gqk = sb("gqk", [P, DEPTH])
        cwcol = sb("cwcol", [P, 2 * CONV_W * DEPTH])
        poolw = sb("poolw", [P, DEPTH, 2, 64])
        stat = sb("stat", [P, 8, 8])
        eps_col = sb("eps_col", [P, 1])
        half_pi = sb("half_pi", [P, 1])
        one_col = sb("one_col", [P, 1])
        unused = sb("unused", [P, 1])
        root = sb("root", [P, 2, 8])
        ssq = sb("ssq", [P, 4 * DEPTH, TT])
        half_ssq = sb("half_ssq", [P, 2, TT])
        srt = sb("srt", [P, 4 * DEPTH, TT])
        rs = sb("rs", [P, 4 * DEPTH, TT])
        rt = sb("rt", [P, KT, NE])
        posi = sb("posi", [P, TT], I32)
        trig = sb("trig", [P, 2, TT, 32])
        zm = xn[:].rearrange("p a b -> p (a b)")[:, 0:1536]
        zs = merged[:].rearrange("p a b -> p (a b)")[:, 0:1536]
        with ExitStack() as s:
            U = [sb(f"U{i}", [P, TT, 512], F32, s) for i in range(5)]
        with ExitStack() as s:
            yT = [[sb(f"yT{i}{part}", [P, KB, SEQ], F32R, s) for part in ("hi", "lo")] for i in range(4)]
        with ExitStack() as s:
            xn_hi = sb("xn_hi", [P, TT, D], F32R, s)
            xn_lo = sb("xn_lo", [P, TT, D], F32R, s)
            spare += [sb("spare4", [P, CH], F32, s)]
        e_raw = raw + spare
        sb("u_hold", [P, 5 * 1024])
        with ExitStack() as s:
            gates = sb("gates", [P, 4, TT, D], F32, s)
        with ExitStack() as s:
            qn = sb("qn", [P, TT, DB], F32, s)
            on = sb("on", [P, TT, DB], F32, s)
            oT_hi = sb("oT_hi", [P, KB, SEQ], F32R, s)
            oT_lo = sb("oT_lo", [P, KB, SEQ], F32R, s)
            mT_hi = sb("mT_hi", [P, KT, SEQ], F32R, s)
            memn = sb("memn", [P, TT, D], F32, s)
            mT_lo = sb("mT_lo", [P, KT, SEQ], F32R, s)
        with ExitStack() as s:
            sb("q_on_oT", [P, TT * D], F32, s)
            probT = sb("probT", [P, TT, NH, SEQ], F32, s)
            prob = sb("prob", [P, TT, NH, SEQ], F32, s)
        with ExitStack() as s:
            silu = sb("silu", [P, TT, FB], F32, s)
            act = sb("act", [P, TT, FB], F32, s)
            actT_hi = sb("actT_hi", [P, 2, SEQ], F32R, s)
            actT_lo = sb("actT_lo", [P, 2, SEQ], F32R, s)
            eT_hi = sb("eT_hi", [P, KT, P], F32R, s)
            eT_lo = sb("eT_lo", [P, KT, P], F32R, s)
            ye_hi = sb("ye_hi", [P, D], F32R, s)
            ye_lo = sb("ye_lo", [P, D], F32R, s)
            sel = sb("sel", [P, TT, P], F32R, s)
            selT = sb("selT", [P, SEQ], F32R, s)
            lg = sb("lg", [P, 12, TT, NE], F32, s)
            posm = sb("posm", [P, TT, 2 * NE], F32, s)
            comb = sb("comb", [P, TT, 2 * NE], F32, s)
            more_items = sb("more_items", [P, 2], I32, s)
            more_items_f32 = sb("more_items_f32", [P, 2], F32, s)
        sb("region_hold", [P, 4 * TT * D])
        rows_g, rows_c, rows_m = (tmp[:].rearrange("p a t c -> p (a t c)")[:, 128 * j:128 * j + 128] for j in range(3))

        ident = cst[:, C_ID:C_ID + P]
        tri_ge = cst[:, C_TRIGE:C_TRIGE + P]
        tri_lt = cst[:, C_TRILT:C_TRILT + P]
        ones = cst[:, C_ONES:C_ONES + P]
        mask = cst[:, C_MASK:C_MASK + SEQ]
        decay = cst[:, C_DECAY:C_DECAY + NH * SEQ].rearrange("p (h q) -> p h q", h=NH)

        A = [ctx.enter_context(nc.psum_tensor(f"A{i}", [P, 512], F32)) for i in range(4)]
        G = [ctx.enter_context(nc.psum_tensor(f"G{i}", [P, 512], F32)) for i in range(2)]
        T = [ctx.enter_context(nc.psum_tensor(f"T{i}", [P, 512], F32)) for i in range(2)]
        TB = [A[0], A[2], A[1], A[3]]

        landed = [sem(f"landed{j}") for j in range(RING)]
        landed_spare = [sem(f"landed_spare{j}") for j in range(E_RING - RING)]
        hi_ready = sem("hi_ready")
        lo_ready = sem("lo_ready")
        used = sem("used")
        half = sem("half")
        act_step = sem("act_step")
        dve_step = sem("dve_step")
        names = {}

        def S(name):
            if name not in names:
                names[name] = sem(name)
            return names[name]

        def slot(k):
            return k % RING

        def number(lap0, k):
            return lap0 * RING + k

        def landing(lap0, k, item=None):
            if item is None:
                return raw[slot(k)], landed[slot(k)], 32 * (lap0 + k // RING + 1)
            j, lap = k % E_RING, k // E_RING
            if j < RING:
                return e_raw[j], landed[j], 32 * (E_LAPS * item + FF_LAP + lap + 1)
            return e_raw[j], landed_spare[j - RING], 32 * (E_LAPS * item + lap + 1)

        MIX, MEM, XA, FFN = range(4)

        def unit_no(l, u):
            return 16 * l + u

        def place(h):
            return (h % 2) * 2 + h // 2

        def half_no(l, j):
            return l * (18 + NF) + j

        block = ctx.enter_context(nc.Block())

        @block.sync
        def _(sp):
            sp.dma_start(cst[:, 0:P], consts[:, 0:P]).then_inc(S("ident_in"), 16)
            sp.dma_start(rows_m[0:DEPTH * KT, :], norm_mix_g.rearrange("l (k p) -> (l k) p", p=P)).then_inc(S("mix_in"), 16)
            x_tiles = x[0].rearrange("(t p) d -> p t d", p=P)

            def load_x(nb):
                sl = slice(nb * 512, nb * 512 + 512)
                sp.dma_start(xs[:, :, sl], x_tiles[:, :, sl]).then_inc(S(f"x_in{nb}"), 16)

            load_x(0)

            def load(lap0, k, view, src, item=None):
                buffer, signal, _ = landing(lap0, k, item)
                if isinstance(item, int) and RING <= k < E_RING:
                    sp.wait_ge(S("xqT"), DEPTH)
                elif item is not None and not (isinstance(item, int) and k < RING):
                    sp.wait_ge(lo_ready, number(lap0, k) - E_RING + 1)
                elif number(lap0, k) >= RING:
                    sp.wait_ge(lo_ready, number(lap0, k) - RING + 1)
                if not isinstance(lap0, int):
                    sp.sem_inc(S("asked"), 1)
                for dst, part in halves(view(buffer[:]), src):
                    sp.dma_start(dst, part).then_inc(signal, 16)

            def halves(dst, src):
                k = src.shape[1] // 2
                return [(dst[:, 0:k], src[:, 0:k]), (dst[:, k:], src[:, k:])]

            def rows2(r):
                return r.rearrange("p (k n) -> p k n", k=2)

            def rows4(r):
                return r.rearrange("p (k n) -> p k n", k=4)

            def pairs(r):
                return r.rearrange("p (k t c) -> p k t c", k=2, t=2)

            def block_of(n, w, col0, chunks=range(4)):
                for c in chunks:
                    load(0, n + c, rows2, w[:, 2 * c:2 * c + 2, col0:col0 + 512])

            def both_halves(lap0, k, w, item=None):
                for nb in range(2):
                    load(lap0, k + nb, rows2, w[:, :, nb * 512:nb * 512 + 512], item)

            def stream_ff(gu, down, lap0, first, prev, n0=0, item=None):
                for f in range(NF):
                    k = n0 + FFS * f
                    for c in range(4):
                        load(lap0, k + c + 2 * (first and f == 0), pairs, gu[:, 2 * c:2 * c + 2, :, f], item)
                    if f:
                        both_halves(lap0, k + 4, down[:, 2 * f - 2:2 * f], item)
                    elif not first:
                        both_halves(lap0, k + 4, prev[:, 2 * NF - 2:2 * NF], item)

            for l in range(DEPTH):
                base = LAYER0[l]
                wi = w_in[l].rearrange("(k p) n -> p k n", p=P)
                for i, b in enumerate(IN_ORDER):
                    block_of(base + IN0 + 4 * i, wi, b * 512, (0, 1))
                    if l + i == 0:
                        load_x(1)
                    block_of(base + IN0 + 4 * i, wi, b * 512, (2, 3))
                    if l == 0 and i == 1:
                        sp.dma_start(cst[:, P:], consts[:, P:]).then_inc(S("cst_in"), 16)
                for g in range(8):
                    wg = w_gate[l, g // 2].rearrange("(k p) n -> p k n", p=P)
                    block_of(base + GATE0 + 4 * g, wg, (g % 2) * 512)
                for i, b in enumerate(BR_ORDER):
                    both_halves(0, base + BR0 + 2 * i, w_branch[l, b].rearrange("(k p) n -> p k n", p=P))
                wo = w_out[l].rearrange("(k p) n -> p k n", p=P)
                for nb in range(2):
                    block_of(base + OUT0 + 4 * nb, wo, nb * 512)
                    if nb == 0:
                        sp.wait_ge(S("prod"), 16 * l + 4)
                        sp.dma_start(memn[:], mem[0].rearrange("(t p) d -> p t d", p=P)).then_inc(S("mem_in"), 16)
                wq = xa_wq[l].rearrange("(k p) n -> p k n", p=P)
                wkv = xa_wkv[l].rearrange("(k p) n -> p k n", p=P)
                for n, w in ((XK0, wkv[:, :, 0:DB]), (XQ0, wq), (XV0, wkv[:, :, DB:])):
                    for c in range(2):
                        load(0, base + n + c, rows4, w[:, 4 * c:4 * c + 4])
                both_halves(0, base + XO0, xa_wo[l].rearrange("(k p) n -> p k n", p=P))
                if l == 0:
                    gu = ffn_w_gu[0].rearrange("(k p) (t f c) -> p k t f c", p=P, t=2, c=FB)
                    down = ffn_w_down[0].rearrange("(k p) n -> p k n", p=P)
                    stream_ff(gu, down, 0, True, None, FF_N0)
                    both_halves(0, FF_N0 + FFS * NF, down[:, 2 * NF - 2:2 * NF])
            gu_e = moe_w_gu[0].rearrange("e (k p) (t f c) -> e p k t f c", p=P, t=2, c=FB)
            dn_e = moe_w_down[0].rearrange("e (k p) n -> e p k n", p=P)
            stream_ff(gu_e[0], dn_e[0], FF_LAP, True, None, item=0)
            sp.wait_ge(S("items"), 1)
            items = sp.snap(NE + sp.value_load(more_items[0:1, 0:1], min_val=0, max_val=NE))
            with sp.Fori(1, items) as i:
                e = sp.snap(i & (NE - 1))
                p = sp.snap((i + (NE - 1)) & (NE - 1))
                stream_ff(gu_e[bass.ds(e, 1)].rearrange("a p k t f c -> (a p) k t f c"),
                          dn_e[bass.ds(e, 1)].rearrange("a p k n -> (a p) k n"),
                          FF_LAP + NF * i, False,
                          dn_e[bass.ds(p, 1)].rearrange("a p k n -> (a p) k n"), item=i)
            both_halves(FF_LAP + NF * items, 0, dn_e[NE - 1, :, 2 * NF - 2:2 * NF], item=items)
            for nb in range(2):
                sl = slice(nb * 512, nb * 512 + 512)
                for tt in range(TT):
                    sp.wait_ge(S("last_added"), 2 * nb + tt + 1)
                    sp.dma_start(out[0].rearrange("(t p) d -> p t d", p=P)[:, tt, sl], xs[:, tt, sl]).then_inc(S("stored"), 16)
            sp.wait_ge(S("stored"), 16 * 4)

        @block.gpsimd
        def _(pool):
            for base, src in ((G_XA, norm_xa_g), (G_FFN, norm_ffn_g), (G_MEM, norm_mem_g)):
                pool.dma_start(rows_g[base:base + DEPTH * KT, :],
                               src.rearrange("l (k p) -> (l k) p", p=P)).then_inc(S("rows_in"), 16)
            for base, src in ((G_CB, conv_b), (G_LG, conv_ln_g), (G_LB, conv_ln_b), (G_PS, pool_scale)):
                pool.dma_start(rows_g[base:base + 2 * DEPTH, :],
                               src.rearrange("l (k p) -> (l k) p", p=P)).then_inc(S("rows_in"), 16)
            for base, src in ((G_QG, xa_q_norm_g), (G_KG, xa_k_norm_g)):
                for j in range(2):
                    pool.dma_start(rows_g[base:base + DEPTH, 64 * j:64 * j + 64], src).then_inc(S("rows_in"), 16)
            pool.dma_start(rows_c[0:2 * CONV_W * DEPTH, :],
                           conv_w.rearrange("l w (k p) -> (l w k) p", p=P)).then_inc(S("rows_in"), 16)
            for l in range(DEPTH):
                for j in range(2):
                    pool.dma_start(poolw[64 * j:64 * j + 64, l],
                                   pool_w[l].rearrange("(g j) c d -> j c g d", j=2)[j]).then_inc(S("poolw_in"), 16)
            pool.dma_start(posi[:], positions[0].rearrange("(t p) -> p t", p=P),
                           allow_slow_non_contiguous=True).then_inc(S("pos_in"), 16)
            pool.dma_start(rt[:], moe_router[0].rearrange("(k p) e -> p k e", p=P)).then_inc(S("rt_in"), 16)
            for l in range(DEPTH):
                for i in range(1, 3):
                    for nb in range(2):
                        for tt in range(TT):
                            step = 16 * l + 4 * i + 2 * nb + tt
                            pool.wait_ge(S("prod"), step + 1)
                            if i > 1:
                                pool.wait_ge(S("summed"), 8 * l + 4 * (i - 2) + 2 * nb + tt + 1)
                            b = BR_ORDER[i]
                            sl = slice(nb * 512, nb * 512 + 512)
                            pool.tensor_tensor(merged[:, tt, sl], merged[:, tt, sl], gates[:, b, tt, sl],
                                               ALU.add).then_inc(S("summed"), 1)
            pool.wait_ge(S("mergedT"), 4 * DEPTH)
            pool.dma_start(merged[:, 0, :], norm_ffn_g[DEPTH - 1:DEPTH, :].to_broadcast([P, D])).then_inc(S("grow_in"), 16)
            pool.wait_ge(S("xn_hi"), 1)
            pool.tensor_tensor(xn_lo[:, 0, :], xn[:, 0, :], xn_hi[:, 0, :].bitcast(F32), ALU.subtract).then_inc(S("xn_lo0"), 1)

        @block.tensor
        def _(pe):
            def product(dst, a_hi, a_lo, b_hi, b_lo, first, last):
                pe.matmul(dst, a_hi, b_hi, start=first, stop=False)
                pe.matmul(dst, a_lo, b_hi, start=False, stop=False)
                return pe.matmul(dst, a_hi, b_lo, start=False, stop=last)

            def have(lap0, k):
                pe.wait_ge(lo_ready, number(lap0, k) + 1)

            def streamed(n0, hi, lo, free, before=None, banks=G, nchunks=4, kts=2, width=512):
                for c in range(nchunks):
                    n = n0 + c
                    if before:
                        before(c)
                    have(0, n)
                    wh = w_hi[slot(n)][:].rearrange("p (k n) -> p k n", k=kts)
                    wl = w_lo[slot(n)][:].rearrange("p (k n) -> p k n", k=kts)
                    for tt in range(TT):
                        if c == 0 and free[tt]:
                            pe.wait_ge(*free[tt])
                        for k in range(kts):
                            kk = c * kts + k
                            mm = product(banks[tt][:, 0:width], hi[:, kk, tt * P:tt * P + P],
                                         lo[:, kk, tt * P:tt * P + P], wh[:, k, :], wl[:, k, :],
                                         kk == 0, kk == nchunks * kts - 1)
                        if tt == 0 and c == nchunks - 1:
                            mm.then_inc(half, 1)
                    mm.then_inc(used, 1)

            def turn(src, banks, done):
                for b in banks:
                    for kt in (2 * b, 2 * b + 1):
                        for tt in range(TT):
                            mm = pe.transpose(TB[b][:, (kt % 2) * 256 + tt * P:(kt % 2) * 256 + tt * P + P],
                                              src[:, tt, kt * P:kt * P + P], ident)
                    mm.then_inc(done, 1)

            def parts(name, count):
                pe.wait_ge(S(name + "_hi"), count)
                pe.wait_ge(S(name + "_lo"), count)

            def keep_warm(bank, times):
                for _ in range(times):
                    pe.matmul(bank[:], w_hi[2][:, 0:P], w_hi[2][:, 0:512], start=True, stop=True)

            def transpose_narrow(dst, src):
                for c in range(KB):
                    for tt in range(TT):
                        mm = pe.transpose(dst[:, c * SEQ + tt * P:c * SEQ + tt * P + P],
                                          src(tt, slice(c * P, c * P + P)), ident)
                return mm

            def scores(q, k, done):
                for h in range(NH):
                    r = slice((h % 2) * HD, (h % 2) * HD + HD)
                    pe.matmul(A[1 + h % 2][:, (h // 2) * SEQ:(h // 2) * SEQ + SEQ], k[r, h // 2, 0:P], q[r, h // 2, :],
                              start=True, stop=True)
                for h in (0, 2, 1, 3):
                    r = slice((h % 2) * HD, (h % 2) * HD + HD)
                    j = place(h)
                    mm = pe.matmul(A[3][:, j * P:j * P + P], k[r, h // 2, P:SEQ], q[r, h // 2, P:SEQ],
                                   start=True, stop=True)
                    if h == 2:
                        rows[0] += 1
                        mm.then_inc(S("even_heads"), 1)
                        pe.wait_ge(S("even_heads"), rows[0])
                mm.then_inc(done, 1)

            rows = [0]

            pe.wait_ge(S("ident_in"), 16)
            pe.wait_ge(S("mix_in"), 16)
            pe.transpose(T[0][:, 0:DEPTH * KT], rows_m[0:DEPTH * KT, :],
                         ident[0:DEPTH * KT, 0:DEPTH * KT]).then_inc(S("mix_cols"), 1)

            def after_unit(l, u):
                n = unit_no(l, u)
                return [(S("emptied"), 2 * n - 1), (S("emptied"), 2 * n)]

            for l in range(DEPTH):
                base = LAYER0[l]
                def second_half(c):
                    if c == 1:
                        if l == 0:
                            pe.wait_ge(S("x_in1"), 16)
                        else:
                            pe.wait_ge(S("ffn_added"), 4)
                        turn(xs, (2, 3), S("xT"))
                    parts("hT", 12 * l + c + 1)

                if l == 0:
                    pe.wait_ge(S("x_in0"), 16)
                    turn(xs, (0, 1), S("xT"))
                    free0 = [None, None]
                else:
                    free0 = [(S("ff_act"), 2 * NF - 1), (S("ff_act"), 2 * NF)]
                streamed(base + IN0, hT_hi, hT_lo, free0, second_half)
                if l == 0:
                    pe.wait_ge(S("rows_in"), 16 * 12)
                    pe.transpose(T[1][:, 0:G_ROWS], rows_g[0:G_ROWS, :], ident[0:G_ROWS, 0:G_ROWS])
                    pe.transpose(T[1][:, 128:128 + 2 * CONV_W * DEPTH], rows_c[0:2 * CONV_W * DEPTH, :],
                                 ident[0:2 * CONV_W * DEPTH, 0:2 * CONV_W * DEPTH]).then_inc(S("cols"), 1)
                streamed(base + IN0 + 4, hT_hi, hT_lo, after_unit(l, 1))
                streamed(base + IN0 + 8, hT_hi, hT_lo, after_unit(l, 2))
                pe.wait_ge(S("emptied"), 2 * unit_no(l, 2))
                if l == 0:
                    pe.wait_ge(S("cols_out"), 1)
                else:
                    pe.wait_ge(S("actT_hi"), NF)
                    pe.wait_ge(S("actT_lo"), NF)
                transpose_narrow(T[0][:], lambda tt, c: U[1][:, tt, 256 + c.start:256 + c.stop])
                transpose_narrow(T[1][:], lambda tt, c: U[2][:, tt, c]).then_inc(S("sb_qk"), 1)
                if l == 0:
                    pe.wait_ge(S("cst_in"), 16)
                for g in range(4):
                    o = A[0][(g % 2) * 64:(g % 2) * 64 + 64, (g // 2) * SEQ:(g // 2) * SEQ + SEQ]
                    c0 = C_BAND + g * 384
                    pe.matmul(o, U[1][:, 0, g * 64:g * 64 + 64], cst[:, c0:c0 + 256], start=True, stop=False)
                    mm = pe.matmul(A[0][(g % 2) * 64:(g % 2) * 64 + 64, (g // 2) * SEQ + P:(g // 2) * SEQ + SEQ],
                                   U[1][:, 1, g * 64:g * 64 + 64], cst[:, c0 + 256:c0 + 384], start=False, stop=True)
                mm.then_inc(S("pool_d"), 1)
                streamed(base + IN0 + 12, hT_hi, hT_lo, after_unit(l, 3))
                pe.wait_ge(S("sb_qk_out"), l + 1)
                scores(qT, kT, S("sb_z"))
                pe.wait_ge(S("dT_out"), l + 1)
                if l == 0:
                    pe.wait_ge(S("poolw_in"), 16 * 4)
                for g in range(4):
                    r = slice((g % 2) * 64, (g % 2) * 64 + 64)
                    mm = pe.matmul(T[0][r, (g // 2) * SEQ:(g // 2) * SEQ + SEQ], poolw[r, l, g // 2, :], dT[r, g // 2, :],
                                   start=True, stop=True)
                mm.then_inc(S("pool_y"), 1)
                streamed(base + IN0 + 16, hT_hi, hT_lo, after_unit(l, 4))
                pe.wait_ge(S("conv_v"), l + 1)
                transpose_narrow(T[1][:], lambda tt, c: convn[:, tt, c]).then_inc(S("conv_vT"), 1)

                def gate(g):
                    streamed(base + GATE0 + 4 * g, hT_hi, hT_lo, after_unit(l, 5 + g))

                gate(0)
                pe.wait_ge(S("sb_sp"), l + 1)
                for j in range(NH):
                    zk0 = zs[:, j * SEQ:j * SEQ + SEQ]
                    zk1 = zs[:, NH * SEQ + j * P:NH * SEQ + j * P + P]
                    o = A[1 + j // 2]
                    pe.matmul(o[:, (j % 2) * SEQ:(j % 2) * SEQ + SEQ], tri_ge, zk0, start=True, stop=False)
                    pe.matmul(o[:, (j % 2) * SEQ + P:(j % 2) * SEQ + SEQ], ones, zk1, start=False, stop=True)
                mm = pe.matmul(A[3][:], tri_ge, zs[:, NH * SEQ:NH * SEQ + NH * P], start=True, stop=True)
                mm.then_inc(S("sb_tail"), 1)
                gate(1)
                pe.wait_ge(S("rotated"), l + 1)
                pe.wait_ge(S("yT_lo1"), l + 1)
                pe.wait_ge(S("vT_out"), l + 1)
                transpose_narrow(T[0][:], lambda tt, c: U[3][:, tt, c])
                transpose_narrow(T[1][:], lambda tt, c: U[3][:, tt, 256 + c.start:256 + c.stop]).then_inc(S("ret_qk"), 1)
                gate(2)
                pe.wait_ge(S("sb_a"), l + 1)
                for h in (0, 2, 1, 3):
                    r = slice((h % 2) * HD, (h % 2) * HD + HD)
                    c0 = (h // 2) * SEQ
                    pe.matmul(A[0][r, c0:c0 + SEQ], U[2][:, 0, 256 + h * HD:256 + h * HD + HD],
                              zm[:, place(h) * SEQ:place(h) * SEQ + SEQ], start=True, stop=False)
                    mm = pe.matmul(A[0][r, c0 + P:c0 + SEQ], U[2][:, 1, 256 + h * HD:256 + h * HD + HD],
                                   zm[:, NH * SEQ + place(h) * P:NH * SEQ + place(h) * P + P], start=False, stop=True)
                mm.then_inc(S("sb_y"), 1)
                gate(3)
                pe.wait_ge(S("ret_qk_out"), l + 1)
                pe.wait_ge(S("sb_w"), l + 1)
                scores(qT, kT, S("ret_z"))
                gate(4)
                pe.wait_ge(S("ret_a"), l + 1)
                for tt in range(TT):
                    for h in range(NH):
                        o = T[1][:, tt * DB + h * HD:tt * DB + h * HD + HD]
                        mm = pe.matmul(o, zs[:, place(h) * SEQ + tt * P:place(h) * SEQ + tt * P + P], U[4][:, 0, h * HD:h * HD + HD],
                                       start=True, stop=(tt == 0))
                        if tt:
                            mm = pe.matmul(o, zs[:, NH * SEQ + place(h) * P:NH * SEQ + place(h) * P + P],
                                           U[4][:, 1, h * HD:h * HD + HD], start=False, stop=True)
                mm.then_inc(S("ret_o"), 1)
                gate(5)
                pe.wait_ge(S("tap"), KB * CONV_W * (l + 1))
                for c in range(KB):
                    for tt in range(TT):
                        mm = pe.transpose(T[0][:, tt * DB + c * P:tt * DB + c * P + P], conv[:, c, tt * P:tt * P + P],
                                          ident)
                mm.then_inc(S("conv_nat"), 1)
                gate(6)
                pe.wait_ge(S("ret_y"), l + 1)
                transpose_narrow(A[1][:], lambda tt, c: tmp[:, 0, tt, c]).then_inc(S("ret_yT"), 1)
                gate(7)
                pe.wait_ge(S("conv_ln"), l + 1)
                transpose_narrow(A[2][:], lambda tt, c: convn[:, tt, c]).then_inc(S("conv_lnT"), 1)
                for i, b in enumerate(BR_ORDER):
                    pe.wait_ge(S(f"yT_lo{b}"), l + 1)
                    pe.wait_ge(S(f"yT_hi{b}"), l + 1)
                    for nb in range(2):
                        n = base + BR0 + 2 * i + nb
                        have(0, n)
                        wh = w_hi[slot(n)][:].rearrange("p (k n) -> p k n", k=2)
                        wl = w_lo[slot(n)][:].rearrange("p (k n) -> p k n", k=2)
                        for tt in range(TT):
                            if i:
                                pe.wait_ge(S("prod"), 16 * l + 4 * (i - 1) + 2 * nb + tt + 1)
                            elif nb == 0:
                                pe.wait_ge(S("emptied"), 2 * unit_no(l, 13))
                            for k in range(KB):
                                mm = product((G, T)[nb][tt][:], yT[b][0][:, k, tt * P:tt * P + P],
                                             yT[b][1][:, k, tt * P:tt * P + P], wh[:, k, :], wl[:, k, :],
                                             k == 0, k == KB - 1)
                            mm.then_inc(S("branch") if tt == 0 else used, 1)
                def second_merged(c):
                    if c == 1:
                        pe.wait_ge(S("merged"), 4 * (l + 1))
                        turn(merged, (2, 3), S("mergedT"))
                    parts("gT", 4 * l + c + 1)

                pe.wait_ge(S("merged"), 4 * l + 2)
                turn(merged, (0, 1), S("mergedT"))
                done = 16 * (l + 1)
                streamed(base + OUT0, hT_hi, hT_lo, [(S("prod"), done), (S("prod"), done)], second_merged)
                pe.wait_ge(S("mem_in"), 16 * (l + 1))
                turn(memn, range(4), S("memT"))
                streamed(base + OUT0 + 4, hT_hi, hT_lo, [(S("out_added"), 4 * l + 1), (S("out_added"), 4 * l + 2)])

                def memory_parts(c):
                    if c == 1:
                        parts("mT", 4 * l + 4)
                        pe.wait_ge(S("out_added"), 4 * (l + 1))
                        turn(xs, range(4), S("xT"))
                    parts("mT", 4 * l + 2 * c + 2)

                streamed(base + XK0, mT_hi, mT_lo, [(S("out_added"), 4 * l + 3), (S("out_added"), 4 * l + 4)],
                         memory_parts, nchunks=2, kts=4, width=DB)
                streamed(base + XQ0, hT_hi, hT_lo, [None, None], lambda c: parts("hT", 12 * l + 4 + 2 * c + 2),
                         banks=T, nchunks=2, kts=4, width=DB)

                def keys_between(c):
                    if c == 1:
                        pe.wait_ge(S("mk_normed"), l + 1)
                        transpose_narrow(A[0][:], lambda tt, c: tmp[:, 0, tt, c]).then_inc(S("memkT"), 1)

                n = 2 * unit_no(l, 14)
                streamed(base + XV0, mT_hi, mT_lo, [(S("emptied"), n - 1), (S("emptied"), n)],
                         keys_between, nchunks=2, kts=4, width=DB)
                pe.wait_ge(S("q_normed"), l + 1)
                transpose_narrow(T[0][:], lambda tt, c: qn[:, tt, c]).then_inc(S("xqT"), 1)
                pe.wait_ge(S("memk_out"), l + 1)
                pe.wait_ge(S("xqT_out"), l + 1)
                for tt in range(TT):
                    for h in range(NH):
                        r = slice((h % 2) * HD, (h % 2) * HD + HD)
                        mm = pe.matmul(A[2 * tt + h % 2][:, (h // 2) * SEQ:(h // 2) * SEQ + SEQ],
                                       qT[r, h // 2, tt * P:tt * P + P], memk[r, h // 2, :], start=True, stop=True)
                    mm.then_inc(S("x_scores"), 1)
                for tt in range(TT):
                    for j in range(NH):
                        if j % 2 == 0:
                            pe.wait_ge(S("xp"), 4 * TT * l + 4 * tt + j + 2)
                        for mt in range(TT):
                            mm = pe.transpose(A[2 * tt + j // 2][:, (j % 2) * SEQ + mt * P:(j % 2) * SEQ + mt * P + P],
                                              prob[:, tt, j, mt * P:mt * P + P], ident)
                        if j % 2:
                            mm.then_inc(S("xpT"), 1)
                pe.wait_ge(S("emptied"), 2 * unit_no(l, 16))
                for tt in range(TT):
                    pe.wait_ge(S("xpT_out"), 4 * l + 2 * tt + 2)
                    for h in range(NH):
                        for mt in range(TT):
                            mm = pe.matmul(T[tt][:, h * HD:h * HD + HD],
                                           probT[:, tt, place(h), mt * P:mt * P + P], memv[:, mt, h * HD:h * HD + HD],
                                           start=(mt == 0), stop=(mt == TT - 1))
                    mm.then_inc(S("xo"), 1)
                for tt in range(TT):
                    pe.wait_ge(S("xo_normed"), TT * l + tt + 1)
                    for c in range(KB):
                        mm = pe.transpose(A[c][:, tt * P:tt * P + P], on[:, tt, c * P:c * P + P], ident)
                        if tt:
                            mm.then_inc(S("xoT"), 1)
                for nb in range(2):
                    n = base + XO0 + nb
                    have(0, n)
                    wh = w_hi[slot(n)][:].rearrange("p (k n) -> p k n", k=2)
                    wl = w_lo[slot(n)][:].rearrange("p (k n) -> p k n", k=2)
                    for tt in range(TT):
                        if nb and tt:
                            pe.wait_ge(S("xo_added"), 4 * l + 2)
                            turn(xs, (0, 1), S("xT"))
                        for k in range(KB):
                            if nb + tt == 0:
                                parts("oT", KB * l + k + 1)
                            mm = product((G, T)[nb][tt][:], oT_hi[:, k, tt * P:tt * P + P],
                                         oT_lo[:, k, tt * P:tt * P + P], wh[:, k, :], wl[:, k, :],
                                         k == 0, k == KB - 1)
                        mm.then_inc(S("xproj") if tt == 0 else used, 1)
                if l:
                    break

                def transposed_act(f):
                    pe.wait_ge(S("ff_act"), 2 * (f + 1))
                    if f:
                        pe.wait_ge(S("actT_hi"), f)
                        pe.wait_ge(S("actT_lo"), f)
                    transpose_narrow(T[0][:], lambda tt, c: act[:, tt, c]).then_inc(S("ff_actT"), 1)

                def down(f):
                    pe.wait_ge(S("actT_hi"), f + 1)
                    pe.wait_ge(S("actT_lo"), f + 1)
                    for nb in range(2):
                        n = FF_N0 + FFS * (f + 1) + (4 if f < NF - 1 else 0) + nb
                        have(0, n)
                        wh = w_hi[slot(n)][:].rearrange("p (k n) -> p k n", k=2)
                        wl = w_lo[slot(n)][:].rearrange("p (k n) -> p k n", k=2)
                        for tt in range(TT):
                            if f == NF - 1 and nb and tt:
                                pe.wait_ge(S("ffn_added"), 2)
                                turn(xs, (0, 1), S("xT"))
                            for k in range(2):
                                mm = product(A[2 * tt + nb][:], actT_hi[:, k, tt * P:tt * P + P],
                                             actT_lo[:, k, tt * P:tt * P + P], wh[:, k, :], wl[:, k, :],
                                             f == 0 and k == 0, f == NF - 1 and k == 1)
                        mm.then_inc(used, 1)

                for f in range(NF):
                    for c in range(4):
                        n = FF_N0 + FFS * f + c + 2 * (f == 0)
                        if f == 0:
                            if c == 1:
                                pe.wait_ge(S("xo_added"), 4 * (l + 1))
                                turn(xs, (2, 3), S("xT"))
                            parts("hT", 12 * l + 8 + c + 1)
                        have(0, n)
                        wh = w_hi[slot(n)][:].rearrange("p (k n) -> p k n", k=2)
                        wl = w_lo[slot(n)][:].rearrange("p (k n) -> p k n", k=2)
                        for tt in range(TT):
                            if c == 0 and f:
                                pe.wait_ge(S("ff_act"), 2 * f - 1 + tt)
                            for k in range(2):
                                mm = product(G[tt][:], hT_hi[:, 2 * c + k, tt * P:tt * P + P],
                                             hT_lo[:, 2 * c + k, tt * P:tt * P + P], wh[:, k, :], wl[:, k, :],
                                             c + k == 0, c == 3 and k == 1)
                            if c == 3 and tt == 0:
                                mm.then_inc(half, 1)
                        mm.then_inc(used, 1)
                        if f and c == 1:
                            transposed_act(f - 1)
                    if f:
                        down(f - 1)
                transposed_act(NF - 1)
                down(NF - 1)

            pe.wait_ge(S("rt_in"), 16)
            for half_k in range(2):
                if half_k:
                    pe.wait_ge(S("xo_added"), 4 * DEPTH)
                    turn(xs, (2, 3), S("xT"))
                if half_k:
                    have(FF_LAP, 2)
                    keep_warm(T[0], 5)
                pe.wait_ge(S("rhT"), 2 * half_k + 2)
                for tt in range(TT):
                    for k in range(4 * half_k, 4 * half_k + 4):
                        mm = pe.matmul(G[tt][:, 0:NE], hT_f32[:, k, tt * P:tt * P + P], rt[:, k, :],
                                       start=(k == 0), stop=(k == KT - 1))
            mm.then_inc(S("logits"), 1)
            keep_warm(T[0], 13)
            pe.wait_ge(S("picked"), 1)
            pe.matmul(T[1][:, 0:NE], tri_lt, lg[:, 6, 0, :], start=True, stop=True)
            pe.matmul(T[1][:, NE:2 * NE], ones, lg[:, 6, 0, :], start=True, stop=False)
            pe.matmul(T[1][:, NE:2 * NE], tri_lt, lg[:, 6, 1, :], start=False, stop=True).then_inc(S("counted"), 1)
            pe.matmul(G[0][:, 0:NE], ones, lg[:, 6, 0, :], start=True, stop=False)
            pe.matmul(G[0][:, 0:NE], ones, lg[:, 6, 1, :], start=False, stop=True).then_inc(S("totals"), 1)
            keep_warm(T[0], 4)
            GB = [G[0], G[1], T[1]]

            def gather(i, tiles=range(KT)):
                pe.wait_ge(S("sel"), i + 1)
                for k in tiles:
                    for tt in range(TT):
                        for part in (xn_hi, xn_lo):
                            mm = pe.matmul(A[2 + k // 4][:, (k % 4) * P:(k % 4) * P + P], part[:, tt, k * P:k * P + P],
                                           sel[:, tt, :], start=(tt == 0 and part is xn_hi),
                                           stop=(tt == TT - 1 and part is xn_lo))
                    if k % 4 == 3:
                        mm.then_inc(S("gathered"), 1)

            def turn_selection(i):
                for tt in range(TT):
                    mm = pe.transpose(T[0][:, 256 + tt * P:256 + tt * P + P], sel[:, tt, :].bitcast(F32), ident)
                mm.then_inc(S("selT"), 1)

            def e_transposed(step, turned=None):
                pe.wait_ge(S("e_act"), step + 1)
                if turned is not None:
                    pe.wait_ge(S("selT_out"), turned)
                for c in range(2):
                    mm = pe.transpose(T[0][:, c * P:c * P + P], act[:, 0, c * P:c * P + P], ident)
                mm.then_inc(S("e_actT"), 1)

            def e_down(lap0, k, step, f):
                pe.wait_ge(S("e_aT_hi"), step + 1)
                pe.wait_ge(S("e_aT_lo"), step + 1)
                for nb in range(2):
                    have(lap0, k + nb)
                    wh = w_hi[slot(k + nb)][:].rearrange("p (k n) -> p k n", k=2)
                    wl = w_lo[slot(k + nb)][:].rearrange("p (k n) -> p k n", k=2)
                    for kk in range(2):
                        mm = product(A[nb][:], actT_hi[:, kk, 0:P], actT_lo[:, kk, 0:P], wh[:, kk, :], wl[:, kk, :],
                                     f == 0 and kk == 0, f == NF - 1 and kk == 1)
                    mm.then_inc(used, 1)

            def scatter(i, tt):
                pe.wait_ge(S("ye_hi"), 2 * i + 2)
                pe.wait_ge(S("ye_lo"), 2 * i + 2)
                pe.wait_ge(S("selT_out"), i + 1)
                if tt:
                    pe.wait_ge(S("scattered"), 4 * i + 2)
                for nb in range(2):
                    for part in (ye_hi, ye_lo):
                        mm = pe.matmul(A[2 + nb][:], selT[:, tt * P:tt * P + P], part[:, nb * 512:nb * 512 + 512],
                                       start=part is ye_hi, stop=part is ye_lo)
                mm.then_inc(S("scat"), 1)

            def item(i, first=False, last=False):
                lap0 = FF_LAP + NF * i
                for f in range(NF):
                    step = NF * i + f
                    for c in range(4):
                        k = FFS * f + c + 2 * (first and f == 0)
                        have(lap0, k)
                        if f == 0 and c % 2 == 0:
                            pe.wait_ge(S("eT_hi"), 2 * i + c // 2 + 1)
                            pe.wait_ge(S("eT_lo"), 2 * i + c // 2 + 1)
                        if c == 0 and (f >= 3 or not first):
                            back = (2, 2, 5)[f] if f < 3 else 3
                            pe.wait_ge(S("e_act"), step - back + 1)
                        wh = w_hi[slot(k)][:].rearrange("p (k n) -> p k n", k=2)
                        wl = w_lo[slot(k)][:].rearrange("p (k n) -> p k n", k=2)
                        for kk in range(2):
                            mm = product(GB[f % 3][:], eT_hi[:, 2 * c + kk, :], eT_lo[:, 2 * c + kk, :],
                                         wh[:, kk, :], wl[:, kk, :], c + kk == 0, c == 3 and kk == 1)
                        mm.then_inc(used, 1)
                        if c == 0 and first and f == 0:
                            gather(0, (6, 7))
                        if c == 1 and not (first and f == 0):
                            e_transposed(step - 1, i + 1 if f == 5 else None)
                    if f:
                        if f == 1 and not first:
                            pe.wait_ge(S("ye_hi"), 2 * i)
                            pe.wait_ge(S("ye_lo"), 2 * i)
                        e_down(lap0, FFS * f + 4, step - 1, f - 1)
                    elif not first:
                        e_down(lap0, 4, step - 1, NF - 1)
                    if f in (1, 3) and not first:
                        scatter(i - 1, f // 2)
                    if f == 4:
                        turn_selection(i)
                    if f == 8 and not last:
                        if not first:
                            pe.wait_ge(S("scattered"), 4 * i)
                        gather(i + 1)

            pe.wait_ge(S("xn_hi"), TT)
            pe.wait_ge(S("xn_lo0"), 1)
            pe.wait_ge(S("xn_lo1"), 1)
            gather(0, range(6))
            item(0, first=True)
            pe.wait_ge(S("items"), 1)
            items = pe.snap(NE + pe.value_load(more_items[0:1, 0:1], min_val=0, max_val=NE))
            with pe.Fori(1, items - 1) as i:
                item(i)
            last = pe.snap(items - 1)
            item(last, last=True)
            e_transposed(last * NF + NF - 1)
            e_down(FF_LAP + NF * items, 0, last * NF + NF - 1, NF - 1)
            pe.wait_ge(S("selT_out"), last + 1)
            for nb in range(2):
                pe.wait_ge(S("ye_hi"), 2 * last + nb + 1)
                pe.wait_ge(S("ye_lo"), 2 * last + nb + 1)
                for tt in range(TT):
                    for part in (ye_hi, ye_lo):
                        mm = pe.matmul((A[2:], G)[nb][tt][:], selT[:, tt * P:tt * P + P],
                                       part[:, nb * 512:nb * 512 + 512], start=part is ye_hi, stop=part is ye_lo)
                    mm.then_inc(S("last_scat"), 1)

        @block.scalar
        def _(act_e):
            steps = [0]

            def link(ins):
                steps[0] += 1
                ins.then_inc(act_step, 1)
                act_e.wait_ge(act_step, steps[0])

            nxt = [0]

            def split_to(k_end, lap0=0, item=None):
                while nxt[0] < k_end:
                    k = nxt[0]
                    buffer, signal, count = landing(lap0, k, item)
                    act_e.wait_ge(signal, count)
                    if not isinstance(lap0, int) or number(lap0, k) >= RING:
                        act_e.wait_ge(used, number(lap0, k) - RING + 1)
                    nc.scalar.activation(w_hi[slot(k)][:], buffer[:], ACT.Copy).then_inc(hi_ready, 1)
                    nxt[0] += 1

            def ahead(k):
                split_to(k + RING)

            def token_roots(l, norm, src):
                token_squares(l, norm, src)
                token_root(l, norm)

            def token_squares(l, norm, src):
                for tt in range(TT):
                    link(nc.scalar.activation(xn[:, tt, :], src[:, tt, :], ACT.Square,
                                              accum_out=ssq[:, 4 * l + norm, tt:tt + 1]))

            def token_root(l, norm):
                j = 4 * l + norm
                nc.scalar.activation(srt[:, j, :], ssq[:, j, :], ACT.Sqrt, scale=1.0 / D,
                                     bias=eps_col[:, 0:1]).then_inc(S("rooted_tokens"), 1)

            def scaled(dst, src, l, norm, tt, func=ACT.Copy):
                return nc.scalar.activation(dst, src, func, scale=rs[:, 4 * l + norm, tt:tt + 1])

            def bring_root():
                nc.scalar.activation(unused[:], one_col[:], ACT.Sqrt)

            roots = [0]

            def square_root():
                roots[0] += 1
                act_e.wait_ge(S("mean_square"), roots[0])
                nc.scalar.activation(root[:, 1, :], root[:, 0, :], ACT.Sqrt).then_inc(S("rooted"), 1)

            def round_wide(dst, gain, done, ready, count, banks=range(4)):
                for b in banks:
                    act_e.wait_ge(ready, count + b + 1)
                    for kt in (2 * b, 2 * b + 1):
                        bank = TB[b][:, (kt % 2) * SEQ:(kt % 2) * SEQ + SEQ]
                        ins = nc.scalar.activation(dst[:, kt, :], bank, ACT.Copy, scale=gain[:, kt:kt + 1])
                    ins.then_inc(done, 1)

            def gains(l, first):
                return gcol[:, first + KT * l:first + KT * l + KT]

            act_e.wait_ge(S("mix_cols"), 1)
            nc.scalar.activation(gmix[:], T[0][:, 0:DEPTH * KT], ACT.Copy).then_inc(S("gmix_out"), 1)
            act_e.wait_ge(S("gmix_out"), 1)
            act_e.wait_ge(S("eps_set"), 3)

            for l in range(DEPTH):
                base = LAYER0[l]
                mix_gain = gmix[:, KT * l:KT * l + KT]
                round_wide(hT_hi, mix_gain, S("hT_hi"), S("xT"), 12 * l, (0,))
                if l == 0:
                    split_to(1)
                round_wide(hT_hi, mix_gain, S("hT_hi"), S("xT"), 12 * l, (1,))
                if l == 0:
                    split_to(2)
                else:
                    split_to(base + 4)
                round_wide(hT_hi, mix_gain, S("hT_hi"), S("xT"), 12 * l, (2, 3))
                if l == 0:
                    split_to(5)
                token_roots(l, MIX, xs)

                def unit(u, n, evacuate, lead=RING):
                    split_to(n + lead)
                    for tt in range(TT):
                        if tt == 0:
                            act_e.wait_ge(half, half_no(l, u if u < 13 else u + 2) + 1)
                        else:
                            act_e.wait_ge(used, n + 1)
                        if tt == 0 and u in (0, 13, 14):
                            act_e.wait_ge(S("token_scale"), 4 * l + {0: MIX, 13: MEM, 14: XA}[u] + 1)
                        evacuate(tt).then_inc(S("emptied"), 1)

                def whole(b):
                    return lambda tt: scaled(U[b][:, tt, :], G[tt][:], l, MIX, tt)

                def two(b, func):
                    def evacuate(tt):
                        scaled(U[b][:, tt, 0:DB], G[tt][:, 0:DB], l, MIX, tt)
                        return scaled(U[b][:, tt, DB:], G[tt][:, DB:], l, MIX, tt, func)
                    return evacuate

                unit(0, base + 3, whole(1), RING if l else 3)
                if l == 0:
                    act_e.wait_ge(S("cols"), 1)
                    nc.scalar.activation(gcol[:], T[1][:, 0:G_ROWS], ACT.Copy)
                    nc.scalar.activation(cwcol[:], T[1][:, 128:128 + 2 * CONV_W * DEPTH],
                                         ACT.Copy).then_inc(S("cols_out"), 1)
                    act_e.wait_ge(S("cols_out"), 1)
                unit(1, base + 7, whole(2))
                unit(2, base + 11, two(0, ACT.Sigmoid))
                act_e.wait_ge(S("sb_qk"), l + 1)
                nc.scalar.activation(qT[:].rearrange("p c t -> p (c t)"), T[0][:], ACT.Copy, scale=HD ** -0.5)
                nc.scalar.activation(kT[:].rearrange("p c t -> p (c t)"), T[1][:], ACT.Copy).then_inc(S("sb_qk_out"), 1)
                act_e.wait_ge(S("pool_d"), l + 1)
                nc.scalar.activation(dT[:].rearrange("p c t -> p (c t)"), A[0][:], ACT.Copy).then_inc(S("dT_out"), 1)
                if l == 0:
                    act_e.wait_ge(S("angles"), 1)
                    ang = tmp[:, 1].rearrange("p t c -> p (t c)")
                    link(nc.scalar.activation(ang[:, 64:128], ang[:, 0:64], ACT.Abs))
                    nc.scalar.activation(trig[:, 1].rearrange("p t c -> p (t c)"), ang[:, 0:64], ACT.Sin)
                    nc.scalar.activation(trig[:, 0].rearrange("p t c -> p (t c)"), ang[:, 64:128],
                                         ACT.Sin, scale=-1.0, bias=half_pi[:, 0:1]).then_inc(S("trig"), 1)
                unit(3, base + 15, whole(3))
                act_e.wait_ge(S("pool_y"), l + 1)
                for c in range(KB):
                    ins = nc.scalar.activation(yT[1][0][:, c, :], T[0][:, c * SEQ:c * SEQ + SEQ], ACT.Copy,
                                               scale=gcol[:, G_PS + 2 * l + c:G_PS + 2 * l + c + 1])
                ins.then_inc(S("yT_hi1"), 1)
                unit(4, base + 19, two(4, ACT.Silu))
                act_e.wait_ge(S("conv_vT"), l + 1)
                nc.scalar.activation(vT[:, :, CONV_W - 1:], T[1][:].rearrange("p (c t) -> p c t", c=KB),
                                     ACT.Copy).then_inc(S("vT_out"), 1)
                act_e.wait_ge(S("sb_zm"), l + 1)
                link(nc.scalar.activation(zs, zm, ACT.Abs))
                link(nc.scalar.activation(zs, zs, ACT.Exp, scale=-1.0))
                nc.scalar.activation(zs, zs, ACT.Ln, bias=one_col[:, 0:1]).then_inc(S("sb_l"), 1)

                def gate(g):
                    unit(5 + g, base + GATE0 + 4 * g + 3, lambda tt: scaled(
                        gates[:, g // 2, tt, (g % 2) * 512:(g % 2) * 512 + 512], G[tt][:], l, MIX, tt, ACT.Sigmoid))

                gate(0)
                gate(1)
                act_e.wait_ge(S("sb_w"), l + 1)
                nc.scalar.activation(zm, zm, ACT.Exp).then_inc(S("sb_exp"), 1)
                act_e.wait_ge(S("ret_qk"), l + 1)
                nc.scalar.activation(qT[:].rearrange("p c t -> p (c t)"), T[0][:], ACT.Copy)
                nc.scalar.activation(kT[:].rearrange("p c t -> p (c t)"), T[1][:], ACT.Copy).then_inc(S("ret_qk_out"), 1)
                gate(2)
                gate(3)
                act_e.wait_ge(S("sb_y"), l + 1)
                nc.scalar.activation(yT[2][0][:].rearrange("p c t -> p (c t)"), A[0][:], ACT.Copy).then_inc(S("yT_hi2"), 1)
                gate(4)
                gate(5)
                square_root()
                gate(6)
                square_root()
                gate(7)
                act_e.wait_ge(S("ret_yT"), l + 1)
                nc.scalar.activation(yT[3][0][:].rearrange("p c t -> p (c t)"), A[1][:], ACT.Copy).then_inc(S("yT_hi3"), 1)
                act_e.wait_ge(S("conv_lnT"), l + 1)
                for c in range(KB):
                    g0, b0 = G_LG + 2 * l + c, G_LB + 2 * l + c
                    link(nc.scalar.activation(conv[:, c, :], A[2][:, c * SEQ:c * SEQ + SEQ], ACT.Silu,
                                              scale=gcol[:, g0:g0 + 1], bias=gcol[:, b0:b0 + 1]))
                nc.scalar.activation(yT[0][0][:], conv[:], ACT.Copy).then_inc(S("yT_hi0"), 1)
                ahead(base + BR0 + 6)
                bring_root()
                for b in range(4):
                    if b == 2:
                        ahead(base + BR0 + 8)
                    act_e.wait_ge(S("mergedT"), 4 * l + b + 1)
                    nc.scalar.activation(hT_hi[:, 2 * b:2 * b + 2, :].rearrange("p c t -> p (c t)"), TB[b][:],
                                         ACT.Copy).then_inc(S("gT_hi"), 1)
                ahead(base + OUT0 + 1)
                act_e.wait_ge(S("mem_in"), 16 * (l + 1))
                token_roots(l, MEM, memn)
                ahead(base + OUT0 + 3)
                round_wide(mT_hi, gains(l, G_MEM), S("mT_hi"), S("memT"), 4 * l)
                ahead(base + OUT0 + 7)
                round_wide(hT_hi, gains(l, G_XA), S("hT_hi"), S("xT"), 12 * l + 4)
                token_roots(l, XA, xs)
                unit(13, base + XK0 + 1, lambda tt: scaled(convn[:, tt, :], G[tt][:, 0:DB], l, MEM, tt), 5)
                square_root()
                unit(14, base + XQ0 + 1, lambda tt: scaled(qn[:, tt, :], T[tt][:, 0:DB], l, XA, tt), 3)
                square_root()
                act_e.wait_ge(S("memkT"), l + 1)
                nc.scalar.activation(memk[:].rearrange("p c t -> p (c t)"), A[0][:], ACT.Copy).then_inc(S("memk_out"), 1)
                unit(15, base + XV0 + 1, lambda tt: scaled(memv[:, tt, :], G[tt][:, 0:DB], l, MEM, tt), 1)
                act_e.wait_ge(S("xqT"), l + 1)
                nc.scalar.activation(qT[:].rearrange("p c t -> p (c t)"), T[0][:], ACT.Copy,
                                     scale=gqk[:, l:l + 1]).then_inc(S("xqT_out"), 1)
                split_to(base + XV0 + 3)
                for tt in range(TT):
                    act_e.wait_ge(S("xmax"), TT * l + tt + 1)
                    for i in range(NH):
                        j = tt * NH + i
                        nc.scalar.activation(prob[:, tt, i, :], A[2 * tt + i // 2][:, (i % 2) * SEQ:(i % 2) * SEQ + SEQ],
                                             ACT.Exp, bias=stat[:, 5, j:j + 1],
                                             accum_out=stat[:, 4, tt * NH + place(i):tt * NH + place(i) + 1]
                                             ).then_inc(S("xp"), 1)
                for tt in range(TT):
                    for hp in range(2):
                        act_e.wait_ge(S("xpT"), 4 * l + 2 * tt + hp + 1)
                        nc.scalar.activation(probT[:, tt, 2 * hp:2 * hp + 2, :].rearrange("p h m -> p (h m)"),
                                             A[2 * tt + hp][:], ACT.Copy).then_inc(S("xpT_out"), 1)
                split_to(base + XV0 + 4)
                bring_root()
                for c in range(KB):
                    act_e.wait_ge(S("xoT"), KB * l + c + 1)
                    nc.scalar.activation(oT_hi[:, c, :], A[c][:, 0:SEQ], ACT.Copy).then_inc(S("oT_hi"), 1)
                ahead(base + XO0)
                if l:
                    break
                round_wide(hT_hi, gains(l, G_FFN), S("hT_hi"), S("xT"), 12 * l + 8, (0, 1))
                ahead(base + XO0 + 2)
                round_wide(hT_hi, gains(l, G_FFN), S("hT_hi"), S("xT"), 12 * l + 8, (2, 3))
                token_roots(l, FFN, xs)

                def ff_round(f):
                    act_e.wait_ge(S("ff_actT"), f + 1)
                    nc.scalar.activation(actT_hi[:].rearrange("p c t -> p (c t)"), T[0][:],
                                         ACT.Copy).then_inc(S("actT_hi"), 1)

                for f in range(NF):
                    if f:
                        ahead(FF_N0 + FFS * f + 1)
                        ff_round(f - 1)
                    else:
                        act_e.wait_ge(S("token_scale"), 4 * l + FFN + 1)
                    k = FF_N0 + FFS * f + 3 + 2 * (f == 0)
                    split_to(k + (RING if f else 3))
                    for tt in range(TT):
                        if tt == 0:
                            act_e.wait_ge(half, half_no(0, 18 + f) + 1)
                        else:
                            act_e.wait_ge(used, k + 1)
                        if f:
                            act_e.wait_ge(S("ff_act"), 2 * f - 1 + tt)
                        scaled(silu[:, tt, :], G[tt][:, 0:FB], l, FFN, tt, ACT.Silu).then_inc(S("ff_silu"), 1)
                ff_round(NF - 1)

            def whole_turned(banks):
                for b in banks:
                    act_e.wait_ge(S("xT"), 12 * (DEPTH - 1) + 8 + b + 1)
                    for kt in (2 * b, 2 * b + 1):
                        g = G_FFN + KT * (DEPTH - 1) + kt
                        ins = nc.scalar.activation(hT_f32[:, kt, :], TB[b][:, (kt % 2) * SEQ:(kt % 2) * SEQ + SEQ],
                                                   ACT.Copy, scale=gcol[:, g:g + 1])
                    ins.then_inc(S("rhT"), 1)

            def half_squares(nb):
                act_e.wait_ge(S("xo_added"), 4 * (DEPTH - 1) + 2 * nb + 2)
                for tt in range(TT):
                    sl = slice(nb * 512, nb * 512 + 512)
                    nc.scalar.activation(xn[:, tt, sl], xs[:, tt, sl], ACT.Square,
                                         accum_out=half_ssq[:, nb, tt:tt + 1]).then_inc(S("squares"), 1)

            half_squares(0)
            whole_turned((0, 1))
            half_squares(1)
            act_e.wait_ge(S("squares_added"), 1)
            token_root(DEPTH - 1, FFN)
            whole_turned((2, 3))
            for tt in range(TT):
                act_e.wait_ge(S("xn"), tt + 1)
                nc.scalar.activation(xn_hi[:, tt, :], xn[:, tt, :], ACT.Copy).then_inc(S("xn_hi"), 1)
            act_e.wait_ge(S("gap"), 1)
            nc.scalar.activation(lg[:, 10, :, 0], lg[:, 10, :, 1], ACT.Exp).then_inc(S("gap_exp"), 1)
            lap0 = FF_LAP
            nxt[0] -= RING * lap0
            split_to(2 + RING, lap0, 0)

            def round_gathered(i):
                for j in range(2):
                    act_e.wait_ge(S("gathered"), 2 * i + j + 1)
                    nc.scalar.activation(eT_hi[:, 4 * j:4 * j + 4, :].rearrange("p k s -> p (k s)"), A[2 + j][:],
                                         ACT.Copy).then_inc(S("eT_hi"), 1)

            def e_round(step):
                act_e.wait_ge(S("e_actT"), step + 1)
                nc.scalar.activation(actT_hi[:, :, 0:P], T[0][:, 0:2 * P].rearrange("p (c t) -> p c t", c=2),
                                     ACT.Copy).then_inc(S("e_aT_hi"), 1)

            def item(i, first=False, last=False):
                lap0 = FF_LAP + NF * i
                end = FFS * NF + (2 if last else LEAD)
                for f in range(NF):
                    step = NF * i + f
                    if not (first and f == 0):
                        split_to(FFS * f + 2 + LEAD, lap0, i)
                        e_round(step - 1)
                    k = FFS * f + 3 + 2 * (first and f == 0)
                    split_to(min(k + 1 + LEAD, end), lap0, i)
                    act_e.wait_ge(used, number(lap0, k) + 1)
                    if not (first and f == 0):
                        act_e.wait_ge(S("e_act"), step)
                    nc.scalar.activation(silu[:, 0, :], (G[0], G[1], T[1])[f % 3][:, 0:FB],
                                         ACT.Silu).then_inc(S("e_silu"), 1)
                    if f == 0 and not first:
                        for nb in range(2):
                            split_to(5 + nb + LEAD, lap0, i)
                            act_e.wait_ge(used, number(lap0, 4 + nb) + 1)
                            nc.scalar.activation(ye_hi[:, nb * 512:nb * 512 + 512], A[nb][:],
                                                 ACT.Copy).then_inc(S("ye_hi"), 1)
                    if f == 4:
                        act_e.wait_ge(S("selT"), i + 1)
                        nc.scalar.activation(selT[:], T[0][:, 2 * P:4 * P], ACT.Copy).then_inc(S("selT_out"), 1)
                if not last:
                    round_gathered(i + 1)

            round_gathered(0)
            item(0, first=True)
            nxt[0] = LEAD - 2
            act_e.wait_ge(S("items"), 1)
            items = act_e.snap(NE + act_e.value_load(more_items[0:1, 0:1], min_val=0, max_val=NE))
            with act_e.Fori(1, items - 1) as i:
                item(i)
            assert nxt[0] == LEAD - 2 + RING * NF
            nxt[0] = LEAD - 2
            last = act_e.snap(items - 1)
            item(last, last=True)
            e_round(last * NF + NF - 1)
            for nb in range(2):
                act_e.wait_ge(used, RING * FF_LAP + RING * NF * items + nb + 1)
                nc.scalar.activation(ye_hi[:, nb * 512:nb * 512 + 512], A[nb][:], ACT.Copy).then_inc(S("ye_hi"), 1)

        @block.vector
        def _(dve):
            v = nc.vector
            steps = [0]

            def link(ins):
                steps[0] += 1
                ins.then_inc(dve_step, 1)
                dve.wait_ge(dve_step, steps[0])

            nxt = [0]

            def split_to(k_end, lap0=0, item=None):
                while nxt[0] < k_end:
                    k = nxt[0]
                    dve.wait_ge(hi_ready, number(lap0, k) + 1)
                    buffer, _, _ = landing(lap0, k, item)
                    v.tensor_tensor(w_lo[slot(k)][:], buffer[:], w_hi[slot(k)][:].bitcast(F32),
                                    ALU.subtract).then_inc(lo_ready, 1)
                    nxt[0] += 1

            def ahead(k):
                split_to(k + RING)

            def power(dst, src, scale, eps=EPS):
                w = dst.shape[1]
                v.tensor_scalar(root[:, 0, 0:w], src, scale, eps, ALU.mult, ALU.add).then_inc(S("mean_square"), 1)
                roots[0] += 1
                dve.wait_ge(S("rooted"), roots[0])
                link(v.reciprocal(dst, root[:, 1, 0:w]))

            roots = [0]
            v.memset(eps_col[:], EPS).then_inc(S("eps_set"), 1)
            v.memset(half_pi[:], float(np.float32(np.pi / 2))).then_inc(S("eps_set"), 1)
            v.memset(one_col[:], 1.0).then_inc(S("eps_set"), 1)
            link(v.memset(root[:], 1.0))
            v.memset(vT[:, :, 0:CONV_W - 1], 0.0)

            def token_scale(l, norm):
                j = 4 * l + norm
                dve.wait_ge(S("rooted_tokens"), j + 1)
                v.reciprocal(rs[:, j, :], srt[:, j, :]).then_inc(S("token_scale"), 1)

            def rest_wide(dst, hi, gain, hi_done, count, done, banks=range(4)):
                for b in banks:
                    dve.wait_ge(hi_done, count + b + 1)
                    for kt in (2 * b, 2 * b + 1):
                        bank = TB[b][:, (kt % 2) * SEQ:(kt % 2) * SEQ + SEQ]
                        ins = v.scalar_tensor_tensor(out=dst[:, kt, :], in0=bank, scalar=gain[:, kt:kt + 1],
                                                     in1=hi[:, kt, :].bitcast(F32), op0=ALU.mult, op1=ALU.subtract)
                    ins.then_inc(done, 1)

            def gains(l, first):
                return gcol[:, first + KT * l:first + KT * l + KT]

            def flat(t):
                return t.rearrange("p c t -> p (c t)")

            def head_scale(src, square, row):
                link(v.tensor_tensor(square, src, src, ALU.mult))
                link(v.tensor_reduce(stat[:, row, :], square.rearrange("p (g d) -> p g d", d=HD), AX.X, ALU.add))
                power(stat[:, row + 1, :], stat[:, row, :], 1.0 / HD)

            def per_head(row):
                return stat[:, row, :].unsqueeze(2).to_broadcast([P, TT * NH, HD])

            heads = "p (g d) -> p g d"

            def add_ffn(l, nb):
                dve.wait_ge(used, FF_N0 + FFS * NF + nb + 1)
                for tt in range(TT):
                    sl = slice(nb * 512, nb * 512 + 512)
                    v.tensor_tensor(xs[:, tt, sl], xs[:, tt, sl], A[2 * tt + nb][:], ALU.add).then_inc(S("ffn_added"), 1)

            def turn_angles():
                dve.wait_ge(S("cols_out"), 1)
                for l in range(DEPTH):
                    v.scalar_tensor_tensor(out=gqk[:, l:l + 1], in0=gcol[:, G_QG + l:G_QG + l + 1], scalar=HD ** -0.5,
                                           in1=gcol[:, G_KG + l:G_KG + l + 1], op0=ALU.mult, op1=ALU.mult)
                dve.wait_ge(S("pos_in"), 16)
                dve.wait_ge(S("cst_in"), 16)
                link(v.tensor_copy(stat[:, 6, 0:TT], posi[:]))
                ang = tmp[:, 1].rearrange("p t c -> p (t c)")
                r, n2, a0 = ang[:, 0:64], ang[:, 128:192], ang[:, 192:256]
                for tt in range(TT):
                    link(v.tensor_scalar(a0[:, tt * 32:tt * 32 + 32], cst[:, C_FREQ:C_FREQ + 32], stat[:, 6, tt:tt + 1],
                                         None, ALU.mult))
                link(v.tensor_scalar(n2, a0, 1.0 / (2 * np.pi), ROUND, ALU.mult, ALU.add))
                link(v.tensor_scalar(n2, n2, -ROUND, None, ALU.add))
                link(v.scalar_tensor_tensor(out=r, in0=n2, scalar=-TWO_PI_1, in1=a0, op0=ALU.mult, op1=ALU.add))
                link(v.scalar_tensor_tensor(out=r, in0=n2, scalar=-TWO_PI_2, in1=r, op0=ALU.mult, op1=ALU.add))
                link(v.scalar_tensor_tensor(out=r, in0=n2, scalar=-TWO_PI_3, in1=r, op0=ALU.mult, op1=ALU.add))
                v.tensor_scalar(r, r, 3.1415925, -3.1415925, ALU.min, ALU.max).then_inc(S("angles"), 1)

            for l in range(DEPTH):
                base = LAYER0[l]
                if l == 0:
                    dve.wait_ge(S("gmix_out"), 1)
                mix_gain = gmix[:, KT * l:KT * l + KT]
                rest_wide(hT_lo, hT_hi, mix_gain, S("hT_hi"), 12 * l, S("hT_lo"), (0,))
                if l == 0:
                    split_to(1)
                rest_wide(hT_lo, hT_hi, mix_gain, S("hT_hi"), 12 * l, S("hT_lo"), (1,))
                if l == 0:
                    split_to(2)
                else:
                    add_ffn(l - 1, 1)
                    split_to(base + 3)
                rest_wide(hT_lo, hT_hi, mix_gain, S("hT_hi"), 12 * l, S("hT_lo"), (2, 3))
                if l == 0:
                    split_to(5)
                token_scale(l, MIX)
                if l == 0:
                    ahead(base + 7)
                    turn_angles()
                ahead(base + 11)
                dve.wait_ge(S("emptied"), 2 * unit_no(l, 2) + 2)
                v.tensor_tensor(convn[:], U[0][:, :, 0:DB], U[0][:, :, DB:], ALU.mult).then_inc(S("conv_v"), 1)
                ahead(base + 15)
                dve.wait_ge(S("sb_z"), l + 1)
                m2 = mask.unsqueeze(1).to_broadcast([P, 2, SEQ])
                m4 = mask.unsqueeze(1).to_broadcast([P, NH, SEQ])
                m4s = mask[:, 0:P].unsqueeze(1).to_broadcast([P, NH, P])

                def near(t):
                    return t[:, 0:NH * SEQ].rearrange("p (h q) -> p h q", h=NH)

                def far(t):
                    return t[:, NH * SEQ:].rearrange("p (h q) -> p h q", h=NH)

                for j in range(2):
                    v.tensor_tensor(near(zm)[:, 2 * j:2 * j + 2], A[1 + j][:].rearrange("p (h q) -> p h q", h=2), m2, ALU.mult)
                v.tensor_tensor(far(zm), A[3][:].rearrange("p (h q) -> p h q", h=NH), m4s, ALU.mult).then_inc(S("sb_zm"), 1)
                dve.wait_ge(S("yT_hi1"), l + 1)
                for c in range(KB):
                    ins = v.scalar_tensor_tensor(out=yT[1][1][:, c, :], in0=T[0][:, c * SEQ:c * SEQ + SEQ],
                                                 scalar=gcol[:, G_PS + 2 * l + c:G_PS + 2 * l + c + 1],
                                                 in1=yT[1][0][:, c, :].bitcast(F32), op0=ALU.mult, op1=ALU.subtract)
                ins.then_inc(S("yT_lo1"), 1)
                dve.wait_ge(S("emptied"), 2 * unit_no(l, 3) + 2)
                if l == 0:
                    dve.wait_ge(S("trig"), 1)
                for tt in range(TT):
                    qk = U[3][:, tt, :].rearrange("p (h two d) -> p h two d", two=2, d=HD // 2)
                    x1, x2 = qk[:, :, 0, :], qk[:, :, 1, :]
                    cos = trig[:, 0, tt, :].unsqueeze(1).to_broadcast([P, 2 * NH, HD // 2])
                    sin = trig[:, 1, tt, :].unsqueeze(1).to_broadcast([P, 2 * NH, HD // 2])
                    t1 = tmp[:, 0, tt, :].rearrange("p (h d) -> p h d", d=HD // 2)
                    t2 = tmp[:, 1, tt, :].rearrange("p (h d) -> p h d", d=HD // 2)
                    v.tensor_tensor(t1, x1, sin, ALU.mult)
                    link(v.tensor_tensor(t2, x2, sin, ALU.mult))
                    v.tensor_tensor(x1, x1, cos, ALU.mult)
                    link(v.tensor_tensor(x2, x2, cos, ALU.mult))
                    v.tensor_tensor(x1, x1, t2, ALU.subtract)
                    ins = v.tensor_tensor(x2, x2, t1, ALU.add)
                ins.then_inc(S("rotated"), 1)
                ahead(base + 19)
                dve.wait_ge(S("sb_l"), l + 1)
                link(v.scalar_tensor_tensor(out=zs, in0=zm, scalar=0.0, in1=zs, op0=ALU.max, op1=ALU.add))
                v.tensor_tensor(near(zs), near(zs), m4, ALU.mult)
                v.tensor_tensor(far(zs), far(zs), m4s, ALU.mult).then_inc(S("sb_sp"), 1)

                dve.wait_ge(S("vT_out"), l + 1)
                taps = [0]

                def conv_taps(count):
                    for w in range(taps[0], min(taps[0] + count, CONV_W)):
                        for c in range(KB):
                            tap = cwcol[:, (l * CONV_W + w) * KB + c:(l * CONV_W + w) * KB + c + 1]
                            src = vT[:, c, w:w + SEQ]
                            if w == 0:
                                bias = gcol[:, G_CB + 2 * l + c:G_CB + 2 * l + c + 1]
                                ins = v.tensor_scalar(conv[:, c, :], src, tap, bias, ALU.mult, ALU.add)
                            else:
                                dve.wait_ge(S("tap"), KB * CONV_W * l + KB * (w - 1) + c + 1)
                                ins = v.scalar_tensor_tensor(out=conv[:, c, :], in0=src, scalar=tap, in1=conv[:, c, :],
                                                             op0=ALU.mult, op1=ALU.add)
                            ins.then_inc(S("tap"), 1)
                    taps[0] = min(taps[0] + count, CONV_W)

                done = [0]

                def gates_to(n):
                    while done[0] <= n:
                        ahead(base + GATE0 + done[0])
                        conv_taps(2 - done[0] % 2)
                        done[0] += 1

                gates_to(3)
                dve.wait_ge(S("sb_tail"), l + 1)
                for j in range(3):
                    ins = v.tensor_tensor(zm[:, 512 * j:512 * j + 512], zm[:, 512 * j:512 * j + 512], A[1 + j][:], ALU.subtract)
                ins.then_inc(S("sb_w"), 1)
                gates_to(7)
                dve.wait_ge(S("sb_exp"), l + 1)
                v.tensor_tensor(near(zm), near(zm), m4, ALU.mult)
                v.tensor_tensor(far(zm), far(zm), m4s, ALU.mult).then_inc(S("sb_a"), 1)
                gates_to(15)
                dve.wait_ge(S("ret_z"), l + 1)
                for j in range(2):
                    v.tensor_tensor(near(zs)[:, 2 * j:2 * j + 2], A[1 + j][:].rearrange("p (h q) -> p h q", h=2),
                                    decay[:, 2 * j:2 * j + 2, :], ALU.mult)
                v.tensor_tensor(far(zs), A[3][:].rearrange("p (h q) -> p h q", h=NH), decay[:, :, 0:P],
                                ALU.mult).then_inc(S("ret_a"), 1)
                dve.wait_ge(S("yT_hi2"), l + 1)
                v.tensor_tensor(flat(yT[2][1][:]), A[0][:], flat(yT[2][0][:]).bitcast(F32),
                                ALU.subtract).then_inc(S("yT_lo2"), 1)
                gates_to(20)
                assert taps[0] == CONV_W

                def centre(bank, groups, width, dst, square, row):
                    src = bank[:].rearrange("p (g d) -> p g d", d=width)
                    to = dst.rearrange("p (g d) -> p g d", d=width)
                    link(v.tensor_reduce(stat[:, row, 0:groups], src, AX.X, ALU.add))
                    link(v.tensor_scalar(stat[:, row, 0:groups], stat[:, row, 0:groups], 1.0 / width, None, ALU.mult))
                    mean = stat[:, row, 0:groups].unsqueeze(2).to_broadcast([P, groups, width])
                    link(v.tensor_tensor(to, src, mean, ALU.subtract))
                    link(v.tensor_tensor(square, dst, dst, ALU.mult))
                    link(v.tensor_reduce(stat[:, row, 0:groups], square.rearrange("p (g d) -> p g d", d=width), AX.X,
                                         ALU.add))
                    power(stat[:, row + 1, 0:groups], stat[:, row, 0:groups], 1.0 / width)
                    return stat[:, row + 1, 0:groups].unsqueeze(2).to_broadcast([P, groups, width])

                ahead(base + GATE0 + 23)
                dve.wait_ge(S("ret_o"), l + 1)
                y, sq = (tmp[:, j].rearrange("p t c -> p (t c)") for j in range(2))
                inv = centre(T[1], TT * NH, HD, y, sq, 0)
                link(v.tensor_tensor(y.rearrange(heads, d=HD), y.rearrange(heads, d=HD), inv, ALU.mult))
                v.tensor_tensor(tmp[:, 0], tmp[:, 0], U[4][:, :, DB:], ALU.mult).then_inc(S("ret_y"), 1)
                ahead(base + GATE0 + 27)
                dve.wait_ge(S("conv_nat"), l + 1)
                cn = convn[:].rearrange("p t c -> p (t c)")
                inv = centre(T[0], TT, DB, cn, flat(dT[:]), 0)
                v.tensor_tensor(cn.rearrange("p (g d) -> p g d", d=DB), cn.rearrange("p (g d) -> p g d", d=DB), inv,
                                ALU.mult).then_inc(S("conv_ln"), 1)
                ahead(base + GATE0 + 31)
                dve.wait_ge(S("yT_hi3"), l + 1)
                v.tensor_tensor(flat(yT[3][1][:]), A[1][:], flat(yT[3][0][:]).bitcast(F32),
                                ALU.subtract).then_inc(S("yT_lo3"), 1)

                def rest_merged(banks):
                    for b in banks:
                        dve.wait_ge(S("gT_hi"), 4 * l + b + 1)
                        v.tensor_tensor(flat(hT_lo[:, 2 * b:2 * b + 2, :]), TB[b][:],
                                        flat(hT_hi[:, 2 * b:2 * b + 2, :]).bitcast(F32), ALU.subtract).then_inc(S("gT_lo"), 1)

                for i, b in enumerate(BR_ORDER):
                    if i == 1:
                        dve.wait_ge(S("yT_hi0"), l + 1)
                        v.tensor_tensor(flat(yT[0][1][:]), flat(conv[:]), flat(yT[0][0][:]).bitcast(F32),
                                        ALU.subtract).then_inc(S("yT_lo0"), 1)
                    for nb in range(2):
                        n = base + BR0 + 2 * i + nb
                        ahead(min(n, base + BR0 + 6))
                        for tt in range(TT):
                            if tt == 0:
                                dve.wait_ge(S("branch"), 2 * (4 * l + i) + nb + 1)
                            else:
                                dve.wait_ge(used, n + 1)
                            sl = slice(nb * 512, nb * 512 + 512)
                            dst = merged if i == 0 else gates[:, b]
                            v.tensor_tensor(dst[:, tt, sl], gates[:, b, tt, sl], (G, T)[nb][tt][:],
                                            ALU.mult).then_inc(S("prod"), 1)
                        if i == 3 and nb:
                            rest_merged((0, 1))
                        if i == 3:
                            dve.wait_ge(S("prod"), 16 * l + 12 + 2 * nb + 2)
                            dve.wait_ge(S("summed"), 8 * l + 4 + 2 * nb + 2)
                            for tt in range(TT):
                                v.tensor_tensor(merged[:, tt, sl], merged[:, tt, sl], gates[:, b, tt, sl],
                                                ALU.add).then_inc(S("merged"), 1)
                ahead(base + BR0 + 8)
                rest_merged((2, 3))
                for nb in range(2):
                    n = base + OUT0 + 4 * nb + 3
                    ahead(n if nb else base + OUT0 + 1)
                    for tt in range(TT):
                        if tt == 0:
                            dve.wait_ge(half, half_no(l, 13 + nb) + 1)
                        else:
                            dve.wait_ge(used, n + 1)
                        sl = slice(nb * 512, nb * 512 + 512)
                        v.tensor_tensor(xs[:, tt, sl], xs[:, tt, sl], G[tt][:], ALU.add).then_inc(S("out_added"), 1)
                    if nb == 0:
                        ahead(n)
                        rest_wide(mT_lo, mT_hi, gains(l, G_MEM), S("mT_hi"), 4 * l, S("mT_lo"))
                token_scale(l, MEM)
                rest_wide(hT_lo, hT_hi, gains(l, G_XA), S("hT_hi"), 12 * l + 4, S("hT_lo"))
                token_scale(l, XA)
                dve.wait_ge(S("emptied"), 2 * unit_no(l, 13) + 2)
                k_nat = convn[:].rearrange("p t c -> p (t c)")
                square = tmp[:, 1].rearrange("p t c -> p (t c)")
                head_scale(k_nat, square, 0)
                v.tensor_tensor(tmp[:, 0].rearrange("p t (h d) -> p (t h) d", d=HD), k_nat.rearrange(heads, d=HD),
                                per_head(1), ALU.mult).then_inc(S("mk_normed"), 1)
                split_to(base + XV0 + 2)
                dve.wait_ge(S("emptied"), 2 * unit_no(l, 14) + 2)
                q_nat = qn[:].rearrange("p t c -> p (t c)")
                head_scale(q_nat, square, 0)
                v.tensor_tensor(q_nat.rearrange(heads, d=HD), q_nat.rearrange(heads, d=HD), per_head(1),
                                ALU.mult).then_inc(S("q_normed"), 1)
                split_to(base + XV0 + 3)
                for tt in range(TT):
                    dve.wait_ge(S("x_scores"), TT * l + tt + 1)
                    for hp in range(2):
                        j = tt * NH + 2 * hp
                        link(v.tensor_reduce(stat[:, 3, j:j + 2], A[2 * tt + hp][:].rearrange("p (h m) -> p h m", h=2), AX.X,
                                             ALU.max))
                    v.tensor_scalar(stat[:, 5, tt * NH:tt * NH + NH], stat[:, 3, tt * NH:tt * NH + NH], -1.0, None,
                                    ALU.mult).then_inc(S("xmax"), 1)
                dve.wait_ge(S("xp"), 8 * (l + 1))
                link(v.reciprocal(stat[:, 6, :], stat[:, 4, :]))
                for tt in range(TT):
                    split_to(base + XV0 + 3 + tt)
                    dve.wait_ge(S("xo"), TT * l + tt + 1)
                    v.tensor_tensor(on[:, tt, :].rearrange(heads, d=HD), T[tt][:, 0:DB].rearrange(heads, d=HD),
                                    per_head(6)[:, tt * NH:tt * NH + NH], ALU.mult).then_inc(S("xo_normed"), 1)
                for c in range(KB):
                    dve.wait_ge(S("oT_hi"), KB * l + c + 1)
                    v.tensor_tensor(oT_lo[:, c, :], A[c][:, 0:SEQ], oT_hi[:, c, :].bitcast(F32),
                                    ALU.subtract).then_inc(S("oT_lo"), 1)
                for nb in range(2):
                    for tt in range(TT):
                        split_to(base + XV0 + 5 + 2 * nb + tt)
                        if nb and tt and l == 0:
                            rest_wide(hT_lo, hT_hi, gains(l, G_FFN), S("hT_hi"), 12 * l + 8, S("hT_lo"), (0, 1))
                        if tt == 0:
                            dve.wait_ge(S("xproj"), 2 * l + nb + 1)
                        else:
                            dve.wait_ge(used, base + XO0 + nb + 1)
                        sl = slice(nb * 512, nb * 512 + 512)
                        v.tensor_tensor(xs[:, tt, sl], xs[:, tt, sl], (G, T)[nb][tt][:], ALU.add).then_inc(S("xo_added"), 1)
                if l:
                    break
                ahead(base + XO0 + 2)
                rest_wide(hT_lo, hT_hi, gains(l, G_FFN), S("hT_hi"), 12 * l + 8, S("hT_lo"), (2, 3))
                token_scale(l, FFN)
                dve.wait_ge(S("token_scale"), 4 * l + FFN + 1)

                def ff_rest(f):
                    dve.wait_ge(S("actT_hi"), f + 1)
                    v.tensor_tensor(flat(actT_lo[:]), T[0][:], flat(actT_hi[:]).bitcast(F32),
                                    ALU.subtract).then_inc(S("actT_lo"), 1)

                for f in range(NF):
                    if f:
                        ahead(FF_N0 + FFS * f + 1)
                        ff_rest(f - 1)
                    split_to(FF_N0 + FFS * f + (3 + RING if f else 8))
                    for tt in range(TT):
                        dve.wait_ge(S("ff_silu"), 2 * f + tt + 1)
                        if f:
                            dve.wait_ge(S("ff_actT"), f)
                        v.scalar_tensor_tensor(out=act[:, tt, :], in0=G[tt][:, FB:], scalar=rs[:, 4 * l + FFN, tt:tt + 1],
                                               in1=silu[:, tt, :], op0=ALU.mult, op1=ALU.mult).then_inc(S("ff_act"), 1)
                ff_rest(NF - 1)
                add_ffn(l, 0)

            j = 4 * (DEPTH - 1) + FFN
            dve.wait_ge(S("squares"), 2 * TT)
            v.tensor_tensor(ssq[:, j, :], half_ssq[:, 0, :], half_ssq[:, 1, :], ALU.add).then_inc(S("squares_added"), 1)
            token_scale(DEPTH - 1, FFN)
            dve.wait_ge(S("token_scale"), j + 1)
            dve.wait_ge(S("grow_in"), 16)
            for tt in range(TT):
                v.scalar_tensor_tensor(out=xn[:, tt, :], in0=xs[:, tt, :], scalar=rs[:, j, tt:tt + 1],
                                       in1=merged[:, 0, :], op0=ALU.mult, op1=ALU.mult).then_inc(S("xn"), 1)
            dve.wait_ge(S("logits"), 1)
            for tt in range(TT):
                ins = v.tensor_copy(lg[:, 0, tt, :], G[tt][:, 0:NE])
            link(ins)
            e8 = cst[:, C_E8:C_E8 + NE].unsqueeze(1).to_broadcast([P, TT, NE])

            def wide(t):
                return t.unsqueeze(2).to_broadcast([P, TT, NE])

            def first_of_max(src, top, onehot, scratch):
                link(v.tensor_reduce(lg[:, top, :, 0], src, AX.X, ALU.max))
                link(v.tensor_tensor(lg[:, scratch], src, wide(lg[:, top, :, 0]), ALU.is_equal))
                link(v.tensor_tensor(lg[:, scratch], lg[:, scratch], e8, ALU.mult))
                link(v.tensor_reduce(lg[:, 11, :, 0], lg[:, scratch], AX.X, ALU.max))
                link(v.tensor_tensor(lg[:, onehot], lg[:, scratch], wide(lg[:, 11, :, 0]), ALU.is_equal))

            first_of_max(lg[:, 0], 1, 2, 3)
            link(v.scalar_tensor_tensor(out=lg[:, 4], in0=lg[:, 2], scalar=NEG, in1=lg[:, 0], op0=ALU.mult, op1=ALU.add))
            first_of_max(lg[:, 4], 5, 7, 3)
            v.tensor_tensor(lg[:, 6], lg[:, 2], lg[:, 7], ALU.add).then_inc(S("picked"), 1)
            link(v.tensor_tensor(lg[:, 10, :, 1], lg[:, 5, :, 0], lg[:, 1, :, 0], ALU.subtract))
            v.tensor_tensor(lg[:, 10, :, 1], lg[:, 10, :, 1], rs[:, j, :], ALU.mult).then_inc(S("gap"), 1)
            dve.wait_ge(S("xn_hi"), 2)
            v.tensor_tensor(xn_lo[:, 1, :], xn[:, 1, :], xn_hi[:, 1, :].bitcast(F32), ALU.subtract).then_inc(S("xn_lo1"), 1)
            dve.wait_ge(S("counted"), 1)
            link(v.tensor_scalar(lg[:, 8].rearrange("p t e -> p (t e)"), T[1][:, 0:TT * NE], 1.0, None, ALU.add))
            link(v.tensor_tensor(lg[:, 8], lg[:, 8], lg[:, 6], ALU.mult))
            link(v.tensor_scalar(posm[:, :, 0:NE], lg[:, 8], -1.0, None, ALU.add))
            link(v.tensor_scalar(posm[:, :, NE:2 * NE], lg[:, 8], -1.0 - P, None, ALU.add))
            iota = cst[:, C_IOTA:C_IOTA + P]

            def select(i):
                for tt in range(TT):
                    ins = v.tensor_scalar(sel[:, tt, :], iota, posm[:, tt, bass.ds(i, 1)], None, ALU.is_equal)
                ins.then_inc(S("sel"), 1)

            def rest_gathered(i, banks=range(2)):
                for j in banks:
                    dve.wait_ge(S("eT_hi"), 2 * i + j + 1)
                    part = slice(4 * j, 4 * j + 4)
                    v.tensor_tensor(eT_lo[:, part, :].rearrange("p k s -> p (k s)"), A[2 + j][:],
                                    eT_hi[:, part, :].rearrange("p k s -> p (k s)").bitcast(F32),
                                    ALU.subtract).then_inc(S("eT_lo"), 1)

            def e_rest(step):
                dve.wait_ge(S("e_aT_hi"), step + 1)
                v.tensor_tensor(actT_lo[:, :, 0:P], T[0][:, 0:2 * P].rearrange("p (c t) -> p c t", c=2),
                                actT_hi[:, :, 0:P].bitcast(F32), ALU.subtract).then_inc(S("e_aT_lo"), 1)

            def add_scattered(i, tt):
                dve.wait_ge(S("scat"), 2 * i + tt + 1)
                for nb in range(2):
                    sl = slice(nb * 512, nb * 512 + 512)
                    v.scalar_tensor_tensor(out=xs[:, tt, sl], in0=A[2 + nb][:], scalar=comb[:, tt, bass.ds(i, 1)],
                                           in1=xs[:, tt, sl], op0=ALU.mult, op1=ALU.add).then_inc(S("scattered"), 1)

            def rest_outputs(i, nb):
                dve.wait_ge(S("ye_hi"), 2 * i + nb + 1)
                sl = slice(nb * 512, nb * 512 + 512)
                v.tensor_tensor(ye_lo[:, sl], A[nb][:], ye_hi[:, sl].bitcast(F32), ALU.subtract).then_inc(S("ye_lo"), 1)

            def item(i, first=False, last=False):
                lap0 = FF_LAP + NF * i
                end = FFS * NF + (2 if last else LEAD)
                for f in range(NF):
                    step = NF * i + f
                    if not (first and f == 0):
                        split_to(FFS * f + 2 + LEAD, lap0, i)
                        e_rest(step - 1)
                    split_to(min(FFS * f + 4 + 2 * (first and f == 0) + LEAD, end), lap0, i)
                    dve.wait_ge(S("e_silu"), step + 1)
                    if not (first and f == 0):
                        dve.wait_ge(S("e_actT"), step)
                    v.tensor_tensor(act[:, 0, :], silu[:, 0, :], (G[0], G[1], T[1])[f % 3][:, FB:],
                                    ALU.mult).then_inc(S("e_act"), 1)
                    if f == 0 and not first:
                        for nb in range(2):
                            split_to(5 + nb + LEAD, lap0, i)
                            rest_outputs(i - 1, nb)
                    if f in (2, 4) and not first:
                        add_scattered(i - 1, f // 2 - 1)
                    if f == 5 and not last:
                        dve.wait_ge(S("gathered"), 2 * i + 2)
                        dve.wait_ge(S("selT"), i + 1)
                        select(i + 1)
                if not last:
                    rest_gathered(i + 1)

            select(0)
            dve.wait_ge(S("totals"), 1)
            link(v.tensor_reduce(more_items_f32[:, 0:1], G[0][:, 0:NE], AX.X, ALU.max))
            link(v.tensor_scalar(more_items_f32[:, 0:1], more_items_f32[:, 0:1], float(P) + 0.5, float(NE), ALU.is_gt, ALU.mult))
            v.tensor_copy(more_items[:, 0:1], more_items_f32[:, 0:1]).then_inc(S("items"), 1)
            dve.wait_ge(S("items"), 1)
            items = dve.snap(NE + dve.value_load(more_items[0:1, 0:1], min_val=0, max_val=NE))
            dve.wait_ge(S("gap_exp"), 1)
            link(v.tensor_scalar(lg[:, 8, :, 0], lg[:, 10, :, 0], 1.0, None, ALU.add))
            link(v.reciprocal(lg[:, 8, :, 1], lg[:, 8, :, 0]))
            link(v.tensor_tensor(lg[:, 8, :, 2], lg[:, 8, :, 1], lg[:, 10, :, 0], ALU.mult))
            link(v.tensor_tensor(lg[:, 3], lg[:, 2], wide(lg[:, 8, :, 1]), ALU.mult))
            link(v.tensor_tensor(lg[:, 7], lg[:, 7], wide(lg[:, 8, :, 2]), ALU.mult))
            for j in range(2):
                link(v.tensor_tensor(comb[:, :, j * NE:j * NE + NE], lg[:, 3], lg[:, 7], ALU.add))
            nxt[0] -= RING * FF_LAP
            rest_gathered(0, (0,))
            split_to(2 + RING, FF_LAP, 0)
            rest_gathered(0, (1,))
            item(0, first=True)
            nxt[0] = LEAD - 2
            with dve.Fori(1, items - 1) as i:
                item(i)
            assert nxt[0] == LEAD - 2 + RING * NF
            nxt[0] = LEAD - 2
            last = dve.snap(items - 1)
            item(last, last=True)
            e_rest(last * NF + NF - 1)
            for nb in range(2):
                rest_outputs(last, nb)
            for nb in range(2):
                sl = slice(nb * 512, nb * 512 + 512)
                for tt in range(TT):
                    dve.wait_ge(S("last_scat"), 2 * nb + tt + 1)
                    v.scalar_tensor_tensor(out=xs[:, tt, sl], in0=(A[2:], G)[nb][tt][:],
                                           scalar=comb[:, tt, bass.ds(last, 1)], in1=xs[:, tt, sl],
                                           op0=ALU.mult, op1=ALU.add).then_inc(S("last_added"), 1)


_INS = ["x", "mem", "positions", "norm_mix_g", "w_in", "conv_w", "conv_b", "conv_ln_g", "conv_ln_b", "pool_w",
        "pool_scale", "w_gate", "w_branch", "w_out", "norm_xa_g", "norm_mem_g", "xa_wq", "xa_wkv", "xa_q_norm_g",
        "xa_k_norm_g", "xa_wo", "norm_ffn_g", "ffn_w_gu", "ffn_w_down", "moe_router", "moe_w_gu", "moe_w_down"]


def kernel(**inputs):
    import concourse.bacc as bacc
    from concourse.bass_utils import run_bass_kernel_spmd

    nc = bacc.Bacc("TRN2", target_bir_lowering=False, num_devices=1)
    arrays = {"shape_constants": shape_constants()}
    arrays.update({name: np.ascontiguousarray(inputs[name]) for name in _INS})
    args = [nc.dram_tensor(f"in_{name}", a.shape, mybir.dt.from_np(a.dtype), kind="ExternalInput").ap()
            for name, a in arrays.items()]
    out = nc.dram_tensor("out_0", inputs["x"].shape, F32, kind="ExternalOutput").ap()
    trunk(nc, *args, out)
    r = run_bass_kernel_spmd(nc, [{f"in_{name}": a for name, a in arrays.items()}], core_ids=[0])
    return r.results[0]["out_0"]
```
